# Optimizing a Trainium2 kernel written in Bass

```python
import math
import jax, jax.numpy as jnp
from jax import lax
import numpy as np

D_MODEL = 1024
BATCH = 1
SEQ = 512
DEPTH = 1

N_META = 16
CONV_WIDTH = 3
D_CONV = D_MODEL
CONV_GROUPS = 16
SB_HEAD_DIM = 64
SB_HEADS = 16
D_ATTN = SB_HEADS * SB_HEAD_DIM
N_BRANCH = 2
D_IN = 3 * D_CONV + 3 * D_ATTN + N_BRANCH * D_MODEL
D_FF = 2816
Q_BLOCK = 128
RMS_EPS = 1e-6


def rms_norm(x, g):
    xf = x.astype(jnp.float32)
    y = xf * lax.rsqrt(jnp.mean(xf * xf, axis=-1, keepdims=True) + RMS_EPS)
    return (y * g.astype(jnp.float32)).astype(x.dtype)

def causal_dwconv(x, w):
    k, c = w.shape
    return lax.conv_general_dilated(
        x, w.reshape(k, 1, c).astype(x.dtype),
        window_strides=(1,), padding=[(k - 1, 0)],
        dimension_numbers=("NWC", "WIO", "NWC"),
        feature_group_count=c)

def stick_breaking_attention(q, k, v):
    seq_len = q.shape[1]
    scale = 1.0 / math.sqrt(q.shape[-1])
    bounds = [(0, N_META)] + [(s, min(s + Q_BLOCK, seq_len))
                              for s in range(N_META, seq_len, Q_BLOCK)]
    outs = []
    for q0, q1 in bounds:
        qb = q[:, q0:q1]
        kb = k[:, :q1]
        vb = v[:, :q1].astype(jnp.float32)
        z = jnp.einsum("bqhd,bkhd->bhqk", qb, kb,
                       preferred_element_type=jnp.float32) * scale
        t_idx = jnp.arange(q0, q1)[:, None]
        s_idx = jnp.arange(q1)[None, :]
        causal = s_idx < t_idx
        log_beta = jax.nn.log_sigmoid(z)
        log_fail = jnp.where(causal, log_beta - z, 0.0)
        survive = lax.cumsum(log_fail, axis=3, reverse=True) - log_fail
        a = jnp.where(causal, jnp.exp(log_beta + survive), 0.0)
        o = jnp.einsum("bhqk,bkhd->bqhd", a, vb)
        outs.append(o.astype(v.dtype))
    return jnp.concatenate(outs, axis=1)

def hybrid_mixer(xn, w_in, conv_w_mix, w_proj_conv, w_proj_attn, b_gate, w_out):
    bsz, seq_len, _ = xn.shape
    h = xn @ w_in
    splits = np.cumsum([D_CONV, D_CONV, D_CONV, D_ATTN, D_ATTN, D_ATTN, D_MODEL])
    b_c, c_c, h_c, q, k, v, g_conv, g_attn = jnp.split(h, list(splits), axis=-1)

    y_conv = b_c * causal_dwconv(c_c * h_c, conv_w_mix)
    branch_conv = y_conv @ w_proj_conv

    hd = (bsz, seq_len, SB_HEADS, SB_HEAD_DIM)
    o = stick_breaking_attention(q.reshape(hd), k.reshape(hd), v.reshape(hd))
    branch_attn = o.reshape(bsz, seq_len, D_ATTN) @ w_proj_attn

    gate_conv = jax.nn.sigmoid(g_conv + b_gate[0])
    gate_attn = jax.nn.sigmoid(g_attn + b_gate[1])
    merged = gate_conv * branch_conv + gate_attn * branch_attn
    return merged @ w_out

def conv_gated_mlp(xn, w_up_gate, conv_w_ffn, w_down):
    u, g = jnp.split(xn @ w_up_gate, 2, axis=-1)
    u = causal_dwconv(u, conv_w_ffn)
    return (jax.nn.gelu(u) * g) @ w_down

def first_inputs(seed: int = 0) -> dict:
    key = jax.random.key(seed)
    ks = jax.random.split(key, 16)
    f32 = jnp.float32

    def normal(k, shape, scale):
        return jax.random.normal(k, shape, f32) * scale

    def gain(k):
        return 1.0 + normal(k, (DEPTH, D_MODEL), 0.05)

    return {
        "x": normal(ks[0], (BATCH, SEQ, D_MODEL), 1.0),
        "meta_tokens": normal(ks[1], (N_META, D_MODEL), 1.0),
        "g_pre_mix": gain(ks[2]),
        "w_in": normal(ks[3], (DEPTH, D_MODEL, D_IN), D_MODEL ** -0.5),
        "conv_w_mix": normal(ks[4], (DEPTH, CONV_WIDTH, D_CONV), CONV_WIDTH ** -0.5),
        "w_proj_conv": normal(ks[5], (DEPTH, D_CONV, D_MODEL), D_CONV ** -0.5),
        "w_proj_attn": normal(ks[6], (DEPTH, D_ATTN, D_MODEL), D_ATTN ** -0.5),
        "b_gate": normal(ks[7], (DEPTH, N_BRANCH, D_MODEL), 0.02),
        "w_out": normal(ks[8], (DEPTH, D_MODEL, D_MODEL), D_MODEL ** -0.5),
        "g_post_mix": gain(ks[9]),
        "g_pre_ffn": gain(ks[10]),
        "w_up_gate": normal(ks[11], (DEPTH, D_MODEL, 2 * D_FF), D_MODEL ** -0.5),
        "conv_w_ffn": normal(ks[12], (DEPTH, CONV_WIDTH, D_FF), CONV_WIDTH ** -0.5),
        "w_down": normal(ks[13], (DEPTH, D_FF, D_MODEL), D_FF ** -0.5),
        "g_post_ffn": gain(ks[14]),
    }

def first_block(x, meta_tokens, g_pre_mix, w_in, conv_w_mix, w_proj_conv, w_proj_attn,
              b_gate, w_out, g_post_mix, g_pre_ffn, w_up_gate, conv_w_ffn, w_down,
              g_post_ffn):
    bsz = x.shape[0]
    meta = jnp.broadcast_to(meta_tokens[None].astype(x.dtype), (bsz, N_META, D_MODEL))
    h = jnp.concatenate([meta, x], axis=1)
    for layer in range(DEPTH):
        mix = hybrid_mixer(rms_norm(h, g_pre_mix[layer]), w_in[layer], conv_w_mix[layer],
                           w_proj_conv[layer], w_proj_attn[layer], b_gate[layer],
                           w_out[layer])
        h = h + rms_norm(mix, g_post_mix[layer])
        ffn = conv_gated_mlp(rms_norm(h, g_pre_ffn[layer]), w_up_gate[layer],
                             conv_w_ffn[layer], w_down[layer])
        h = h + rms_norm(ffn, g_post_ffn[layer])
    return h[:, N_META:, :]


CHUNK = 64
SSM_WIDTH = 1024
SSM_GROUP = 16
SSM_GROUPS = SSM_WIDTH // SSM_GROUP
SSM_STATE = 64
DT_MIN = 1e-3
DT_MAX = 1e-1
MLA_HEADS = 16
QK_NOPE = 64
QK_ROPE = 32
V_HEAD = 64
Q_LORA = 256
KV_LORA = 256
MLA_WIDTH = MLA_HEADS * V_HEAD
ROPE_BASE = 10000.0
EPS = 1e-6
IN_SPLITS = (SSM_WIDTH, SSM_WIDTH, Q_LORA, KV_LORA, QK_ROPE, MLA_WIDTH, D_MODEL, D_MODEL)
IN_WIDTH = sum(IN_SPLITS)


def _rmsnorm(x, g):
    xf = x.astype(jnp.float32)
    y = xf * lax.rsqrt(jnp.mean(xf * xf, axis=-1, keepdims=True) + EPS)
    return (y * g.astype(jnp.float32)).astype(x.dtype)

def _cmul(ar, ai, br, bi):
    return ar * br - ai * bi, ar * bi + ai * br

def _ssm_branch(u, log_dt, a_re, a_im, b_re, b_im, c_re, c_im, d_skip):
    f32 = jnp.float32
    out_dtype = u.dtype
    bsz, seq, _ = u.shape
    n_chunks = seq // CHUNK
    u = u.astype(f32).reshape(bsz, n_chunks, CHUNK, SSM_GROUPS, SSM_GROUP)
    u = jnp.moveaxis(u, 1, 0)
    dt = jnp.exp(log_dt.astype(f32))[:, None]
    lr, li = a_re.astype(f32), a_im.astype(f32)
    mag = jnp.exp(lr * dt)
    abar_re, abar_im = mag * jnp.cos(li * dt), mag * jnp.sin(li * dt)
    den = lr * lr + li * li
    nr, ni = abar_re - 1.0, abar_im
    fr = (nr * lr + ni * li) / den
    fi = (ni * lr - nr * li) / den
    br, bi = b_re.astype(f32), b_im.astype(f32)
    bbar_re, bbar_im = _cmul(fr[..., None], fi[..., None], br, bi)
    cr_w, ci_w = c_re.astype(f32), c_im.astype(f32)
    d = d_skip.astype(f32).reshape(SSM_GROUPS, SSM_GROUP)

    def combine(e1, e2):
        a1r, a1i, b1r, b1i = e1
        a2r, a2i, b2r, b2i = e2
        ar, ai = _cmul(a2r, a2i, a1r, a1i)
        xr, xi = _cmul(a2r, a2i, b1r, b1i)
        return ar, ai, xr + b2r, xi + b2i

    def chunk_step(carry, u_c):
        sr, si = carry
        bur = jnp.einsum('btgp,gnp->btgn', u_c, bbar_re)
        bui = jnp.einsum('btgp,gnp->btgn', u_c, bbar_im)
        ar = jnp.broadcast_to(abar_re, bur.shape)
        ai = jnp.broadcast_to(abar_im, bur.shape)
        pr, pi_, xr, xi = lax.associative_scan(combine, (ar, ai, bur, bui), axis=1)
        cr, ci = _cmul(pr, pi_, sr[:, None], si[:, None])
        xr, xi = xr + cr, xi + ci
        y = (jnp.einsum('btgn,gpn->btgp', xr, cr_w)
             - jnp.einsum('btgn,gpn->btgp', xi, ci_w) + d * u_c)
        return (xr[:, -1], xi[:, -1]), y

    init = (jnp.zeros((bsz, SSM_GROUPS, SSM_STATE), f32),
            jnp.zeros((bsz, SSM_GROUPS, SSM_STATE), f32))
    _, ys = lax.scan(chunk_step, init, u)
    return jnp.moveaxis(ys, 0, 1).reshape(bsz, seq, SSM_WIDTH).astype(out_dtype)

def _rope(t, cos, sin):
    half = t.shape[-1] // 2
    t1, t2 = t[..., :half], t[..., half:]
    return jnp.concatenate([t1 * cos - t2 * sin, t2 * cos + t1 * sin], axis=-1).astype(t.dtype)

def _mla_branch(q_lat, kv_lat, k_rope, positions, g_q_norm, w_q_up, g_kv_norm, w_kv_up):
    bsz, seq, _ = q_lat.shape
    q = (_rmsnorm(q_lat, g_q_norm) @ w_q_up).reshape(bsz, seq, MLA_HEADS, QK_NOPE + QK_ROPE)
    q_nope, q_rope = q[..., :QK_NOPE], q[..., QK_NOPE:]
    kv = (_rmsnorm(kv_lat, g_kv_norm) @ w_kv_up).reshape(bsz, seq, MLA_HEADS, QK_NOPE + V_HEAD)
    k_nope, v = kv[..., :QK_NOPE], kv[..., QK_NOPE:]
    inv_freq = ROPE_BASE ** (-jnp.arange(0, QK_ROPE, 2, dtype=jnp.float32) / QK_ROPE)
    ang = positions.astype(jnp.float32)[..., None] * inv_freq
    cos, sin = jnp.cos(ang), jnp.sin(ang)
    q_rope = _rope(q_rope, cos[:, :, None], sin[:, :, None])
    k_rope = _rope(k_rope, cos, sin)
    n_blk = seq // Q_BLOCK
    key_chunk = jnp.arange(seq) // CHUNK
    scale = (QK_NOPE + QK_ROPE) ** -0.5

    def to_blocks(t):
        return jnp.moveaxis(t.reshape(bsz, n_blk, Q_BLOCK, *t.shape[2:]), 1, 0)

    def attend(args):
        qn, qr, blk = args
        s = (jnp.einsum('bqhd,bkhd->bhqk', qn, k_nope)
             + jnp.einsum('bqhr,bkr->bhqk', qr, k_rope)).astype(jnp.float32) * scale
        q_chunk = (blk * Q_BLOCK + jnp.arange(Q_BLOCK)) // CHUNK
        mask = key_chunk[None, :] <= q_chunk[:, None]
        p = jax.nn.softmax(jnp.where(mask, s, -jnp.inf), axis=-1).astype(v.dtype)
        return jnp.einsum('bhqk,bkhd->bqhd', p, v)

    o = lax.map(attend, (to_blocks(q_nope), to_blocks(q_rope), jnp.arange(n_blk)))
    return jnp.moveaxis(o, 0, 1).reshape(bsz, seq, MLA_WIDTH)

def second_inputs(seed: int = 0) -> dict:
    key = jax.random.key(seed)
    ks = jax.random.split(key, 25)
    f32 = jnp.float32

    def nrm(k, shape, scale):
        return jax.random.normal(k, shape, f32) * scale

    positions = (jax.random.randint(ks[2], (BATCH, 1), 0, 2048, dtype=jnp.int32)
                 + jnp.arange(SEQ, dtype=jnp.int32)[None, :])
    return {
        "x": nrm(ks[0], (BATCH, SEQ, D_MODEL), 1.0),
        "c": nrm(ks[1], (BATCH, D_MODEL), 1.0),
        "positions": positions,
        "w_ada": nrm(ks[3], (DEPTH, D_MODEL, 3 * D_MODEL), 0.5 * D_MODEL ** -0.5),
        "b_ada": nrm(ks[4], (DEPTH, 3 * D_MODEL), 0.01),
        "g_pre": 1.0 + nrm(ks[5], (DEPTH, D_MODEL), 0.01),
        "w_in": nrm(ks[6], (DEPTH, D_MODEL, IN_WIDTH), D_MODEL ** -0.5),
        "ssm_log_dt": jax.random.uniform(ks[7], (DEPTH, SSM_GROUPS), f32,
                                         math.log(DT_MIN), math.log(DT_MAX)),
        "ssm_a_re": -0.5 + nrm(ks[8], (DEPTH, SSM_GROUPS, SSM_STATE), 0.01),
        "ssm_a_im": (jnp.pi * jnp.arange(SSM_STATE, dtype=f32)
                     + nrm(ks[9], (DEPTH, SSM_GROUPS, SSM_STATE), 0.01)),
        "ssm_b_re": nrm(ks[10], (DEPTH, SSM_GROUPS, SSM_STATE, SSM_GROUP), (2 * SSM_GROUP) ** -0.5),
        "ssm_b_im": nrm(ks[11], (DEPTH, SSM_GROUPS, SSM_STATE, SSM_GROUP), (2 * SSM_GROUP) ** -0.5),
        "ssm_c_re": nrm(ks[12], (DEPTH, SSM_GROUPS, SSM_GROUP, SSM_STATE), (2 * SSM_STATE) ** -0.5),
        "ssm_c_im": nrm(ks[13], (DEPTH, SSM_GROUPS, SSM_GROUP, SSM_STATE), (2 * SSM_STATE) ** -0.5),
        "ssm_d": nrm(ks[14], (DEPTH, SSM_WIDTH), 0.5),
        "w_glu": nrm(ks[15], (DEPTH, SSM_WIDTH, 2 * SSM_WIDTH), SSM_WIDTH ** -0.5),
        "b_glu": nrm(ks[16], (DEPTH, 2 * SSM_WIDTH), 0.01),
        "g_q_norm": 1.0 + nrm(ks[17], (DEPTH, Q_LORA), 0.01),
        "w_q_up": nrm(ks[18], (DEPTH, Q_LORA, MLA_HEADS * (QK_NOPE + QK_ROPE)), Q_LORA ** -0.5),
        "g_kv_norm": 1.0 + nrm(ks[19], (DEPTH, KV_LORA), 0.01),
        "w_kv_up": nrm(ks[20], (DEPTH, KV_LORA, MLA_HEADS * (QK_NOPE + V_HEAD)), KV_LORA ** -0.5),
        "w_br_ssm": nrm(ks[21], (DEPTH, SSM_WIDTH, D_MODEL), SSM_WIDTH ** -0.5),
        "w_br_mla": nrm(ks[22], (DEPTH, MLA_WIDTH, D_MODEL), MLA_WIDTH ** -0.5),
        "w_out": nrm(ks[23], (DEPTH, D_MODEL, D_MODEL), D_MODEL ** -0.5),
        "g_post": 1.0 + nrm(ks[24], (DEPTH, D_MODEL), 0.01),
    }

def second_block(x, c, positions, w_ada, b_ada, g_pre, w_in, ssm_log_dt, ssm_a_re, ssm_a_im,
              ssm_b_re, ssm_b_im, ssm_c_re, ssm_c_im, ssm_d, w_glu, b_glu, g_q_norm, w_q_up,
              g_kv_norm, w_kv_up, w_br_ssm, w_br_mla, w_out, g_post):
    split_at = np.cumsum(IN_SPLITS)[:-1].tolist()
    for l in range(DEPTH):
        mod = c @ w_ada[l] + b_ada[l]
        shift, scale, gate = jnp.split(mod, 3, axis=-1)
        h = _rmsnorm(x, g_pre[l]) * (1.0 + scale[:, None]) + shift[:, None]
        proj = h @ w_in[l]
        u_s, z_s, q_lat, kv_lat, k_rope, z_m, gl_s, gl_m = jnp.split(proj, split_at, axis=-1)
        y_s = _ssm_branch(u_s, ssm_log_dt[l], ssm_a_re[l], ssm_a_im[l], ssm_b_re[l],
                          ssm_b_im[l], ssm_c_re[l], ssm_c_im[l], ssm_d[l])
        glu_a, glu_b = jnp.split(jax.nn.gelu(y_s) @ w_glu[l] + b_glu[l], 2, axis=-1)
        y_s = ((glu_a * jax.nn.sigmoid(glu_b)) * jax.nn.silu(z_s)) @ w_br_ssm[l]
        y_m = _mla_branch(q_lat, kv_lat, k_rope, positions, g_q_norm[l], w_q_up[l],
                          g_kv_norm[l], w_kv_up[l])
        y_m = (y_m * jax.nn.silu(z_m)) @ w_br_mla[l]
        merged = jax.nn.sigmoid(gl_s) * y_s + jax.nn.sigmoid(gl_m) * y_m
        out = merged @ w_out[l]
        x = x + gate[:, None] * _rmsnorm(out, g_post[l])
    return x


def setup_inputs(seed=0):
    out = dict(first_inputs(seed))
    for name, value in second_inputs(seed + 1).items():
        if name != "x":
            out[name + "_2"] = value
    return out


def reference(
    x, meta_tokens, g_pre_mix, w_in, conv_w_mix, w_proj_conv, w_proj_attn, b_gate, w_out,
    g_post_mix, g_pre_ffn, w_up_gate, conv_w_ffn, w_down, g_post_ffn, c_2, positions_2, w_ada_2,
    b_ada_2, g_pre_2, w_in_2, ssm_log_dt_2, ssm_a_re_2, ssm_a_im_2, ssm_b_re_2, ssm_b_im_2,
    ssm_c_re_2, ssm_c_im_2, ssm_d_2, w_glu_2, b_glu_2, g_q_norm_2, w_q_up_2, g_kv_norm_2,
    w_kv_up_2, w_br_ssm_2, w_br_mla_2, w_out_2, g_post_2,
):
    x = first_block(
        x, meta_tokens, g_pre_mix, w_in, conv_w_mix, w_proj_conv, w_proj_attn, b_gate, w_out,
        g_post_mix, g_pre_ffn, w_up_gate, conv_w_ffn, w_down, g_post_ffn,
    )
    return second_block(
        x, c_2, positions_2, w_ada_2, b_ada_2, g_pre_2, w_in_2, ssm_log_dt_2, ssm_a_re_2,
        ssm_a_im_2, ssm_b_re_2, ssm_b_im_2, ssm_c_re_2, ssm_c_im_2, ssm_d_2, w_glu_2, b_glu_2,
        g_q_norm_2, w_q_up_2, g_kv_norm_2, w_kv_up_2, w_br_ssm_2, w_br_mla_2, w_out_2, g_post_2,
    )


_drawn_inputs = setup_inputs


def setup_inputs(seed=0):
    import zlib

    import numpy as np

    out = dict(_drawn_inputs(seed))
    spreads = {}
    factors = {'b_gate': 8.0,
     'b_ada_2': 6.686,
     'g_pre_2': 8.0,
     'ssm_log_dt_2': 34.12,
     'ssm_a_re_2': 64.0,
     'ssm_a_im_2': 24.296,
     'ssm_b_re_2': 36.664,
     'ssm_b_im_2': 37.4,
     'ssm_c_re_2': 35.4,
     'ssm_c_im_2': 37.784,
     'b_glu_2': 62.835,
     'g_q_norm_2': 8.0,
     'g_kv_norm_2': 8.0,
     'g_post_2': 50.31}
    for name, (base, spread) in spreads.items():
        noise = np.random.default_rng([zlib.crc32(name.encode()), seed]).standard_normal(out[name].shape)
        drawn = base * np.exp(spread * noise) if base else spread * noise
        out[name] = __import__('jax').numpy.asarray(drawn.astype(out[name].dtype))
    for name, factor in factors.items():
        out[name] = (out[name] * factor).astype(out[name].dtype)
    return out
```

```python
from contextlib import ExitStack

import concourse.bass as bass
from concourse import mybir
import numpy as np

F32 = mybir.dt.float32
F32R = mybir.dt.float32r
I32 = mybir.dt.int32
ALU = mybir.AluOpType
ACT = mybir.ActivationFunctionType
AX = mybir.AxisListType

P = 128
D = 1024
DT = D // P
META = 16
SEQ = 512
L1 = META + SEQ
HALF = L1 // 2
FF = 2816
FT = FF // P
HEADS = 16
EPS = 1e-6

JOB = 8 * P
N_MIX = 0
N_GATE = N_MIX + 8 * DT
N_OUT = N_GATE + 4 * DT
N_UP = N_OUT + 2 * DT
N_DOWN = N_UP + 2 * FT
N_END1 = N_DOWN + FT * DT // 8
N_U = N_END1
N_SSM = N_U + DT
N_LAT = N_SSM + DT
N_ATT = N_LAT + 5
N_GLU = N_ATT + 2 * DT
N_MERGE = N_GLU + 2 * DT
N_OUT2 = N_MERGE + 4 * DT
N_LAST = N_OUT2 + DT
RAW = 2
SPLIT = 4

T_MIX = 0
T_GATE = T_MIX + 12 * DT + 1
T_OUT = T_GATE + 4 * DT
T_UP = T_OUT + 2 * DT
T_DOWN = T_UP + 2 * FT
T_U = T_DOWN + DT
T_SSM = T_U + DT
T_LAT = T_SSM + 5 * DT
T_ATT = T_LAT + 5
T_GLU = T_ATT + 8 * DT
T_MERGE = T_GLU + 2 * DT
T_OUT2 = T_MERGE + 4 * DT

PIECES = [(i, P * i, P, P * i) for i in range(4)] + [
    (4, 512, 16, 512), (3, 512, 16, 528), (0, 128, 400, 544),
    (1, 256, 80, 944), (1, 336, 192, 1024), (2, 384, 144, 1216)]
SCORE = 1360
KPAD = 5 * P

Q_PRE, Q_MIX, Q_PREF, Q_FFN, Q_PRE2, Q_LAT, Q_KV, Q_POST2 = 0, 8, 16, 24, 32, 40, 42, 44

S2 = SEQ
GROUPS, GP, NS = 64, 16, 64
SUB = 8
NC = SEQ // SUB
PAIRS = GROUPS // 2
PT_ = PAIRS // DT
GT = GROUPS // DT
LATT = 256 // P
ROPE = 32
QK = 96
SCALE2 = float(np.float32(QK ** -0.5))
MASKED = -float(2 ** 99)

TURN1 = 6.28125
TURN2 = float(np.float32(int((2 * np.pi - TURN1) * 2 ** 20) / 2 ** 20))
TURN3 = float(np.float32(2 * np.pi - TURN1 - TURN2))
MAGIC = 1.5 * 2 ** 23
PI_BELOW = float(np.nextafter(np.float32(np.pi), np.float32(0)))


class Lin:

    def __init__(self, base, coef=0, reg=None):
        self.base, self.coef, self.reg = base, coef, reg

    def __add__(self, k):
        if isinstance(k, Lin):
            return Lin(self.base + k.base, self.coef + k.coef, self.reg if self.reg is not None else k.reg)
        return Lin(self.base + k, self.coef, self.reg)

    __radd__ = __add__

    def __sub__(self, k):
        return self + (-k)

    def __mul__(self, k):
        return Lin(self.base * k, self.coef * k, self.reg)

    __rmul__ = __mul__

    def __mod__(self, k):
        assert self.coef % k == 0
        return self.base % k

    def __floordiv__(self, k):
        assert self.coef % k == 0
        return Lin(self.base // k, self.coef // k, self.reg)

    @property
    def value(self):
        return self.base if self.reg is None or not self.coef else self.reg * self.coef + self.base


def as_lin(x):
    return x if isinstance(x, Lin) else Lin(x)


def val(x):
    return as_lin(x).value


def positive(x):
    x = as_lin(x)
    return x.base + (x.coef if x.reg is not None else 0) > 0


def slot(turn):
    return as_lin(turn) % 2


def nth(turn):
    return (as_lin(turn) // 2).value


def cols(start, size):
    return bass.ds(as_lin(start).value, size)


def repeat(eng, steps, unroll, body):
    for j in range(unroll):
        body(Lin(j))
    if steps > unroll:
        with eng.Fori(1, steps // unroll) as i:
            for j in range(unroll):
                body(Lin(j, unroll, i))


def halves(ap):
    return ap.rearrange("p (h t) -> p h t", h=2)


def build(nc, weights, cond, params, tokens, bmat, cmat, positions, out):
    ctx = ExitStack()
    with ctx:
        def sem(name):
            return ctx.enter_context(nc.semaphore(name))

        BASE = 16512

        def sb(name, shape, offset, dt=F32):
            return nc.alloc_sbuf_tensor_at(name, shape, dt, offset=BASE + offset)

        UNIT = DT * L1 * 4
        WH = sb("WH", [P, SPLIT, JOB], 0, F32R)
        WL = sb("WL", [P, SPLIT, JOB], 16384, F32R)
        WR = sb("WR", [P, RAW, JOB], 32768)
        U = [40960 + UNIT * k for k in range(9)]

        def act_tile(name, unit, dt=F32R):
            return sb(name, [P, DT * L1], U[unit], dt)

        XH, XL = act_tile("XH", 0), act_tile("XL", 1)
        YH, YL = act_tile("YH", 2), act_tile("YL", 3)
        OH, OL = act_tile("OH", 4), act_tile("OL", 5)
        MH, ML = act_tile("MH", 6), act_tile("ML", 7)
        H = act_tile("H", 2, F32)
        F = act_tile("F", 3, F32)
        FH = sb("FH", [P, FT * L1], U[3], F32R)
        FL = sb("FL", [P, FT * L1], U[3] + FT * L1 * 4, F32R)
        F2 = act_tile("F2", 0, F32)
        X0 = act_tile("X0", 2, F32)

        A0 = U[6]
        LH = sb("LH", [P, SCORE], A0, F32R)
        LL = sb("LL", [P, SCORE], A0 + 5440, F32R)
        AH = sb("AH", [P, SCORE], A0 + 10880, F32R)
        AL = sb("AL", [P, SCORE], A0 + 16320, F32R)
        QH = sb("QH", [P, L1], A0 + 21760, F32R)
        QL = sb("QL", [P, L1], A0 + 23872, F32R)
        VH = sb("VH", [P, 5 * P], A0 + 25984, F32R)
        VL = sb("VL", [P, 5 * P], A0 + 28544, F32R)

        M0 = U[8]
        E = sb("E", [P, SCORE], M0)
        KH = sb("KH", [P, KPAD], M0 + 5440, F32R)
        KL = sb("KL", [P, KPAD], M0 + 8000, F32R)
        M1 = M0 + 10560
        CT = sb("CT", [P, L1], M1)
        VT = sb("VT", [P, L1], M1 + 2112)
        CV = sb("CV", [P, L1], M1 + 4224)
        PP = sb("PP", [P, L1 + 2], M1 + 6336)
        RB = sb("RB", [P, 2, L1], M1 + 8480)
        SQ = sb("SQ", [P, 2, L1], M1 + 12704)
        M2 = M1 + 16928
        IDENT = sb("IDENT", [P, P], M2)
        ONES = sb("ONES", [P, P], M2 + 512)
        STAGE = sb("STAGE", [P, 2, P], M2 + 1024)
        NTRI = sb("NTRI", [P, P], M2 + 2048, F32R)
        NONE = sb("NONE", [P, P], M2 + 2560, F32R)
        CR = sb("CR", [P, 16], M2 + 3072)
        CH = sb("CH", [P, 16], M2 + 3136, F32R)
        CL = sb("CL", [P, 16], M2 + 3200, F32R)
        MOD = sb("MOD", [P, 24], M2 + 3264)
        NP = params.shape[1]
        PRM = sb("PRM", [P, NP], M2 + 3360)
        M3 = -(-(M2 + 3360 + NP * 4) // 32) * 32
        MB = sb("MB", [P, 24], M3)
        GG = sb("GG", [P, 16], M3 + 96)
        assert M3 + 160 <= 212800

        V = [40960 + 16384 * k for k in range(9)]
        assert V[8] == 172032

        def tile2(name, unit, dt=F32R):
            return sb(name, [P, DT * S2], V[unit], dt)

        X2H, X2L = tile2("X2H", 0), tile2("X2L", 1)
        US = sb("US", [P, GROUPS, NC], V[2])
        SZS = tile2("SZS", 3, F32)
        YG = tile2("YG", 4, F32)
        OMH, OML = tile2("OMH", 6), tile2("OML", 7)
        YGH, YGL = tile2("YGH", 2), tile2("YGL", 5)
        YSH = tile2("YSH", 4)
        YSL = sb("YSL", [P, DT * S2], V[8], F32R)
        G1 = sb("G1", [P, S2], V[8] + 16384)
        G2 = sb("G2", [P, S2], V[8] + 16384 + 2048)
        G3 = sb("G3", [P, S2], V[8] + 16384 + 4096)
        G4 = sb("G4", [P, S2], V[8] + 16384 + 6144)
        M2H, M2L = tile2("M2H", 2), tile2("M2L", 5)
        F3 = tile2("F3", 0, F32)
        RES = tile2("RES", 6, F32)

        def places(start, end):
            at = [start]

            def place(name, shape, dt=F32):
                size = 4 * int(np.prod(shape[1:]))
                t = sb(name, shape, at[0], dt)
                at[0] += -(-size // 32) * 32
                assert at[0] <= end, name
                return t
            return place, at

        place, at5 = places(V[5], V[6])
        UT = place("UT", [P, 2, SUB, NC])
        TK = place("TK", [P, GT, P])
        BT = place("BT", [P, 2, PT_ * P])
        BPR = place("BPR", [P, PT_, SUB, GP])
        BPI = place("BPI", [P, PT_, SUB, GP])
        place, at6 = places(V[6], M1)
        BM = place("BM", [P, 2, PAIRS, GP])
        CM = place("CM", [P, 2, PAIRS, GP])
        BBR = place("BBR", [P, PAIRS, GP])
        BBI = place("BBI", [P, PAIRS, GP])
        NBBI = place("NBBI", [P, PAIRS, GP])
        NCI = place("NCI", [P, PAIRS, GP])
        C1 = place("C1", [P, PAIRS, GP])
        C2 = place("C2", [P, PAIRS, GP])
        PWR = place("PWR", [P, PAIRS, SUB + 1])
        PWI = place("PWI", [P, PAIRS, SUB + 1])
        RVR = place("RVR", [P, PAIRS, SUB])
        RVI = place("RVI", [P, PAIRS, SUB])
        WAR_ = place("WAR_", [P, PAIRS, 8])
        WAI = place("WAI", [P, PAIRS, 8])
        WBR = place("WBR", [P, PAIRS, 8])
        WBI = place("WBI", [P, PAIRS, 8])
        SM = [place(f"SM{i}", [P, PAIRS]) for i in range(24)]
        TS = place("TS", [P, 2, 8 * PAIRS])
        after_setup = at6[0]
        place, at7 = places(after_setup, M2)
        CPR = place("CPR", [P, PT_, SUB + 1, GP])
        CPI = place("CPI", [P, PT_, SUB + 1, GP])
        K1 = place("K1", [P, PT_, SUB + 1, GP])
        K2 = place("K2", [P, PT_, SUB + 1, GP])
        GS = place("GS", [GP, GT * P])
        WC = place("WC", [P, PT_, 8, 8])
        WS = place("WS", [P, PT_, 8, 8])
        VR = place("VR", [P, PT_, NC])
        VI = place("VI", [P, PT_, NC])
        V1 = place("V1", [P, PT_, NC])
        V2 = place("V2", [P, PT_, NC])
        MT = place("MT", [P, PT_, NC])
        SR = place("SR", [P, PT_, NC + 1])
        SI = place("SI", [P, PT_, NC + 1])
        UD = place("UD", [P, GT, NC])
        YT = place("YT", [P, GT, NC])
        YF = place("YF", [P, SUB, NC])

        place, at8 = places(V[2], V[3])
        LQH = place("LQH", [P, LATT * S2], F32R)
        LQL = place("LQL", [P, LATT * S2], F32R)
        LKH = place("LKH", [P, LATT * S2], F32R)
        LKL = place("LKL", [P, LATT * S2], F32R)
        place, at9 = places(V[5], V[6])
        Q2H = [place(f"Q2H{x}", [P, S2], F32R) for x in range(2)]
        Q2L = [place(f"Q2L{x}", [P, S2], F32R) for x in range(2)]
        K2H = [place(f"K2H{x}", [P, S2], F32R) for x in range(2)]
        K2L = [place(f"K2L{x}", [P, S2], F32R) for x in range(2)]
        LATF = sb("LATF", [P, 2 * LATT * S2], V[6])
        place, at10 = places(V[8], M2)
        TAB = place("TAB", [P, S2])
        RO = place("RO", [P, S2])
        POSI = sb("POSI", [P, S2], V[8] + 2048, I32)
        PTH = place("PTH", [P, 4, S2], F32R)
        PTL = place("PTL", [P, 4, S2], F32R)
        V2H = place("V2H", [P, 4 * P], F32R)
        V2L = place("V2L", [P, 4 * P], F32R)
        PB = place("PB", [P, 2, S2])
        VZ = place("VZ", [P, S2])
        MX = place("MX", [P, 8])
        NM = place("NM", [P, 8])
        SU = place("SU", [P, 8])
        RC = place("RC", [P, 8])
        R2 = sb("R2", [P, S2], M2 + 1024)

        u_dram = nc.dram_tensor("u_dram", (D, SUB, NC), F32).ap()
        y_dram = nc.dram_tensor("y_dram", (DT, P, GT, NC), F32).ap()
        res_dram = nc.dram_tensor("res_dram", (P, DT, S2), F32).ap()

        J = [nc.alloc_psum_tensor(f"J{s}", [P, 1024], F32) for s in range(2)]
        Z = nc.alloc_psum_tensor("Z", [P, 1536], F32)
        ZT = nc.alloc_psum_tensor("ZT", [P, 512], F32)
        PTB = [Z[:, 1024:1536], ZT[:]]
        JV = [halves(j[:])[:, :, 0:HALF] for j in J]
        ZV = halves(Z[:, 0:1024])[:, :, 0:HALF]

        g_pre, g_mix, g_pref, g_ffn, b_gate, cw_mix, cw_ffn = (PARAM[k] for k in (
            "g_pre_mix", "g_post_mix", "g_pre_ffn", "g_post_ffn", "b_gate", "conv_w_mix", "conv_w_ffn"))

        (a_bada, a_gpre2, a_gpost2, a_glat, a_bglu, a_are, a_aim, a_ldt, a_d, a_inv, a_sgn) = (PARAM[k] for k in (
            "b_ada", "g_pre_2", "g_post_2", "g_lat", "b_glu", "a_re", "a_im", "log_dt", "ssm_d", "inv_freq", "sign"))

        in_landed = sem("in_landed")
        x_landed = sem("x_landed")
        h_landed = sem("h_landed")
        w_landed = [sem(f"w_landed{s}") for s in range(RAW)]
        w_hi = sem("w_hi")
        w_lo = sem("w_lo")
        job_done = sem("job_done")
        read_out = [sem(f"read_out{s}") for s in range(2)]
        consts = sem("consts")
        const_r = sem("const_r")
        zeroed = sem("zeroed")
        zeroed_act = sem("zeroed_act")
        c_lo = sem("c_lo")
        sq_done = sem("sq_done")
        sq_summed = sem("sq_summed")
        r_step = sem("r_step")
        r_ready = sem("r_ready")
        xf_ready = sem("xf_ready")
        xh_ready = sem("xh_ready")
        xl_ready = sem("xl_ready")
        t_ready = sem("t_ready")
        h_ready = sem("h_ready")
        qk_hi = sem("qk_hi")
        z_done = sem("z_done")
        soft_step = sem("soft_step")
        sp_ready = sem("sp_ready")
        lf_masked = sem("lf_masked")
        lf_hi = sem("lf_hi")
        lf_lo = sem("lf_lo")
        cum_done = sem("cum_done")
        a_exp = sem("a_exp")
        a_masked = sem("a_masked")
        a_hi = sem("a_hi")
        a_lo = sem("a_lo")
        pv_done = sem("pv_done")
        o_hi = sem("o_hi")
        vt_done = sem("vt_done")
        v_hi = sem("v_hi")
        conv_step = sem("conv_step")
        y_hi = sem("y_hi")
        y_lo = sem("y_lo")
        gate_step = sem("gate_step")
        mf_ready = sem("mf_ready")
        m_hi = sem("m_hi")
        m_lo = sem("m_lo")
        u_copied = sem("u_copied")
        fconv_step = sem("fconv_step")
        gelu_done = sem("gelu_done")
        f_hi = sem("f_hi")
        f_lo = sem("f_lo")
        down_done = sem("down_done")
        stored = sem("stored")
        zeroed_pool = sem("zeroed_pool")

        res_saved = sem("res_saved")
        mat_landed = sem("mat_landed")
        mod_step = sem("mod_step")
        setup = sem("setup")
        trig_in = sem("trig_in")
        trig_out = sem("trig_out")
        ut_copied = sem("ut_copied")
        u_stored = [sem(f"u_stored{k}") for k in range(2)]
        us_landed = [sem(f"us_landed{k}") for k in range(2)]
        pool_step = sem("pool_step")
        cp_ready = sem("cp_ready")
        bp_ready = sem("bp_ready")
        ud_ready = sem("ud_ready")
        pow_ready = sem("pow_ready")
        bt_turned = sem("bt_turned")
        g_done = sem("g_done")
        tk_landed = sem("tk_landed")
        b_done = sem("b_done")
        s_ready = sem("s_ready")
        y_done = sem("y_done")
        tk_zeroed = sem("tk_zeroed")
        ygelu = sem("ygelu")
        y_stored = sem("y_stored")
        yf_landed = sem("yf_landed")
        yg_ready = sem("yg_ready")
        pos_landed = sem("pos_landed")
        pattern = sem("pattern")
        up_done = sem("up_done")
        q_top = sem("q_top")
        rope_ready = sem("rope_ready")
        rope_hi = sem("rope_hi")
        q_ready = sem("q_ready")
        kr_ready = sem("kr_ready")
        k_hi = sem("k_hi")
        kr_hi = sem("kr_hi")
        roped = sem("roped")
        v2_turned = sem("v2_turned")
        v2_hi = sem("v2_hi")
        s_done = sem("s_done")
        nm_ready = sem("nm_ready")
        p_exp = sem("p_exp")
        rc_ready = sem("rc_ready")
        mx_ready = sem("mx_ready")
        pn_ready = sem("pn_ready")
        pt_done = sem("pt_done")
        pt_hi = sem("pt_hi")
        pt_lo = sem("pt_lo")
        pv2_done = sem("pv2_done")
        om_ready = sem("om_ready")
        om_hi = sem("om_hi")
        om_lo = sem("om_lo")
        yg_hi = sem("yg_hi")
        yg_lo = sem("yg_lo")
        glu_step = sem("glu_step")
        ys_hi = sem("ys_hi")
        ys_lo = sem("ys_lo")
        m2_ready = sem("m2_ready")
        m2_hi = sem("m2_hi")
        m2_lo = sem("m2_lo")
        res_landed = sem("res_landed")
        fin = sem("fin")
        stored2 = sem("stored2")

        def down_slots_after(m):
            return min(N_DOWN + FT * (m + 1) // 8 + SPLIT, N_U + SPLIT - 1)

        block = ctx.enter_context(nc.Block())

        @block.sync
        def _(sp):
            sp.dma_start(PRM[:], params).then_inc(in_landed, 16)
            sp.dma_start(CR[:], cond).then_inc(in_landed, 16)
            x_view = tokens.rearrange("(m p) t -> p m t", p=P)
            for m in range(0, DT, 2):
                sp.dma_start(X0[:, m * L1:(m + 2) * L1].rearrange("p (m t) -> p m t", m=2),
                             x_view[:, m:m + 2]).then_inc(x_landed, 16)

            def load_weights(n, slots=RAW):
                n = as_lin(n)
                for s in range(slots):
                    if positive(n + s - RAW + 1):
                        sp.wait_ge(w_lo, val(n + s - RAW + 1))
                    sp.dma_start(WR[:, s, :], weights[cols(n + s, 1)].rearrange("a p n -> (a p) n"))\
                      .then_inc(w_landed[s], 16)

            def stream(first, last):
                repeat(sp, (last - first) // RAW, 1, lambda i: load_weights(first + RAW * i))

            stream(0, N_OUT + 2)
            sp.wait_ge(job_done, N_OUT)
            sp.dma_start(H[:].rearrange("p (m t) -> p m t", m=DT), x_view).then_inc(h_landed, 16)
            def load_one(n):
                s = n % RAW
                sp.wait_ge(w_lo, val(n - RAW + 1))
                sp.dma_start(WR[:, s, :], weights[n]).then_inc(w_landed[s], 16)

            stream(N_OUT + 2, N_U)
            for m in range(3):
                load_one(N_U + m)
            sp.wait_ge(h_ready, 2 * DT)
            sp.dma_start(res_dram, H[:].rearrange("p (m t) -> p m t", m=DT)[:, :, META:]).then_inc(res_saved, 16)
            sp.dma_start(BM[:], bmat).then_inc(mat_landed, 16)
            sp.dma_start(CM[:], cmat).then_inc(mat_landed, 16)

            def store_u(m):
                sp.wait_ge(ut_copied, val(m + 1))
                sp.dma_start(u_dram[m * P:(m + 1) * P], UT[:, m % 2]).then_inc(u_stored[m % 2], 16)

            def load_us(half):
                for k in range(2):
                    sp.wait_ge(u_stored[k], val(16 * (2 * half + 2)))
                g = slice(half * GROUPS // 2, (half + 1) * GROUPS // 2)
                src = u_dram.rearrange("(g p) j c -> j p g c", p=GP)
                for j in range(SUB):
                    sp.dma_start(US[j * GP:(j + 1) * GP, g], src[j][:, g]).then_inc(us_landed[half], 16)

            for m in range(3, DT):
                load_one(N_U + m)
                if m >= 4:
                    store_u(m - 4)
            sp.wait_ge(res_saved, 16)
            sp.wait_ge(xl_ready, 3 * DT)
            for k in range(4):
                load_one(N_SSM + k)
                store_u(4 + k)
                if k == 0:
                    load_us(0)
            load_us(1)

            def load_kernel(m):
                sp.wait_ge(read_out[slot(T_SSM + 5 * m + 2)], nth(T_SSM + 5 * m + 2) + 1)
                if positive(m):
                    sp.wait_ge(y_done, val(m))
                sp.wait_ge(tk_zeroed, 1)
                src = GS[:].rearrange("p (g n) -> p g n", g=GT)
                for j in range(SUB):
                    sp.dma_start(TK[j * GP:(j + 1) * GP, :, j * GP:], src[:, :, 0:P - j * GP]).then_inc(tk_landed, 16)

            def turn_y(m):
                sp.wait_ge(ygelu, val(m + 1))
                sp.dma_start(y_dram[m], YT[:]).then_inc(y_stored, 16)
                sp.wait_ge(y_stored, 16 * (m + 1))
                if positive(m):
                    sp.wait_ge(yg_ready, val(m))
                src = y_dram[m].rearrange("(i q) g c -> g q i c", q=GP)
                for g in range(GT):
                    sp.dma_start(YF[g * GP:(g + 1) * GP], src[g]).then_inc(yf_landed, 16)

            for m in range(DT):
                load_kernel(m)
                if N_SSM + 4 + m < N_ATT:
                    load_one(N_SSM + 4 + m)
                turn_y(m)
            for n in range(N_SSM + 4 + DT, N_ATT):
                load_one(n)
            sp.dma_start(POSI[64:P], positions.partition_broadcast(64)).then_inc(pos_landed, 16)
            n = N_ATT
            if n % 2:
                load_one(n)
                n += 1
            stream(n, n + (N_LAST - n) // 2 * 2)
            for n in range(n + (N_LAST - n) // 2 * 2, N_LAST):
                load_one(n)
            sp.wait_ge(job_done, N_OUT2)
            sp.dma_start(RES[:].rearrange("p (m t) -> p m t", m=DT), res_dram).then_inc(res_landed, 16)
            o_view = out.rearrange("(m p) t -> p m t", p=P)
            for m in range(DT):
                sp.wait_ge(fin, val(m + 1))
                sp.dma_start(o_view[:, m], F3[:, m * S2:(m + 1) * S2]).then_inc(stored, 16)
            sp.wait_ge(stored, 16 * DT)

        @block.tensor
        def _(pe):
            def job(n, t, xh, xl):
                n, t = as_lin(n), as_lin(t)
                s, o = n % SPLIT, J[t % 2]
                if positive(t - 1):
                    pe.wait_ge(read_out[slot(t)], nth(t))
                pe.wait_ge(w_lo, val(n + 1))
                for k in range(8):
                    w = slice(k * P, (k + 1) * P)
                    for i, (ws, xs) in enumerate(((WH, xh), (WH, xl), (WL, xh))):
                        for h in range(2):
                            mm = pe.matmul(o[:, 512 * h:512 * h + HALF], ws[:, s, w],
                                           xs[:, k * L1 + h * HALF:k * L1 + (h + 1) * HALF],
                                           start=(k == 0 and i == 0), stop=(k == 7 and i == 2))
                mm.then_inc(job_done, 1)

            def ada(n, t):
                n, t = as_lin(n), as_lin(t)
                s, o = n % SPLIT, J[t % 2]
                pe.wait_ge(read_out[slot(t)], nth(t))
                pe.wait_ge(w_lo, val(n + 1))
                for k in range(8):
                    w = slice(k * P, (k + 1) * P)
                    for i, (ws, xs) in enumerate(((WH, CH), (WH, CL), (WL, CH))):
                        mm = pe.matmul(o[:, 0:2], ws[:, s, w], xs[:, 2 * k:2 * k + 2],
                                       start=(k == 0 and i == 0), stop=(k == 7 and i == 2))
                mm.then_inc(job_done, 1)

            def sum_squares(q, first, last):
                q = as_lin(q)
                pe.wait_ge(sq_done, val(q + 1))
                for h in range(2):
                    mm = pe.matmul(Z[:, 512 * h:512 * h + HALF], ONES[:],
                                   SQ[:, q % 2, h * HALF:(h + 1) * HALF], start=first, stop=last,
                                   skip_group_check=True)
                mm.then_inc(sq_summed, 1)

            pe.wait_ge(consts, 3)
            for m in range(DT):
                sum_squares(Q_PRE + m, m == 0, m == DT - 1)

            def scores(h):
                h = as_lin(h)
                r = slice(64 * (h % 2), 64 * (h % 2) + 64)
                if positive(h):
                    pe.wait_ge(a_exp, val(h))
                banks = set()
                for kt, t0, w, c in PIECES:
                    for ks, qs in ((KH, QH), (KH, QL), (KL, QH)):
                        mm = pe.matmul(Z[:, c:c + w], ks[r, kt * P:(kt + 1) * P], qs[r, t0:t0 + w],
                                       start=c // 512 not in banks, stop=True, skip_group_check=True)
                        banks.add(c // 512)
                mm.then_inc(z_done, 1)

            def accumulate(h):
                h = as_lin(h)
                pe.wait_ge(lf_lo, val(h + 1))
                for kt, t0, w, c in PIECES:
                    for jt, u0, v, d in PIECES:
                        a, b = max(t0, u0), min(t0 + w, u0 + v)
                        if jt < kt or a >= b:
                            continue
                        for ls in (LH, LL):
                            mm = pe.matmul(Z[:, c + a - t0:c + b - t0], (NTRI if jt == kt else NONE)[:],
                                           ls[:, d + a - u0:d + b - u0], start=False, stop=True,
                                           skip_group_check=True)
                mm.then_inc(cum_done, 1)

            def values(h, t):
                h, t = as_lin(h), as_lin(t)
                pe.wait_ge(read_out[slot(t)], nth(t))
                pe.wait_ge(a_lo, val(h + 1))
                o = J[t % 2]
                parts = [(kt, max(t0, x), min(t0 + w, x + HALF), c - t0)
                         for x in (0, HALF) for kt, t0, w, c in PIECES
                         if max(t0, x) < min(t0 + w, x + HALF)]
                seen = set()
                for kt, a, b, c in parts:
                    half = a // HALF
                    at = 512 * half - HALF * half
                    for vs, ps in ((VH, AH), (VH, AL), (VL, AH)):
                        mm = pe.matmul(o[:, at + a:at + b], vs[:, kt * P:(kt + 1) * P], ps[:, c + a:c + b],
                                       start=half not in seen, stop=True, skip_group_check=True)
                        seen.add(half)
                mm.then_inc(pv_done, 1)

            def turn_values(t, tiles):
                t = as_lin(t)
                pe.wait_ge(read_out[slot(t)], nth(t))
                for i, kt in enumerate(tiles):
                    w = min(P, L1 - kt * P)
                    mm = pe.transpose(J[t % 2][0:w, P * i:P * (i + 1)], VT[:, kt * P:kt * P + w], IDENT[:])
                mm.then_inc(vt_done, 1)

            pe.wait_ge(c_lo, 1)
            pe.wait_ge(const_r, 2)
            pe.wait_ge(zeroed_act, 2)
            pe.wait_ge(zeroed, 2)
            pe.wait_ge(xl_ready, DT)

            def mix(m):
                n, t, h = N_MIX + 8 * m, T_MIX + 12 * m, 2 * m
                job(n, t, XH, XL)
                job(n + 1, t + 1, XH, XL)
                pe.wait_ge(read_out[slot(t)], nth(t) + 1)
                pe.wait_ge(read_out[slot(t + 1)], nth(t + 1) + 1)
                scores(h)
                if m.base or m.reg is not None:
                    values(h - 1, t + 2)
                job(n + 2, t + 3, XH, XL)
                job(n + 3, t + 4, XH, XL)
                accumulate(h)
                pe.wait_ge(read_out[slot(t + 3)], nth(t + 3) + 1)
                turn_values(t + 5, (0, 1, 2))
                turn_values(t + 6, (3, 4))
                job(n + 4, t + 7, XH, XL)
                scores(h + 1)
                job(n + 5, t + 8, XH, XL)
                pe.wait_ge(read_out[slot(t + 5)], nth(t + 5) + 1)
                pe.wait_ge(read_out[slot(t + 6)], nth(t + 6) + 1)
                values(h, t + 9)
                ada(n + 6, t + 10)
                ada(n + 7, t + 11)
                accumulate(h + 1)

            repeat(pe, DT, 1, mix)
            values(HEADS - 1, T_MIX + 12 * DT)

            def gates(m):
                n, t = N_GATE + 4 * m, T_GATE + 4 * m
                job(n, t, XH, XL)
                job(n + 1, t + 1, XH, XL)
                if m.reg is None and m.base == 0:
                    pe.wait_ge(y_lo, DT)
                    pe.wait_ge(read_out[slot(T_MIX + 12 * DT)], nth(T_MIX + 12 * DT) + 1)
                job(n + 2, t + 2, YH, YL)
                job(n + 3, t + 3, OH, OL)

            repeat(pe, DT, 1, gates)

            pe.wait_ge(m_lo, DT)
            for m in range(DT):
                job(N_OUT + 2 * m, T_OUT + 2 * m, MH, ML)
                if m:
                    sum_squares(Q_MIX + m - 1, m == 1, False)
                ada(N_OUT + 2 * m + 1, T_OUT + 2 * m + 1)
            sum_squares(Q_MIX + DT - 1, False, True)
            pe.wait_ge(r_ready, 2)
            for m in range(DT):
                sum_squares(Q_PREF + m, m == 0, m == DT - 1)
            pe.wait_ge(xl_ready, 2 * DT)

            def up(i):
                job(N_UP + 2 * i, T_UP + 2 * i, XH, XL)
                job(N_UP + 2 * i + 1, T_UP + 2 * i + 1, XH, XL)

            repeat(pe, FT, 2, up)

            pe.wait_ge(f_lo, FT)
            for m in range(DT):
                t = T_DOWN + m
                pe.wait_ge(read_out[slot(t)], nth(t))
                for k in range(FT):
                    b = FT * m + k
                    n, w = N_DOWN + b // 8, slice(b % 8 * P, (b % 8 + 1) * P)
                    if b % 8 == 0:
                        pe.wait_ge(w_lo, val(n + 1))
                    for i, (ws, xs) in enumerate(((WH, FH), (WH, FL), (WL, FH))):
                        for h in range(2):
                            mm = pe.matmul(J[t % 2][:, 512 * h:512 * h + HALF], ws[:, n % SPLIT, w],
                                           xs[:, k * L1 + h * HALF:k * L1 + (h + 1) * HALF],
                                           start=(k == 0 and i == 0), stop=(k == FT - 1 and i == 2))
                    if b % 8 == 7:
                        mm.then_inc(job_done, 1)
                    elif k == FT - 1:
                        mm.then_inc(down_done, 1)
                if m:
                    if m == 1:
                        pe.wait_ge(r_ready, 3)
                    sum_squares(Q_FFN + m - 1, m == 1, False)
            sum_squares(Q_FFN + DT - 1, False, True)

            def sum_squares2(q, first, last):
                q = as_lin(q)
                pe.wait_ge(sq_done, val(q + 1))
                pe.matmul(Z[:, 0:S2], ONES[:], SQ[:, q % 2, 0:S2], start=first, stop=last,
                          skip_group_check=True).then_inc(sq_summed, 1)

            def job2(n, t, xh, xl):
                n, t = as_lin(n), as_lin(t)
                s, o = n % SPLIT, J[t % 2]
                pe.wait_ge(read_out[slot(t)], nth(t))
                pe.wait_ge(w_lo, val(n + 1))
                for k in range(8):
                    w = slice(k * P, (k + 1) * P)
                    for i, (ws, xs) in enumerate(((WH, xh), (WH, xl), (WL, xh))):
                        mm = pe.matmul(o[:, 0:S2], ws[:, s, w], xs[:, k * S2:(k + 1) * S2],
                                       start=(k == 0 and i == 0), stop=(k == 7 and i == 2))
                mm.then_inc(job_done, 1)

            pe.wait_ge(r_step, 2 * 3 + 2)
            for m in range(DT):
                sum_squares2(Q_PRE2 + m, m == 0, m == DT - 1)
            pe.wait_ge(xl_ready, 3 * DT)
            for m in range(DT):
                job2(N_U + m, T_U + m, X2H, X2L)

            def half_rows(x):
                return slice(64 * x, 64 * x + 64)

            for m in range(DT):
                t = T_SSM + 5 * m
                job2(N_SSM + m, t, X2H, X2L)
                pe.wait_ge(read_out[slot(t + 1)], nth(t + 1))
                pe.wait_ge(bp_ready, val(m + 1))
                for x, b in enumerate((BPR, BPI)):
                    for pr in range(PT_):
                        mm = pe.transpose(J[(t + 1) % 2][:, 512 * x + P * pr:512 * x + P * (pr + 1)],
                                          b[:, pr].rearrange("p j q -> p (j q)"), IDENT[:])
                mm.then_inc(bt_turned, 1)
                pe.wait_ge(read_out[slot(t + 2)], nth(t + 2))
                pe.wait_ge(cp_ready, val(m + 1))
                for g in range(GT):
                    pr, r = g // 2, half_rows(g % 2)
                    for x, (bb, cp) in enumerate(((BBR, CPR), (BBI, CPI))):
                        at = 512 * (g % 2) + P * (g // 2)
                        mm = pe.matmul(J[(t + 2) % 2][0:GP, at:at + P], bb[r, PT_ * m + pr],
                                       cp[r, pr, 0:SUB].rearrange("p i q -> p (i q)"),
                                       start=x == 0, stop=x == 1, skip_group_check=True)
                mm.then_inc(g_done, 1)
                pe.wait_ge(read_out[slot(t + 3)], nth(t + 3))
                pe.wait_ge(read_out[slot(t + 1)], nth(t + 1) + 1)
                pe.wait_ge(us_landed[m // 4], 16 * SUB)
                for g in range(GT):
                    pr, r = g // 2, half_rows(g % 2)
                    for x in range(2):
                        mm = pe.matmul(J[(t + 3) % 2][r, 512 * x + NC * pr:512 * x + NC * (pr + 1)],
                                       BT[:, x, P * pr + 64 * (g % 2):P * pr + 64 * (g % 2) + 64],
                                       US[:, GT * m + g], start=True, stop=True, skip_group_check=True)
                mm.then_inc(b_done, 1)
                pe.wait_ge(read_out[slot(t + 4)], nth(t + 4))
                pe.wait_ge(tk_landed, val(16 * SUB * (m + 1)))
                pe.wait_ge(s_ready, val(m + 1))
                for g in range(GT):
                    pr, r = g // 2, half_rows(g % 2)
                    at = 512 * (g % 2) + NC * (g // 2)
                    o = J[(t + 4) % 2][:, at:at + NC]
                    pe.matmul(o, TK[:, g], US[:, GT * m + g], start=True, stop=False, skip_group_check=True)
                    for x, (cp, s) in enumerate(((CPR, SR), (CPI, SI))):
                        mm = pe.matmul(o, cp[r, pr, 1:SUB + 1].rearrange("p i q -> p (i q)"), s[r, pr, 0:NC],
                                       start=False, stop=x == 1, skip_group_check=True)
                mm.then_inc(y_done, 1)

            for k in range(4):
                job2(N_LAT + k, T_LAT + k, X2H, X2L)
                if k:
                    if k == 3:
                        pe.wait_ge(r_step, 2 * 5 + 2)
                    sum_squares2(Q_LAT + k - 1, k % 2 == 1, k % 2 == 0)
            job2(N_LAT + 4, T_LAT + 4, X2H, X2L)
            sum_squares2(Q_LAT + 3, False, True)
            pe.wait_ge(xl_ready, 3 * DT + 2 * LATT)
            pe.wait_ge(kr_ready, 1)

            def attend(m):
                n, t, h = N_ATT + 2 * m, T_ATT + 8 * m, 2 * m
                s = n % SPLIT
                pe.wait_ge(w_lo, val(n + 1))
                for j, (xh, xl) in enumerate(((LQH, LQL), (LQH, LQL), (LKH, LKL), (LKH, LKL))):
                    pe.wait_ge(read_out[slot(t + j)], nth(t + j))
                    for k in range(LATT):
                        w = slice((LATT * j + k) * P, (LATT * j + k + 1) * P)
                        for i, (ws, xs) in enumerate(((WH, xh), (WH, xl), (WL, xh))):
                            mm = pe.matmul(J[(t + j) % 2][:, 0:S2], ws[:, s, w], xs[:, k * S2:(k + 1) * S2],
                                           start=(k == 0 and i == 0), stop=(k == LATT - 1 and i == 2))
                    if j < 3:
                        mm.then_inc(up_done, 1)
                mm.then_inc(job_done, 1)

                def score(u):
                    g, x, i = 8 * m + u, u // 4, u % 4
                    if positive(g - 1):
                        pe.wait_ge(p_exp, val(g - 1))
                    for a, (qs, ks) in enumerate(((Q2H, K2H), (Q2H, K2L), (Q2L, K2H))):
                        mm = pe.matmul(Z[:, 512 * (u % 2):512 * (u % 2) + P * (i + 1)], qs[x][:, P * i:P * (i + 1)],
                                       ks[x][:, 0:P * (i + 1)], start=a == 0, stop=a == 2, skip_group_check=True)
                    mm.then_inc(s_done, 1)

                def turn_weights(u):
                    g, i = 8 * m + u, u % 4
                    pe.wait_ge(pn_ready, val(g + 1))
                    if positive(g - 1):
                        pe.wait_ge(pt_lo, val(g - 1))
                    for j in range(i + 1):
                        mm = pe.transpose(PTB[u % 2][:, P * j:P * (j + 1)], PB[:, u % 2, P * j:P * (j + 1)], IDENT[:])
                    mm.then_inc(pt_done, 1)

                def values2(x):
                    pe.wait_ge(read_out[slot(t + 6 + x)], nth(t + 6 + x))
                    pe.wait_ge(read_out[slot(t + 4)], nth(t + 4) + 1)
                    pe.wait_ge(pt_lo, val(8 * m + 4 * x + 4))
                    for j in range(4):
                        for a, (vs, ps) in enumerate(((V2H, PTH), (V2H, PTL), (V2L, PTH))):
                            mm = pe.matmul(J[(t + 6 + x) % 2][:, P * j:S2], vs[:, P * j:P * (j + 1)],
                                           ps[:, j, P * j:], start=(j == 0 and a == 0), stop=(j == 3 and a == 2),
                                           skip_group_check=True)
                    mm.then_inc(pv2_done, 1)

                pe.wait_ge(read_out[slot(t + 2)], nth(t + 2) + 1)
                pe.wait_ge(read_out[slot(t + 3)], nth(t + 3) + 1)
                pe.wait_ge(q_ready, val(h + 2))
                score(0)
                score(1)
                pe.wait_ge(read_out[slot(t + 4)], nth(t + 4))
                for k in range(4):
                    mm = pe.transpose(J[(t + 4) % 2][:, P * k:P * (k + 1)], VZ[:, P * k:P * (k + 1)], IDENT[:])
                mm.then_inc(v2_turned, 1)
                job2(n + 1, t + 5, X2H, X2L)
                for u in range(8):
                    turn_weights(u)
                    if u + 2 < 8:
                        score(u + 2)
                    if u == 4:
                        values2(0)
                values2(1)

            repeat(pe, DT, 2, attend)

            pe.wait_ge(yg_lo, DT)

            def glu(m):
                job2(N_GLU + 2 * m, T_GLU + 2 * m, YGH, YGL)
                job2(N_GLU + 2 * m + 1, T_GLU + 2 * m + 1, YGH, YGL)

            repeat(pe, DT, 2, glu)
            pe.wait_ge(om_lo, 2 * DT)
            pe.wait_ge(ys_lo, DT)

            def merge(m):
                for j, (xh, xl) in enumerate(((X2H, X2L), (X2H, X2L), (YSH, YSL), (OMH, OML))):
                    job2(N_MERGE + 4 * m + j, T_MERGE + 4 * m + j, xh, xl)

            repeat(pe, DT, 1, merge)
            pe.wait_ge(m2_lo, DT)
            for m in range(DT):
                job2(N_OUT2 + m, T_OUT2 + m, M2H, M2L)
                if m:
                    sum_squares2(Q_POST2 + m - 1, m == 1, False)
            sum_squares2(Q_POST2 + DT - 1, False, True)

        @block.scalar
        def _(act):
            def split_hi(n):
                n = as_lin(n)
                if n.base >= N_LAST:
                    return
                act.wait_ge(w_landed[n % RAW], val(16 * (n // RAW) + 16))
                if positive(n - SPLIT + 1):
                    act.wait_ge(job_done, val(n - SPLIT + 1))
                act.activation(WH[:, n % SPLIT, :], WR[:, n % RAW, :], ACT.Copy).then_inc(w_hi, 1)

            def square(q, src, inc=None):
                q = as_lin(q)
                if positive(q - 1):
                    act.wait_ge(sq_summed, val(q - 1))
                act.activation(halves(SQ[:, q % 2, :]), src, ACT.Square).then_inc(sq_done, 1)

            def job_result(t, n):
                act.wait_ge(job_done, val(as_lin(n) + 1))
                return JV[as_lin(t) % 2]

            act.wait_ge(consts, 3)
            act.activation(NTRI[:], STAGE[:, 0, :], ACT.Copy, scale=-1.0).then_inc(const_r, 1)
            act.activation(NONE[:], STAGE[:, 1, :], ACT.Copy, scale=-1.0).then_inc(const_r, 1)
            act.activation(KH[:, L1:], STAGE[:, 1, 0:KPAD - L1], ACT.Copy, scale=0.0).then_inc(zeroed_act, 1)
            act.activation(KL[:, L1:], STAGE[:, 1, 0:KPAD - L1], ACT.Copy, scale=0.0).then_inc(zeroed_act, 1)
            act.wait_ge(in_landed, 32)
            act.activation(CH[:], CR[:], ACT.Copy).then_inc(w_hi, 1)

            for m in range(DT):
                if m % 2 == 0:
                    act.wait_ge(x_landed, 16 * (DT // 2))
                square(Q_PRE + m, halves(X0[:, m * L1:(m + 1) * L1]))
            for n in range(SPLIT - 1):
                split_hi(n)

            def root(e, width=L1):
                r = RB[:, e % 2, 0:width]
                act.wait_ge(r_step, val(2 * e + 2))
                act.activation(r, r, ACT.Sqrt).then_inc(r_ready, 1)

            root(0)
            for m in range(DT):
                act.wait_ge(xf_ready, val(m + 1))
                act.activation(XH[:, m * L1:(m + 1) * L1], [CT, VT][m % 2][:], ACT.Copy).then_inc(xh_ready, 1)

            def softplus(h):
                h = as_lin(h)
                act.wait_ge(z_done, val(h + 1))
                if positive(h):
                    act.wait_ge(a_lo, val(h))
                act.activation(E[:], Z[:, 0:SCORE], ACT.Abs).then_inc(soft_step, 1)
                act.wait_ge(soft_step, val(3 * h + 1))
                act.activation(E[:], E[:], ACT.Exp, scale=-1.0).then_inc(soft_step, 1)
                act.wait_ge(soft_step, val(3 * h + 2))
                act.activation(E[:], E[:], ACT.Ln, bias=1.0).then_inc(soft_step, 1)

            def fail_hi(h):
                h = as_lin(h)
                act.wait_ge(lf_masked, val(2 * h + 2))
                if positive(h):
                    act.wait_ge(cum_done, val(h))
                act.activation(LH[:], E[:], ACT.Copy).then_inc(lf_hi, 1)

            def weight_exp(h):
                h = as_lin(h)
                act.wait_ge(cum_done, val(h + 1))
                act.wait_ge(lf_lo, val(h + 1))
                act.activation(E[:], Z[:, 0:SCORE], ACT.Exp).then_inc(a_exp, 1)

            def weight_hi(h):
                h = as_lin(h)
                act.wait_ge(a_masked, val(2 * h + 2))
                if positive(h):
                    act.wait_ge(pv_done, val(h))
                act.activation(AH[:], E[:], ACT.Copy).then_inc(a_hi, 1)

            def head_out(h, m, t):
                h = as_lin(h)
                r = slice(64 * (h % 2), 64 * (h % 2) + 64)
                act.wait_ge(pv_done, val(h + 1))
                act.activation(halves(OH[r, cols(m * L1, L1)]), JV[as_lin(t) % 2][r], ACT.Copy).then_inc(o_hi, 1)

            def mix(m):
                n, t, h = N_MIX + 8 * m, T_MIX + 12 * m, 2 * m
                later = m.base or m.reg is not None
                split_hi(n + 3)
                src = job_result(t, n)
                if positive(h):
                    act.wait_ge(z_done, val(h))
                act.activation(halves(QH[:]), src, ACT.Copy, scale=0.125).then_inc(qk_hi, 1)
                split_hi(n + 4)
                src = job_result(t + 1, n + 1)
                act.activation(halves(KH[:, 0:L1]), src, ACT.Copy).then_inc(qk_hi, 1)
                softplus(h)
                if later:
                    head_out(h - 1, m - 1, t + 2)
                split_hi(n + 5)
                src = job_result(t + 3, n + 2)
                if positive(2 * m):
                    act.wait_ge(vt_done, val(2 * m))
                act.activation(halves(VT[:]), src, ACT.Copy).then_inc(read_out[(t + 3) % 2], 1)
                fail_hi(h)
                split_hi(n + 6)
                src = job_result(t + 4, n + 3)
                if positive(m):
                    act.wait_ge(y_lo, val(m))
                act.activation(halves(CT[:]), src, ACT.Copy).then_inc(read_out[(t + 4) % 2], 1)
                weight_exp(h)
                act.wait_ge(vt_done, val(2 * m + 1))
                if positive(h):
                    act.wait_ge(pv_done, val(h))
                act.activation(VH[:, 0:3 * P], J[(t + 5) % 2][:, 0:3 * P], ACT.Copy).then_inc(v_hi, 1)
                act.wait_ge(vt_done, val(2 * m + 2))
                act.activation(VH[:, 3 * P:4 * P], J[(t + 6) % 2][:, 0:P], ACT.Copy)
                act.activation(VH[0:META, 4 * P:], J[(t + 6) % 2][0:META, P:2 * P], ACT.Copy).then_inc(v_hi, 1)
                weight_hi(h)
                split_hi(n + 7)
                split_hi(n + 8)
                softplus(h + 1)
                act.wait_ge(read_out[slot(t + 8)], nth(t + 8) + 1)
                act.activation(YH[:, cols(m * L1, L1)], CT[:], ACT.Copy).then_inc(y_hi, 1)
                head_out(h, m, t + 9)
                fail_hi(h + 1)
                split_hi(n + 9)
                split_hi(n + 10)
                weight_exp(h + 1)
                weight_hi(h + 1)

            repeat(act, DT, 1, mix)
            head_out(HEADS - 1, DT - 1, T_MIX + 12 * DT)

            def gates(m):
                n, t = N_GATE + 4 * m, T_GATE + 4 * m
                for j, g in enumerate((CT, CV)):
                    split_hi(n + 3 + j)
                    src = job_result(t + j, n + j)
                    if m.base == 0 and m.reg is None:
                        act.wait_ge(y_lo, DT)
                    else:
                        act.wait_ge(read_out[slot(t + j - 2)], nth(t + j - 2) + 1)
                    act.activation(halves(g[:]), src, ACT.Sigmoid, bias=PRM[:, cols(b_gate + j * DT + m, 1)])\
                       .then_inc(read_out[(t + j) % 2], 1)
                split_hi(n + 5)
                split_hi(n + 6)
                act.wait_ge(mf_ready, val(m + 1))
                act.activation(MH[:, cols(m * L1, L1)], PP[:, 2:], ACT.Copy).then_inc(m_hi, 1)

            repeat(act, DT, 1, gates)

            for m in range(DT):
                n, t = N_OUT + 2 * m, T_OUT + 2 * m
                split_hi(n + 3)
                split_hi(n + 4)
                src = job_result(t, n)
                act.activation(halves(F[:, m * L1:(m + 1) * L1]), src, ACT.Copy)
                act.wait_ge(sq_summed, val(Q_MIX + m - 1))
                act.activation(halves(SQ[:, m % 2, :]), src, ACT.Square).then_inc(sq_done, 1)

            def pre_norm_hi(q, e, count):
                for m in range(DT):
                    act.wait_ge(h_ready, val(count * DT + m + 1))
                    square(q + m, halves(H[:, m * L1:(m + 1) * L1]))
                root(e)
                for m in range(DT):
                    act.wait_ge(xf_ready, val((count + 1) * DT + m + 1))
                    act.activation(XH[:, m * L1:(m + 1) * L1], [CT, VT][m % 2][:], ACT.Copy).then_inc(xh_ready, 1)

            root(1)
            pre_norm_hi(Q_PREF, 2, 0)

            def up(i):
                n, t = N_UP + 2 * i, T_UP + 2 * i
                split_hi(n + 3)
                src = job_result(t, n)
                if positive(3 * i):
                    act.wait_ge(fconv_step, val(3 * i))
                act.activation(halves(PP[:, 2:]), src, ACT.Copy).then_inc(read_out[t % 2], 1)
                split_hi(n + 4)
                act.wait_ge(fconv_step, val(3 * i + 3))
                if i.base or i.reg is not None:
                    act.wait_ge(read_out[slot(t - 1)], nth(t - 1) + 1)
                act.activation(VT[:], CV[:], ACT.Gelu_apprx_tanh).then_inc(gelu_done, 1)
                act.wait_ge(read_out[slot(t + 1)], nth(t + 1) + 1)
                act.activation(FH[:, cols(i * L1, L1)], CT[:], ACT.Copy).then_inc(f_hi, 1)

            repeat(act, FT, 2, up)

            n = N_DOWN + SPLIT - 1
            for m in range(DT):
                t = T_DOWN + m
                while n < down_slots_after(m):
                    split_hi(n)
                    n += 1
                if m % 4 == 3:
                    act.wait_ge(job_done, val(N_DOWN + FT * (m + 1) // 8))
                else:
                    act.wait_ge(down_done, val(m + 1 - m // 4))
                src = JV[t % 2]
                act.activation(halves(F2[:, m * L1:(m + 1) * L1]), src, ACT.Copy)
                act.wait_ge(sq_summed, val(Q_FFN + m - 1))
                act.activation(halves(SQ[:, m % 2, :]), src, ACT.Square).then_inc(sq_done, 1)
            root(3)

            def square2(q, src):
                q = as_lin(q)
                act.wait_ge(sq_summed, val(q - 1))
                return act.activation(SQ[:, q % 2, 0:S2], src, ACT.Square).then_inc(sq_done, 1)

            def result2(n, t):
                act.wait_ge(job_done, val(as_lin(n) + 1))
                return J[as_lin(t) % 2][:, 0:S2]

            for m in range(DT):
                act.wait_ge(h_ready, val(DT + m + 1))
                square2(Q_PRE2 + m, H[:, m * L1 + META:(m + 1) * L1])
            root(4, S2)
            for m in range(DT):
                act.wait_ge(xf_ready, val(2 * DT + m + 1))
                act.activation(X2H[:, m * S2:(m + 1) * S2], [CT, VT][m % 2][:, 0:S2], ACT.Identity,
                               bias=MB[:, m:m + 1]).then_inc(xh_ready, 1)
            for m in range(DT):
                split_hi(N_U + 3 + m)
                src = result2(N_U + m, T_U + m)
                if m >= 2:
                    act.wait_ge(u_stored[m % 2], val(16 * (m // 2)))
                act.activation(UT[:, m % 2], src.rearrange("p (c j) -> p j c", j=SUB), ACT.Copy)\
                   .then_inc(ut_copied, 1)
                if m == 0:
                    act.wait_ge(trig_in, 1)
                    act.activation(SM[0][:], PRM[:, a_ldt:a_ldt + PAIRS], ACT.Exp).then_inc(trig_out, 1)
                if m == 1:
                    act.wait_ge(trig_in, 2)
                    act.activation(SM[5][:], SM[1][:], ACT.Exp).then_inc(trig_out, 1)
                if m == 2:
                    act.wait_ge(trig_in, 3)
                    act.activation(SM[6][:], SM[2][:], ACT.Sin).then_inc(trig_out, 1)
                    act.activation(SM[7][:], SM[2][:], ACT.Sin, scale=0.5).then_inc(trig_out, 1)

            for m in range(DT):
                n, t = N_SSM + m, T_SSM + 5 * m
                split_hi(n + 3)
                src = result2(n, t)
                act.activation(SZS[:, m * S2:(m + 1) * S2], src, ACT.Silu).then_inc(read_out[t % 2], 1)
                act.wait_ge(bt_turned, val(m + 1))
                if positive(m):
                    act.wait_ge(b_done, val(m))
                act.activation(BT[:].rearrange("p x n -> p (x n)"), J[(t + 1) % 2][:], ACT.Copy)\
                   .then_inc(read_out[(t + 1) % 2], 1)
                act.wait_ge(g_done, val(m + 1))
                if positive(16 * SUB * m):
                    act.wait_ge(tk_landed, val(16 * SUB * m))
                act.activation(GS[:].rearrange("p (r x n) -> p x r n", x=2, n=P),
                               J[(t + 2) % 2][0:GP, :].rearrange("p (x r n) -> p x r n", x=2, n=P), ACT.Copy).then_inc(read_out[(t + 2) % 2], 1)
                act.wait_ge(read_out[slot(t + 4)], nth(t + 4) + 1)
                if positive(16 * m):
                    act.wait_ge(y_stored, val(16 * m))
                act.activation(YT[:], UD[:], ACT.Gelu_apprx_tanh).then_inc(ygelu, 1)
                act.wait_ge(yf_landed, val(16 * GT * (m + 1)))
                act.activation(YG[:, m * S2:(m + 1) * S2].rearrange("p (c i) -> p i c", i=SUB), YF[:], ACT.Copy)\
                   .then_inc(yg_ready, 1)

            act.wait_ge(trig_in, 4)
            act.wait_ge(yg_ready, DT)
            act.activation(TAB[64:P], TAB[64:P], ACT.Sin, scale=PRM[64:P, a_sgn:a_sgn + 1]).then_inc(trig_out, 1)
            for k in range(4):
                split_hi(N_LAT + 3 + k)
                src = result2(N_LAT + k, T_LAT + k)
                act.activation(LATF[:, k * S2:(k + 1) * S2], src, ACT.Copy)
                square2(Q_LAT + k, src)
            root(5, S2)
            root(6, S2)
            for k in range(4):
                act.wait_ge(xf_ready, val(3 * DT + k + 1))
                dst = (LQH, LKH)[k // LATT]
                act.activation(dst[:, k % LATT * S2:(k % LATT + 1) * S2], [CT, VT][k % 2][:, 0:S2], ACT.Copy)\
                   .then_inc(xh_ready, 1)
            split_hi(N_LAT + 7)
            act.wait_ge(rope_ready, 1)
            for x in range(2):
                act.activation(K2H[x][64:96], RO[64:96], ACT.Copy).then_inc(rope_hi, 1)
            act.wait_ge(pattern, 6)
            for x in range(2):
                act.activation(Q2H[x][96:P], PB[96:P, 0], ACT.Copy)
                act.activation(Q2L[x][96:P], PB[96:P, 0], ACT.Copy, scale=0.0)
                act.activation(K2H[x][96:P], PB[96:P, 1], ACT.Copy, scale=MASKED)
                act.activation(K2L[x][96:P], PB[96:P, 0], ACT.Copy, scale=0.0).then_inc(kr_hi, 1)

            def attend(m):
                n, t, h = N_ATT + 2 * m, T_ATT + 8 * m, 2 * m
                split_hi(n + 3)
                for x in range(2):
                    act.wait_ge(up_done, val(3 * m + x + 1))
                    if positive(8 * m):
                        act.wait_ge(s_done, val(8 * m))
                    act.activation(Q2H[x][0:64], J[(t + x) % 2][0:64, 0:S2], ACT.Copy).then_inc(q_top, 1)
                    act.wait_ge(rope_ready, val(h + x + 2))
                    act.activation(Q2H[x][64:96], RO[64:96], ACT.Copy).then_inc(rope_hi, 1)
                act.wait_ge(up_done, val(3 * m + 3))
                for x in range(2):
                    mm = act.activation(K2H[x][0:64], J[t % 2][64 * x:64 * x + 64, 0:S2], ACT.Copy)
                mm.then_inc(k_hi, 1)
                act.wait_ge(job_done, val(n + 1))
                if positive(2 * m):
                    act.wait_ge(om_ready, val(2 * m))
                act.activation(VZ[:], J[(t + 3) % 2][:, 0:S2], ACT.Copy).then_inc(read_out[(t + 3) % 2], 1)

                def exponent(u):
                    g, i = 8 * m + u, u % 4
                    act.wait_ge(nm_ready, val(g + 1))
                    if positive(g - 1):
                        act.wait_ge(pt_done, val(g - 1))
                    act.activation(PB[:, u % 2, 0:P * (i + 1)], Z[:, 512 * (u % 2):512 * (u % 2) + P * (i + 1)],
                                   ACT.Exp, scale=SCALE2, bias=NM[:, u:u + 1], accum_out=SU[:, u:u + 1])\
                       .then_inc(p_exp, 1)

                def weights_hi(u):
                    g, i = 8 * m + u, u % 4
                    act.wait_ge(pt_done, val(g + 1))
                    if i == 0:
                        if positive(h + u // 4):
                            act.wait_ge(pv2_done, val(h + u // 4))
                    act.activation(PTH[:, 0:i + 1, P * i:P * (i + 1)],
                                   PTB[u % 2][:, 0:P * (i + 1)].rearrange("p (j s) -> p j s", s=P), ACT.Copy)\
                       .then_inc(pt_hi, 1)

                exponent(0)
                exponent(1)
                act.wait_ge(v2_turned, val(m + 1))
                if positive(h):
                    act.wait_ge(pv2_done, val(h))
                act.activation(V2H[:], J[(t + 4) % 2][:, 0:S2], ACT.Copy).then_inc(v2_hi, 1)
                split_hi(n + 4)
                src = result2(n + 1, t + 5)
                act.activation(VZ[:], src, ACT.Silu).then_inc(read_out[(t + 5) % 2], 1)
                for u in range(8):
                    weights_hi(u)
                    if u + 2 < 8:
                        exponent(u + 2)
                    if u == 5:
                        out_hi(m, 0)
                out_hi(m, 1)

            def out_hi(m, x):
                r = slice(64 * x, 64 * x + 64)
                act.wait_ge(om_ready, val(2 * m + x + 1))
                act.activation(OMH[r, cols(m * S2, S2)], RO[r], ACT.Copy).then_inc(om_hi, 1)

            repeat(act, DT, 2, attend)

            for m in range(DT):
                s = slice(m * S2, (m + 1) * S2)
                act.activation(YGH[:, s], YG[:, s], ACT.Copy).then_inc(yg_hi, 1)

            def glu(m):
                n, t = N_GLU + 2 * m, T_GLU + 2 * m
                split_hi(n + 3)
                src = result2(n, t)
                if positive(2 * m):
                    act.wait_ge(glu_step, val(2 * m))
                act.activation(G2[:], src, ACT.Sigmoid, bias=PRM[:, cols(a_bglu + DT + m, 1)])\
                   .then_inc(read_out[t % 2], 1)
                split_hi(n + 4)
                act.wait_ge(glu_step, val(2 * m + 2))
                if m.base == 0 and m.reg is None:
                    act.wait_ge(yg_lo, DT)
                act.activation(YSH[:, cols(m * S2, S2)], G1[:], ACT.Copy).then_inc(ys_hi, 1)

            repeat(act, DT, 2, glu)

            def merge(m):
                n, t = N_MERGE + 4 * m, T_MERGE + 4 * m
                for j, g in enumerate((G1, G2)):
                    split_hi(n + 3 + j)
                    src = result2(n + j, t + j)
                    if m.base == 0 and m.reg is None:
                        act.wait_ge(ys_lo, DT)
                    else:
                        act.wait_ge(read_out[slot(t + j - 2)], nth(t + j - 2) + 1)
                    act.activation(g[:], src, ACT.Sigmoid).then_inc(read_out[(t + j) % 2], 1)
                split_hi(n + 5)
                split_hi(n + 6)
                act.wait_ge(m2_ready, val(m + 1))
                act.activation(M2H[:, cols(m * S2, S2)], G4[:], ACT.Copy).then_inc(m2_hi, 1)

            repeat(act, DT, 1, merge)

            for m in range(DT):
                n, t = N_OUT2 + m, T_OUT2 + m
                split_hi(n + 3)
                src = result2(n, t)
                act.activation(F3[:, m * S2:(m + 1) * S2], src, ACT.Copy)
                square2(Q_POST2 + m, src)
            root(7, S2)

        @block.vector
        def _(dve):
            def split_lo(n):
                n = as_lin(n)
                if n.base >= N_LAST:
                    return
                dve.wait_ge(w_hi, val(n + 2))
                dve.tensor_tensor(WL[:, n % SPLIT, :], WR[:, n % RAW, :], WH[:, n % SPLIT, :].bitcast(F32),
                                  ALU.subtract).then_inc(w_lo, 1)

            def low(dst, src, hi):
                return dve.tensor_tensor(dst, src, hi.bitcast(F32), ALU.subtract)

            dve.memset(PP[:, 0:2], 0.0).then_inc(zeroed, 1)
            dve.memset(VH[:, 4 * P:].bitcast(F32), 0.0)
            dve.memset(VL[:, 4 * P:].bitcast(F32), 0.0).then_inc(zeroed, 1)
            dve.wait_ge(w_hi, 1)
            low(CL[:], CR[:], CH[:]).then_inc(c_lo, 1)

            def root(e, last):
                dve.wait_ge(sq_summed, val(last))
                r = RB[:, e % 2, :]
                dve.tensor_scalar(halves(r), ZV, 1.0 / D, EPS, ALU.mult, ALU.add).then_inc(r_step, 1)
                dve.wait_ge(r_step, val(2 * e + 1))
                dve.reciprocal(r, r).then_inc(r_step, 1)
                dve.wait_ge(r_ready, val(e + 1))
                return r

            def normed(src, g, e, r, count):
                for m in range(DT):
                    xf = [CT, VT][m % 2]
                    if m >= 2:
                        dve.wait_ge(xl_ready, val(count * DT + m - 1))
                    dve.scalar_tensor_tensor(out=xf[:], in0=src[:, m * L1:(m + 1) * L1], scalar=PRM[:, g + m:g + m + 1],
                                             in1=r, op0=ALU.mult, op1=ALU.mult).then_inc(xf_ready, 1)
                    if m:
                        k = m - 1
                        dve.wait_ge(xh_ready, val(count * DT + k + 1))
                        low(XL[:, k * L1:(k + 1) * L1], [CT, VT][k % 2][:], XH[:, k * L1:(k + 1) * L1]).then_inc(xl_ready, 1)
                k = DT - 1
                dve.wait_ge(xh_ready, val(count * DT + k + 1))
                low(XL[:, k * L1:(k + 1) * L1], [CT, VT][k % 2][:], XH[:, k * L1:(k + 1) * L1]).then_inc(xl_ready, 1)

            for n in range(SPLIT - 1):
                split_lo(n)
            r = root(0, Q_PRE + DT)
            normed(X0, g_pre, 0, r, 0)

            def softplus(h):
                h = as_lin(h)
                dve.wait_ge(soft_step, val(3 * h + 3))
                dve.scalar_tensor_tensor(out=E[:], in0=Z[:, 0:SCORE], scalar=0.0, in1=E[:],
                                         op0=ALU.max, op1=ALU.add).then_inc(sp_ready, 1)

            def fail_lo(h):
                h = as_lin(h)
                dve.wait_ge(lf_hi, val(h + 1))
                low(LL[:], E[:], LH[:]).then_inc(lf_lo, 1)

            def weight_lo(h):
                h = as_lin(h)
                dve.wait_ge(a_hi, val(h + 1))
                low(AL[:], E[:], AH[:]).then_inc(a_lo, 1)

            def head_out(h, m, t):
                h, t = as_lin(h), as_lin(t)
                r = slice(64 * (h % 2), 64 * (h % 2) + 64)
                dve.wait_ge(o_hi, val(h + 1))
                low(halves(OL[r, cols(m * L1, L1)]), JV[t % 2][r], halves(OH[r, cols(m * L1, L1)]))\
                    .then_inc(read_out[t % 2], 1)

            def mix(m):
                n, t, h = N_MIX + 8 * m, T_MIX + 12 * m, 2 * m
                later = m.base or m.reg is not None
                split_lo(n + 3)
                dve.wait_ge(qk_hi, val(2 * m + 1))
                dve.scalar_tensor_tensor(out=halves(QL[:]), in0=JV[t % 2], scalar=0.125, in1=halves(QH[:]).bitcast(F32),
                                         op0=ALU.mult, op1=ALU.subtract).then_inc(read_out[t % 2], 1)
                split_lo(n + 4)
                dve.wait_ge(qk_hi, val(2 * m + 2))
                low(halves(KL[:, 0:L1]), JV[(t + 1) % 2], halves(KH[:, 0:L1])).then_inc(read_out[(t + 1) % 2], 1)
                softplus(h)
                if later:
                    head_out(h - 1, m - 1, t + 2)
                else:
                    dve.nop().then_inc(read_out[(t + 2) % 2], 1)
                split_lo(n + 5)
                fail_lo(h)
                split_lo(n + 6)
                dve.wait_ge(v_hi, val(2 * m + 1))
                low(VL[:, 0:3 * P], J[(t + 5) % 2][:, 0:3 * P], VH[:, 0:3 * P]).then_inc(read_out[(t + 5) % 2], 1)
                dve.wait_ge(v_hi, val(2 * m + 2))
                low(VL[:, 3 * P:4 * P], J[(t + 6) % 2][:, 0:P], VH[:, 3 * P:4 * P])
                low(VL[0:META, 4 * P:], J[(t + 6) % 2][0:META, P:2 * P], VH[0:META, 4 * P:])\
                    .then_inc(read_out[(t + 6) % 2], 1)
                weight_lo(h)
                split_lo(n + 7)
                dve.wait_ge(job_done, val(n + 5))
                dve.tensor_tensor(halves(PP[:, 2:]), JV[(t + 7) % 2], halves(CT[:]), ALU.mult)\
                   .then_inc(read_out[(t + 7) % 2], 1)
                dve.wait_ge(read_out[slot(t + 7)], nth(t + 7) + 1)
                if m.base or m.reg is not None:
                    dve.wait_ge(read_out[slot(t + 8 - 12)], nth(t + 8 - 12) + 1)
                taps(m, cw_mix, DT, conv_step)
                split_lo(n + 8)
                softplus(h + 1)
                dve.wait_ge(job_done, val(n + 6))
                dve.tensor_tensor(halves(CT[:]), JV[(t + 8) % 2], halves(CV[:]), ALU.mult)\
                   .then_inc(read_out[(t + 8) % 2], 1)
                dve.wait_ge(y_hi, val(m + 1))
                low(YL[:, cols(m * L1, L1)], CT[:], YH[:, cols(m * L1, L1)]).then_inc(y_lo, 1)
                head_out(h, m, t + 9)
                fail_lo(h + 1)
                for j in range(2):
                    split_lo(n + 9 + j)
                    dve.wait_ge(job_done, val(n + 7 + j))
                    dve.tensor_copy(MOD[:, cols(2 * m + j, 1)], J[(t + 10 + j) % 2][:, 0:1])\
                       .then_inc(read_out[(t + 10 + j) % 2], 1)
                weight_lo(h + 1)

            def taps(m, w, tiles, step):
                for k in range(3):
                    tap = PRM[:, cols(w + (2 - k) * tiles + m, 1)]
                    src = PP[:, 2 - k:2 - k + L1]
                    if k == 0:
                        dve.tensor_scalar(CV[:], src, tap, None, ALU.mult).then_inc(step, 1)
                    else:
                        dve.scalar_tensor_tensor(out=CV[:], in0=src, scalar=tap, in1=CV[:],
                                                 op0=ALU.mult, op1=ALU.add).then_inc(step, 1)
                    dve.wait_ge(step, val(3 * m + k + 1))

            repeat(dve, DT, 1, mix)
            head_out(HEADS - 1, DT - 1, T_MIX + 12 * DT)

            def gates(m):
                n, t = N_GATE + 4 * m, T_GATE + 4 * m
                split_lo(n + 3)
                split_lo(n + 4)
                split_lo(n + 5)
                dve.wait_ge(job_done, val(n + 3))
                dve.wait_ge(read_out[slot(t)], nth(t) + 1)
                if positive(m):
                    dve.wait_ge(mf_ready, val(m))
                dve.tensor_tensor(halves(VT[:]), JV[(t + 2) % 2], halves(CT[:]), ALU.mult)\
                   .then_inc(read_out[(t + 2) % 2], 1)
                split_lo(n + 6)
                dve.wait_ge(job_done, val(n + 4))
                dve.wait_ge(read_out[slot(t + 1)], nth(t + 1) + 1)
                if positive(m):
                    dve.wait_ge(m_lo, val(m))
                dve.tensor_tensor(halves(PP[:, 2:]), JV[(t + 3) % 2], halves(CV[:]), ALU.mult)\
                   .then_inc(read_out[(t + 3) % 2], 1)
                dve.wait_ge(read_out[slot(t + 3)], nth(t + 3) + 1)
                dve.tensor_tensor(PP[:, 2:], PP[:, 2:], VT[:], ALU.add).then_inc(mf_ready, 1)
                dve.wait_ge(m_hi, val(m + 1))
                low(ML[:, cols(m * L1, L1)], PP[:, 2:], MH[:, cols(m * L1, L1)]).then_inc(m_lo, 1)

            repeat(dve, DT, 1, gates)

            for m in range(DT):
                n, t = N_OUT + 2 * m, T_OUT + 2 * m
                split_lo(n + 3)
                split_lo(n + 4)
                dve.wait_ge(sq_done, val(Q_MIX + m + 1))
                dve.nop().then_inc(read_out[t % 2], 1)
                dve.wait_ge(job_done, val(n + 2))
                dve.tensor_copy(MOD[:, 2 * DT + m:2 * DT + m + 1], J[(t + 1) % 2][:, 0:1])\
                   .then_inc(read_out[(t + 1) % 2], 1)

            def add_normed(f, g, r, count):
                for m in range(DT):
                    s = slice(m * L1, (m + 1) * L1)
                    tmp = [CT, VT][m % 2]
                    if m >= 2:
                        dve.wait_ge(h_ready, val(count * DT + m - 1))
                    dve.scalar_tensor_tensor(out=tmp[:], in0=f[:, s], scalar=PRM[:, g + m:g + m + 1], in1=r,
                                             op0=ALU.mult, op1=ALU.mult).then_inc(t_ready, 1)
                    dve.wait_ge(t_ready, val(count * DT + m + 1))
                    dve.tensor_tensor(H[:, s], H[:, s], tmp[:], ALU.add).then_inc(h_ready, 1)

            r = root(1, Q_MIX + DT)
            dve.wait_ge(h_landed, 16)
            add_normed(F, g_mix, r, 0)
            r = root(2, Q_PREF + DT)
            dve.wait_ge(h_ready, DT)
            normed(H, g_pref, 2, r, 1)

            def up(i):
                n, t = N_UP + 2 * i, T_UP + 2 * i
                split_lo(n + 3)
                dve.wait_ge(read_out[slot(t)], nth(t) + 1)
                if positive(i):
                    dve.wait_ge(gelu_done, val(i))
                taps(i, cw_ffn, FT, fconv_step)
                split_lo(n + 4)
                dve.wait_ge(job_done, val(n + 2))
                dve.wait_ge(gelu_done, val(i + 1))
                if positive(i):
                    dve.wait_ge(f_lo, val(i))
                dve.tensor_tensor(halves(CT[:]), JV[(t + 1) % 2], halves(VT[:]), ALU.mult)\
                   .then_inc(read_out[(t + 1) % 2], 1)
                dve.wait_ge(f_hi, val(i + 1))
                low(FL[:, cols(i * L1, L1)], CT[:], FH[:, cols(i * L1, L1)]).then_inc(f_lo, 1)

            repeat(dve, FT, 2, up)

            n = N_DOWN + SPLIT - 1
            for m in range(DT):
                while n < down_slots_after(m):
                    split_lo(n)
                    n += 1
                dve.wait_ge(sq_done, val(Q_FFN + m + 1))
                dve.nop().then_inc(read_out[(T_DOWN + m) % 2], 1)
            r = root(3, Q_FFN + DT)
            add_normed(F2, g_ffn, r, 1)

            steps = [0]

            def link(ins):
                steps[0] += 1
                ins.then_inc(setup, 1)
                dve.wait_ge(setup, steps[0])

            def mul(o, x, y):
                link(dve.tensor_tensor(o, x, y, ALU.mult))

            def add(o, x, y, op=ALU.add):
                link(dve.tensor_tensor(o, x, y, op))

            def cmul(o_r, o_i, a_r, a_i, b_r, b_i, t1, t2):
                mul(t1, a_r, b_r)
                mul(t2, a_i, b_i)
                add(o_r, t1, t2, ALU.subtract)
                mul(t1, a_r, b_i)
                mul(t2, a_i, b_r)
                add(o_i, t1, t2)

            def reduce_angle(x, n):
                link(dve.tensor_scalar(n, x, float(1 / (2 * np.pi)), MAGIC, ALU.mult, ALU.add))
                link(dve.tensor_scalar(n, n, MAGIC, None, ALU.subtract))
                for part in (TURN1, TURN2, TURN3):
                    link(dve.scalar_tensor_tensor(out=x, in0=n, scalar=-part, in1=x, op0=ALU.mult, op1=ALU.add))
                link(dve.tensor_scalar(x, x, PI_BELOW, -PI_BELOW, ALU.min, ALU.max))

            dve.wait_ge(job_done, N_U)
            link(dve.tensor_tensor(MB[:], MOD[:], PRM[:, a_bada:a_bada + 24], ALU.add))
            link(dve.scalar_tensor_tensor(out=GG[:, 0:8], in0=MB[:, 8:16], scalar=1.0, in1=PRM[:, a_gpre2:a_gpre2 + 8],
                                          op0=ALU.add, op1=ALU.mult))
            link(dve.tensor_tensor(GG[:, 8:16], MB[:, 16:24], PRM[:, a_gpost2:a_gpost2 + 8], ALU.mult))

            def root2(e, last, count):
                dve.wait_ge(sq_summed, val(last))
                r = RB[:, e % 2, 0:S2]
                dve.tensor_scalar(r, Z[:, 0:S2], 1.0 / count, EPS, ALU.mult, ALU.add).then_inc(r_step, 1)
                dve.wait_ge(r_step, val(2 * e + 1))
                dve.reciprocal(r, r).then_inc(r_step, 1)
                dve.wait_ge(r_ready, val(e + 1))
                return r

            dve.wait_ge(h_ready, 2 * DT)
            r = root2(4, Q_PRE2 + DT, D)

            def low2(m):
                dve.wait_ge(xh_ready, val(2 * DT + m + 1))
                s = slice(m * S2, (m + 1) * S2)
                dve.scalar_tensor_tensor(out=X2L[:, s], in0=[CT, VT][m % 2][:, 0:S2], scalar=MB[:, m:m + 1],
                                         in1=X2H[:, s].bitcast(F32), op0=ALU.add, op1=ALU.subtract).then_inc(xl_ready, 1)

            for m in range(DT):
                if m >= 2:
                    dve.wait_ge(xl_ready, val(2 * DT + m - 1))
                dve.scalar_tensor_tensor(out=[CT, VT][m % 2][:, 0:S2], in0=H[:, m * L1 + META:(m + 1) * L1],
                                         scalar=GG[:, m:m + 1], in1=r, op0=ALU.mult, op1=ALU.mult).then_inc(xf_ready, 1)
                if m:
                    low2(m - 1)
            low2(DT - 1)

            split_lo(N_U + 3)
            are, aim = PRM[:, a_are:a_are + PAIRS], PRM[:, a_aim:a_aim + PAIRS]
            dt_, lrdt, th, nn, mag, sn, sh, cs = SM[0][:], SM[1][:], SM[2][:], SM[3][:], SM[5][:], SM[6][:], SM[7][:], SM[8][:]
            dve.nop().then_inc(trig_in, 1)
            dve.wait_ge(trig_out, 1)
            mul(th, aim, dt_)
            reduce_angle(th, nn)
            mul(lrdt, are, dt_)
            dve.nop().then_inc(trig_in, 1)
            split_lo(N_U + 4)
            dve.nop().then_inc(trig_in, 1)

            for m in range(DT):
                if m >= 2:
                    split_lo(N_U + 3 + m)
                dve.wait_ge(ut_copied, val(m + 1))
                dve.nop().then_inc(read_out[(T_U + m) % 2], 1)
                if m == 2:
                    dve.wait_ge(trig_out, 4)
                    mul(cs, sh, sh)
                    link(dve.tensor_scalar(cs, cs, -2.0, 1.0, ALU.mult, ALU.add))
                    ar, ai = SM[9][:], SM[10][:]
                    mul(ar, mag, cs)
                    mul(ai, mag, sn)
                    den, t1, t2, nr, fr, fi = (SM[k][:] for k in range(11, 17))
                    mul(t1, are, are)
                    mul(t2, aim, aim)
                    add(den, t1, t2)
                    link(dve.reciprocal(den, den))
                    link(dve.tensor_scalar(nr, ar, 1.0, None, ALU.subtract))
                    mul(t1, nr, are)
                    mul(t2, ai, aim)
                    add(fr, t1, t2)
                    mul(fr, fr, den)
                    mul(t1, ai, are)
                    mul(t2, nr, aim)
                    add(fi, t1, t2, ALU.subtract)
                    mul(fi, fi, den)
                if m == 3:
                    dve.wait_ge(mat_landed, 32)
                    wide = [P, PAIRS, GP]
                    frb, fib = fr.unsqueeze(2).to_broadcast(wide), fi.unsqueeze(2).to_broadcast(wide)
                    cmul(BBR[:], BBI[:], frb, fib, BM[:, 0], BM[:, 1], C1[:], C2[:])
                    link(dve.tensor_scalar(NBBI[:], BBI[:], -1.0, None, ALU.mult))
                    link(dve.tensor_scalar(NCI[:], CM[:, 1], -1.0, None, ALU.mult))
                if m == 4:
                    link(dve.memset(PWR[:, :, 0:1], 1.0))
                    link(dve.memset(PWI[:, :, 0:1], 0.0))
                    link(dve.tensor_copy(PWR[:, :, 1], ar))
                    link(dve.tensor_copy(PWI[:, :, 1], ai))
                    for k in (1, 2, 4):
                        w = [P, PAIRS, k]
                        t1_, t2_ = (TS[:, x, 0:PAIRS * k].rearrange("p (a b) -> p a b", b=k) for x in range(2))
                        cmul(PWR[:, :, k + 1:2 * k + 1], PWI[:, :, k + 1:2 * k + 1],
                             PWR[:, :, k:k + 1].to_broadcast(w), PWI[:, :, k:k + 1].to_broadcast(w),
                             PWR[:, :, 1:k + 1], PWI[:, :, 1:k + 1], t1_, t2_)
                    for j in range(SUB):
                        dve.tensor_copy(RVR[:, :, j], PWR[:, :, SUB - 1 - j])
                        ins = dve.tensor_copy(RVI[:, :, j], PWI[:, :, SUB - 1 - j])
                    ins.then_inc(pow_ready, 1)
                if m == 5:
                    ur, ui, m8 = SM[17][:], SM[18][:], SM[21][:]
                    link(dve.tensor_copy(ur, cs))
                    link(dve.tensor_copy(ui, sn))
                    link(dve.tensor_copy(m8, mag))
                    p1, p2 = SM[19][:], SM[20][:]

                    def square_turn():
                        t3, t4 = SM[22][:], SM[23][:]
                        cmul(p1, p2, ur, ui, ur, ui, t3, t4)
                        link(dve.tensor_copy(ur, p1))
                        link(dve.tensor_copy(ui, p2))

                    for _ in range(3):
                        square_turn()
                        mul(m8, m8, m8)

                    def table(tr, ti):
                        link(dve.memset(tr[:, :, 0:1], 1.0))
                        link(dve.memset(ti[:, :, 0:1], 0.0))
                        for k in (1, 2, 4):
                            w = [P, PAIRS, k]
                            t1_, t2_ = (TS[:, x, 0:PAIRS * k].rearrange("p (a b) -> p a b", b=k) for x in range(2))
                            cmul(tr[:, :, k:2 * k], ti[:, :, k:2 * k],
                                 ur.unsqueeze(2).to_broadcast(w), ui.unsqueeze(2).to_broadcast(w),
                                 tr[:, :, 0:k], ti[:, :, 0:k], t1_, t2_)
                            square_turn()

                    table(WBR, WBI)
                if m == 6:
                    table(WAR_, WAI)
                    link(dve.memset(SR[:, :, 0:1], 0.0))
                    link(dve.memset(SI[:, :, 0:1], 0.0))
                    dve.memset(TK[:], 0.0).then_inc(tk_zeroed, 1)

            for m in range(DT):
                t = T_SSM + 5 * m
                split_lo(N_SSM + m + 3)
                ps = slice(PT_ * m, PT_ * (m + 1))
                w4 = [P, PT_, 8, 8]
                cmul(WC[:], WS[:], WAR_[:, ps].unsqueeze(3).to_broadcast(w4), WAI[:, ps].unsqueeze(3).to_broadcast(w4),
                     WBR[:, ps].unsqueeze(2).to_broadcast(w4), WBI[:, ps].unsqueeze(2).to_broadcast(w4),
                     VR[:].rearrange("p a (b c) -> p a b c", b=8), VI[:].rearrange("p a (b c) -> p a b c", b=8))
                link(dve.tensor_copy(MT[:], SM[21][:, ps].unsqueeze(2).to_broadcast([P, PT_, NC])))
                link(dve.memset(MT[:, :, 0:1], 0.0))
                wc, ws = (x[:].rearrange("p a b c -> p a (b c)") for x in (WC, WS))
                dve.wait_ge(b_done, val(m + 1))
                br, bi = (J[(t + 3) % 2][:, 512 * x:512 * x + PT_ * NC].rearrange("p (a c) -> p a c", a=PT_) for x in range(2))
                mul(V1[:], br, wc)
                mul(V2[:], bi, ws)
                add(VR[:], V1[:], V2[:])
                mul(V1[:], bi, wc)
                mul(V2[:], br, ws)
                dve.nop().then_inc(read_out[(t + 3) % 2], 1)
                add(VI[:], V1[:], V2[:], ALU.subtract)
                flat = [x[:].rearrange("p a c -> p (a c)") for x in (MT, VR, VI, V1, V2)]
                link(dve.tensor_tensor_scan(flat[3], flat[0], flat[1], 0.0, ALU.mult, ALU.add))
                link(dve.tensor_tensor_scan(flat[4], flat[0], flat[2], 0.0, ALU.mult, ALU.add))
                if positive(m):
                    dve.wait_ge(y_done, val(m))
                mul(VR[:], V1[:], wc)
                mul(VI[:], V2[:], ws)
                add(SR[:, :, 1:], VR[:], VI[:], ALU.subtract)
                mul(VR[:], V1[:], ws)
                mul(VI[:], V2[:], wc)
                dve.tensor_tensor(SI[:, :, 1:], VR[:], VI[:], ALU.add).then_inc(s_ready, 1)
                dve.wait_ge(s_ready, m + 1)
                dve.wait_ge(y_done, val(m + 1))
                dve.wait_ge(ud_ready, val(m + 1))
                ud = UD[:].rearrange("p (r x) c -> p x r c", x=2)
                ys = J[(t + 4) % 2][:].rearrange("p (x r c) -> p x r c", x=2, c=NC)[:, :, 0:PT_]
                dve.tensor_tensor(ud, ys, ud, ALU.add).then_inc(read_out[(t + 4) % 2], 1)

            dve.wait_ge(pos_landed, 16)
            link(dve.tensor_copy(TAB[64:P], POSI[64:P]))
            link(dve.tensor_scalar(TAB[64:P], TAB[64:P], PRM[64:P, a_inv:a_inv + 1], None, ALU.mult))
            reduce_angle(TAB[64:P], R2[64:P])
            dve.nop().then_inc(trig_in, 1)
            for k in range(4):
                split_lo(N_LAT + 3 + k)
                dve.wait_ge(sq_done, val(Q_LAT + k + 1))
                dve.nop().then_inc(read_out[(T_LAT + k) % 2], 1)
                if k == 2:
                    r5 = root2(5, Q_LAT + LATT, 256)
            dve.wait_ge(trig_out, 5)
            mul(R2[64:96], TAB[64:96], TAB[64:96])
            link(dve.tensor_scalar(TAB[64:96], R2[64:96], -2.0, 1.0, ALU.mult, ALU.add))
            r6 = root2(6, Q_KV + LATT, 256)

            def low_lat(k):
                dve.wait_ge(xh_ready, val(3 * DT + k + 1))
                s = slice(k % LATT * S2, (k % LATT + 1) * S2)
                low((LQL, LKL)[k // LATT][:, s], [CT, VT][k % 2][:, 0:S2], (LQH, LKH)[k // LATT][:, s]).then_inc(xl_ready, 1)

            for k in range(2 * LATT):
                if k >= 2:
                    dve.wait_ge(xl_ready, val(3 * DT + k - 1))
                dve.scalar_tensor_tensor(out=[CT, VT][k % 2][:, 0:S2], in0=LATF[:, k * S2:(k + 1) * S2],
                                         scalar=PRM[:, a_glat + k:a_glat + k + 1], in1=(r5, r6)[k // LATT],
                                         op0=ALU.mult, op1=ALU.mult).then_inc(xf_ready, 1)
                if k:
                    low_lat(k - 1)
            low_lat(2 * LATT - 1)

            def rope(src):
                link(dve.tensor_tensor(RO[64:96], src[96:P], TAB[96:P], ALU.mult))
                link(dve.tensor_tensor(R2[64:96], src[64:96], TAB[64:96], ALU.mult))

            split_lo(N_LAT + 7)
            dve.wait_ge(job_done, N_LAT + 5)
            rope(J[(T_LAT + 4) % 2][:, 0:S2])
            dve.nop().then_inc(read_out[(T_LAT + 4) % 2], 1)
            dve.tensor_tensor(RO[64:96], RO[64:96], R2[64:96], ALU.add).then_inc(rope_ready, 1)
            dve.wait_ge(rope_hi, 2)
            for x in range(2):
                ins = low(K2L[x][64:96], RO[64:96], K2H[x][64:96])
            ins.then_inc(kr_ready, 1)
            dve.wait_ge(kr_ready, 1)
            dve.wait_ge(kr_hi, 2)

            def attend(m):
                n, t, h = N_ATT + 2 * m, T_ATT + 8 * m, 2 * m
                split_lo(n + 3)
                for x in range(2):
                    src = J[(t + x) % 2][:, 0:S2]
                    dve.wait_ge(up_done, val(3 * m + x + 1))
                    if positive(h):
                        dve.wait_ge(om_lo, val(h))
                    if positive(h + x):
                        dve.wait_ge(q_ready, val(h + x))
                    dve.tensor_tensor(RO[64:96], src[96:P], TAB[96:P], ALU.mult)
                    dve.tensor_tensor(R2[64:96], src[64:96], TAB[64:96], ALU.mult).then_inc(roped, 1)
                    dve.wait_ge(q_top, val(h + x + 1))
                    low(Q2L[x][0:64], src[0:64], Q2H[x][0:64]).then_inc(read_out[(t + x) % 2], 1)
                    dve.wait_ge(roped, val(h + x + 1))
                    dve.tensor_tensor(RO[64:96], RO[64:96], R2[64:96], ALU.add).then_inc(rope_ready, 1)
                    dve.wait_ge(rope_hi, val(h + x + 3))
                    low(Q2L[x][64:96], RO[64:96], Q2H[x][64:96]).then_inc(q_ready, 1)
                dve.wait_ge(k_hi, val(m + 1))
                for x in range(2):
                    ins = low(K2L[x][0:64], J[t % 2][64 * x:64 * x + 64, 0:S2], K2H[x][0:64])
                ins.then_inc(read_out[t % 2], 1)

                def peak(u):
                    g, i = 8 * m + u, u % 4
                    dve.wait_ge(s_done, val(g + 1))
                    dve.reduce_max(MX[:, u:u + 1], Z[:, 512 * (u % 2):512 * (u % 2) + P * (i + 1)], AX.X)\
                       .then_inc(mx_ready, 1)
                    dve.wait_ge(mx_ready, val(g + 1))
                    dve.tensor_scalar(NM[:, u:u + 1], MX[:, u:u + 1], -SCALE2, None, ALU.mult).then_inc(nm_ready, 1)

                def normalise(u):
                    g, i = 8 * m + u, u % 4
                    dve.wait_ge(p_exp, val(g + 1))
                    dve.reciprocal(RC[:, u:u + 1], SU[:, u:u + 1]).then_inc(rc_ready, 1)
                    dve.wait_ge(rc_ready, val(g + 1))
                    p = PB[:, u % 2, 0:P * (i + 1)]
                    dve.tensor_scalar(p, p, RC[:, u:u + 1], None, ALU.mult).then_inc(pn_ready, 1)

                def weights_lo(u):
                    g, i = 8 * m + u, u % 4
                    dve.wait_ge(pt_hi, val(g + 1))
                    low(PTL[:, 0:i + 1, P * i:P * (i + 1)],
                        PTB[u % 2][:, 0:P * (i + 1)].rearrange("p (j s) -> p j s", s=P),
                        PTH[:, 0:i + 1, P * i:P * (i + 1)]).then_inc(pt_lo, 1)

                def out_lo(x):
                    r = slice(64 * x, 64 * x + 64)
                    dve.wait_ge(pv2_done, val(h + x + 1))
                    if positive(h + x):
                        dve.wait_ge(om_lo, val(h + x))
                    dve.wait_ge(read_out[slot(t + 5)], nth(t + 5) + 1)
                    dve.tensor_tensor(RO[r], J[(t + 6 + x) % 2][r, 0:S2], VZ[r], ALU.mult).then_inc(om_ready, 1)
                    dve.wait_ge(om_ready, val(h + x + 1))
                    dve.nop().then_inc(read_out[(t + 6 + x) % 2], 1)
                    dve.wait_ge(om_hi, val(h + x + 1))
                    low(OML[r, cols(m * S2, S2)], RO[r], OMH[r, cols(m * S2, S2)]).then_inc(om_lo, 1)

                peak(0)
                normalise(0)
                peak(1)
                normalise(1)
                dve.wait_ge(v2_hi, val(m + 1))
                low(V2L[:], J[(t + 4) % 2][:, 0:S2], V2H[:]).then_inc(read_out[(t + 4) % 2], 1)
                split_lo(n + 4)
                for u in range(8):
                    weights_lo(u)
                    if u + 2 < 8:
                        peak(u + 2)
                        normalise(u + 2)
                    if u == 5:
                        out_lo(0)
                out_lo(1)

            repeat(dve, DT, 2, attend)

            for m in range(DT):
                s = slice(m * S2, (m + 1) * S2)
                dve.wait_ge(yg_hi, val(m + 1))
                low(YGL[:, s], YG[:, s], YGH[:, s]).then_inc(yg_lo, 1)

            def glu(m):
                n, t = N_GLU + 2 * m, T_GLU + 2 * m
                split_lo(n + 3)
                split_lo(n + 4)
                dve.wait_ge(job_done, val(n + 2))
                dve.wait_ge(read_out[slot(t)], nth(t) + 1)
                if positive(m):
                    dve.wait_ge(ys_lo, val(m))
                dve.scalar_tensor_tensor(out=G1[:], in0=J[(t + 1) % 2][:, 0:S2], scalar=PRM[:, cols(a_bglu + m, 1)],
                                         in1=G2[:], op0=ALU.add, op1=ALU.mult).then_inc(glu_step, 1)
                dve.wait_ge(glu_step, val(2 * m + 1))
                dve.nop().then_inc(read_out[(t + 1) % 2], 1)
                dve.tensor_tensor(G1[:], G1[:], SZS[:, cols(m * S2, S2)], ALU.mult).then_inc(glu_step, 1)
                dve.wait_ge(ys_hi, val(m + 1))
                low(YSL[:, cols(m * S2, S2)], G1[:], YSH[:, cols(m * S2, S2)]).then_inc(ys_lo, 1)

            repeat(dve, DT, 2, glu)

            def merge(m):
                n, t = N_MERGE + 4 * m, T_MERGE + 4 * m
                split_lo(n + 3)
                split_lo(n + 4)
                split_lo(n + 5)
                dve.wait_ge(job_done, val(n + 3))
                dve.wait_ge(read_out[slot(t)], nth(t) + 1)
                if positive(m):
                    dve.wait_ge(m2_ready, val(m))
                dve.tensor_tensor(G3[:], J[(t + 2) % 2][:, 0:S2], G1[:], ALU.mult).then_inc(read_out[(t + 2) % 2], 1)
                split_lo(n + 6)
                dve.wait_ge(job_done, val(n + 4))
                dve.wait_ge(read_out[slot(t + 1)], nth(t + 1) + 1)
                if positive(m):
                    dve.wait_ge(m2_lo, val(m))
                dve.tensor_tensor(G4[:], J[(t + 3) % 2][:, 0:S2], G2[:], ALU.mult).then_inc(read_out[(t + 3) % 2], 1)
                dve.wait_ge(read_out[slot(t + 3)], nth(t + 3) + 1)
                dve.tensor_tensor(G4[:], G4[:], G3[:], ALU.add).then_inc(m2_ready, 1)
                dve.wait_ge(m2_hi, val(m + 1))
                low(M2L[:, cols(m * S2, S2)], G4[:], M2H[:, cols(m * S2, S2)]).then_inc(m2_lo, 1)

            repeat(dve, DT, 1, merge)

            for m in range(DT):
                split_lo(N_OUT2 + m + 3)
                dve.wait_ge(sq_done, val(Q_POST2 + m + 1))
                dve.nop().then_inc(read_out[(T_OUT2 + m) % 2], 1)
            r = root2(7, Q_POST2 + DT, D)
            dve.wait_ge(res_landed, 16)
            for m in range(DT):
                s = slice(m * S2, (m + 1) * S2)
                link(dve.scalar_tensor_tensor(out=F3[:, s], in0=F3[:, s], scalar=GG[:, 8 + m:9 + m], in1=r,
                                              op0=ALU.mult, op1=ALU.mult))
                dve.tensor_tensor(F3[:, s], F3[:, s], RES[:, s], ALU.add).then_inc(fin, 1)

        @block.gpsimd
        def _(pool):
            pool.memset(STAGE[:], 1.0).then_inc(zeroed_pool, 1)
            pool.memset(IDENT[:], 1.0).then_inc(zeroed_pool, 1)
            pool.wait_ge(zeroed_pool, 2)
            pool.memset(ONES[:], 1.0).then_inc(consts, 1)
            pool.affine_select(out=STAGE[:, 0, :], in_=STAGE[:, 0, :], compare_op=ALU.is_ge, fill=0.0,
                               base=0, pattern=[[-1, P]], channel_multiplier=1).then_inc(consts, 1)
            pool.affine_select(out=IDENT[:], in_=IDENT[:], compare_op=ALU.is_equal, fill=0.0,
                               base=0, pattern=[[-1, P]], channel_multiplier=1).then_inc(consts, 1)

            def mask(done):
                d = E[:, 0:4 * P].rearrange("p (b t) -> p b t", b=4)
                pool.affine_select(out=d, in_=d, compare_op=ALU.is_gt, fill=0.0, base=0,
                                   pattern=[[0, 4], [1, P]], channel_multiplier=-1).then_inc(done, 1)
                d = E[:, 4 * P:4 * P + META]
                pool.affine_select(out=d, in_=d, compare_op=ALU.is_gt, fill=0.0, base=0,
                                   pattern=[[1, META]], channel_multiplier=-1).then_inc(done, 1)

            def mix(m):
                for h in (2 * m, 2 * m + 1):
                    pool.wait_ge(sp_ready, val(h + 1))
                    mask(lf_masked)
                    pool.wait_ge(a_exp, val(h + 1))
                    mask(a_masked)

            for m in range(DT):
                mix(m)

            steps = [0]

            def link(ins):
                steps[0] += 1
                ins.then_inc(pool_step, 1)
                pool.wait_ge(pool_step, steps[0])

            def tt(o, x, y, op=ALU.mult):
                return pool.tensor_tensor(o, x, y, op)

            pool.wait_ge(pow_ready, 1)
            for m in range(DT):
                ps = slice(PT_ * m, PT_ * (m + 1))
                w = [P, PT_, SUB, GP]
                rr, ri = (x[:, ps].unsqueeze(3).to_broadcast(w) for x in (RVR, RVI))
                bbr, bbi = (x[:, ps].unsqueeze(2).to_broadcast(w) for x in (BBR, BBI))
                k1, k2 = (x[:, :, 0:SUB] for x in (K1, K2))
                if positive(m):
                    pool.wait_ge(bt_turned, val(m))
                link(tt(k1, bbr, rr))
                link(tt(k2, bbi, ri))
                link(tt(BPR[:], k1, k2, ALU.subtract))
                link(tt(k1, bbr, ri))
                link(tt(k2, bbi, rr))
                tt(BPI[:], k1, k2, ALU.add).then_inc(bp_ready, 1)
                pool.wait_ge(bp_ready, m + 1)
                w = [P, PT_, SUB + 1, GP]
                pr, pi = (x[:, ps].unsqueeze(3).to_broadcast(w) for x in (PWR, PWI))
                cr, nci = CM[:, 0, ps].unsqueeze(2).to_broadcast(w), NCI[:, ps].unsqueeze(2).to_broadcast(w)
                if positive(m):
                    pool.wait_ge(y_done, val(m))
                link(tt(K1[:], cr, pr))
                link(tt(K2[:], nci, pi))
                link(tt(CPR[:], K1[:], K2[:], ALU.add))
                link(tt(K1[:], nci, pr))
                link(tt(K2[:], cr, pi))
                tt(CPI[:], K1[:], K2[:], ALU.subtract).then_inc(cp_ready, 1)
                pool.wait_ge(cp_ready, m + 1)
                pool.wait_ge(us_landed[m // 4], 16 * SUB)
                if positive(m):
                    pool.wait_ge(ygelu, val(m))
                g = slice(GT * m, GT * (m + 1))
                tt(UD[:], US[:, g], PRM[:, a_d + GT * m:a_d + GT * (m + 1)].unsqueeze(2).to_broadcast([P, GT, NC]))\
                    .then_inc(ud_ready, 1)

            pool.wait_ge(xl_ready, 3 * DT + 2 * LATT)
            pool.memset(PB[:], 0.0).then_inc(pattern, 1)
            pool.wait_ge(pattern, 1)
            for x in range(2):
                v = PB[:, x].rearrange("p (i h t) -> p i h t", i=4, h=2)[:, :, x]
                pool.memset(v, 1.0).then_inc(pattern, 1)
                pool.wait_ge(pattern, 2 + 2 * x)
                pool.affine_select(out=v, in_=v, compare_op=ALU.is_equal, fill=0.0, base=96,
                                   pattern=[[1, 4], [0, 64]], channel_multiplier=-1).then_inc(pattern, 1)
                pool.wait_ge(pattern, 3 + 2 * x)
            pool.nop().then_inc(pattern, 1)


PARAM = {}


def tiles(v):
    v = np.asarray(v)
    return np.ascontiguousarray(v.reshape(-1, P).T)


def blocks(w, columns=None):
    w = np.asarray(w)
    k, m = w.shape
    return w.reshape(k // P, P, m // P, P).transpose(2, 0, 1, 3)


def jobs(b):
    b = b.reshape(-1, 8, P, P)
    return b.transpose(0, 2, 1, 3).reshape(-1, P, 8 * P)


def interleave(*ws):
    return np.concatenate([w[:, None] for w in ws], axis=1)


INV_FREQ = np.tile(np.power(np.float32(10000.0), -np.arange(0, ROPE, 2, dtype=np.float32) / np.float32(ROPE)), 8)
SIGN = np.concatenate([np.full(96, 0.5), np.full(16, -1.0), np.full(16, 1.0)]).astype(np.float32)


def kernel(**inputs):
    import concourse.bacc as bacc
    from concourse.bass_utils import run_bass_kernel_spmd

    a = {k: np.asarray(v) for k, v in inputs.items()}
    w_in = blocks(a["w_in"][0]).reshape(8, DT, DT, P, P)
    b_c, c_c, h_c, q, k, v, g_conv, g_attn = w_in
    ada = blocks(a["w_ada_2"][0])
    stream = [
        interleave(q, k, v, c_c, h_c, b_c, ada[0:16:2], ada[1:16:2]),
        interleave(g_conv, g_attn, blocks(a["w_proj_conv"][0]), blocks(a["w_proj_attn"][0])),
        interleave(blocks(a["w_out"][0]), ada[16:]),
        blocks(a["w_up_gate"][0]).reshape(2, FT, DT, P, P).transpose(1, 0, 2, 3, 4),
        blocks(a["w_down"][0]),
    ]
    w2 = a["w_in_2"][0]
    u_s, z_s, q_lat, kv_lat, k_rope, z_m, gl_s, gl_m = np.split(
        w2, np.cumsum([1024, 1024, 256, 256, 32, 1024, 1024])[:8], axis=1)

    def swapped(w):
        return np.concatenate([w[..., 16:], w[..., :16]], axis=-1)

    kr = np.concatenate([k_rope, swapped(k_rope)] * 2, axis=1)
    wq = a["w_q_up_2"][0].reshape(256, HEADS, 96)
    wq = np.concatenate([wq, swapped(wq[..., 64:])], axis=-1).reshape(256, HEADS * P)
    wkv = a["w_kv_up_2"][0].reshape(256, HEADS, 128)
    wk = wkv[..., :64].reshape(256, 1024)
    wv = wkv[..., 64:].reshape(256, 1024)
    bq = blocks(wq).reshape(8, 2, 2, P, P)
    up = np.concatenate([bq[:, 0], bq[:, 1], blocks(wk), blocks(wv)], axis=1)
    glu = blocks(a["w_glu_2"][0])
    stream += [
        blocks(u_s), blocks(z_s), blocks(q_lat), blocks(kv_lat), blocks(kr),
        interleave(up, blocks(z_m)),
        interleave(glu[8:], glu[:8]),
        interleave(blocks(gl_s), blocks(gl_m), blocks(a["w_br_ssm_2"][0]), blocks(a["w_br_mla_2"][0])),
        blocks(a["w_out_2"][0]),
    ]
    weights = np.concatenate([jobs(s) for s in stream])
    assert weights.shape[0] == N_LAST
    vectors = [
        ("g_pre_mix", a["g_pre_mix"]), ("g_post_mix", a["g_post_mix"]), ("g_pre_ffn", a["g_pre_ffn"]),
        ("g_post_ffn", a["g_post_ffn"]), ("b_gate", a["b_gate"]), ("conv_w_mix", a["conv_w_mix"]),
        ("conv_w_ffn", a["conv_w_ffn"]),
        ("b_ada", a["b_ada_2"]), ("g_pre_2", a["g_pre_2"]), ("g_post_2", a["g_post_2"]),
        ("g_lat", np.concatenate([a["g_q_norm_2"], a["g_kv_norm_2"]])), ("b_glu", a["b_glu_2"]),
        ("a_re", a["ssm_a_re_2"]), ("a_im", a["ssm_a_im_2"]), ("log_dt", np.repeat(a["ssm_log_dt_2"], NS)),
        ("ssm_d", np.tile(a["ssm_d_2"].reshape(GROUPS, GP), (1, SUB))),
        ("inv_freq", INV_FREQ), ("sign", SIGN),
    ]
    params, at = [], 0
    for name, vec in vectors:
        params.append(tiles(vec))
        PARAM[name] = at
        at += params[-1].shape[1]
    params = np.concatenate(params, axis=1)
    cond = np.repeat(tiles(a["c_2"]), 2, axis=1)
    tokens = np.ascontiguousarray(np.concatenate([a["meta_tokens"], a["x"][0]]).T)

    nc = bacc.Bacc("TRN2", target_bir_lowering=False, num_devices=1)
    def states(x):
        return x.reshape(PAIRS, P, GP).transpose(1, 0, 2)

    bmat = np.stack([states(a["ssm_b_re_2"][0]), states(a["ssm_b_im_2"][0])], axis=1)
    cmat = np.stack([states(a["ssm_c_re_2"][0].transpose(0, 2, 1)),
                     states(a["ssm_c_im_2"][0].transpose(0, 2, 1))], axis=1)
    arrays = {"weights": weights, "cond": cond, "params": params, "tokens": tokens,
              "bmat": bmat, "cmat": cmat, "positions": a["positions_2"]}
    aps = [nc.dram_tensor(n, x.shape, mybir.dt.from_np(x.dtype), kind="ExternalInput").ap()
           for n, x in arrays.items()]
    out = nc.dram_tensor("out", (D, SEQ), F32, kind="ExternalOutput").ap()
    build(nc, *aps, out)
    r = run_bass_kernel_spmd(nc, [arrays], core_ids=[0])
    return np.ascontiguousarray(r.results[0]["out"].T)[None]
```

```python
from contextlib import ExitStack

import concourse.bass as bass
from concourse import mybir
import numpy as np

F32 = mybir.dt.float32
F32R = mybir.dt.float32r
I32 = mybir.dt.int32
ALU = mybir.AluOpType
ACT = mybir.ActivationFunctionType
AX = mybir.AxisListType

P = 128
D = 1024
DT = D // P
META = 16
SEQ = 512
L1 = META + SEQ
HALF = L1 // 2
FF = 2816
FT = FF // P
HEADS = 16
EPS = 1e-6

JOB = 8 * P
N_MIX = 0
N_GATE = N_MIX + 8 * DT
N_OUT = N_GATE + 4 * DT
N_UP = N_OUT + 2 * DT
N_DOWN = N_UP + 2 * FT
N_END1 = N_DOWN + FT * DT // 8
N_U = N_END1
N_SSM = N_U + DT
N_LAT = N_SSM + DT
N_ATT = N_LAT + 5
N_GLU = N_ATT + 2 * DT
N_MERGE = N_GLU + 2 * DT
N_OUT2 = N_MERGE + 4 * DT
N_LAST = N_OUT2 + DT
RAW = 2
SPLIT = 4

T_MIX = 0
T_GATE = T_MIX + 10 * DT + 1
T_OUT = T_GATE + 4 * DT
T_UP = T_OUT + DT
T_DOWN = T_UP + 2 * FT
T_U = T_DOWN + DT
T_SSM = T_U + DT
T_LAT = T_SSM + 5 * DT
T_ATT = T_LAT + 5
T_GLU = T_ATT + 8 * DT
T_MERGE = T_GLU + 2 * DT
T_OUT2 = T_MERGE + 4 * DT

PIECES = [(0, 0, 512, 0), (1, 48, 480, 512), (0, 512, 16, 992), (4, 512, 16, 1008),
          (2, 256, 272, 1024), (3, 384, 144, 1296)]
SCORE = 1440
DIAGONAL = [(0, P), (512 + 80, P), (1024, P), (1296, P), (1008, META)]
KPAD = 5 * P

Q_PRE, Q_MIX, Q_PREF, Q_FFN, Q_PRE2, Q_LAT, Q_KV, Q_POST2 = 0, 8, 16, 24, 32, 40, 42, 44

S2 = SEQ
GROUPS, GP, NS = 64, 16, 64
SUB = 8
NC = SEQ // SUB
PAIRS = GROUPS // 2
PT_ = PAIRS // DT
GT = GROUPS // DT
LATT = 256 // P
ROPE = 32
QK = 96
SCALE2 = float(np.float32(QK ** -0.5))
MASKED = -float(2 ** 99)

TURN1 = 6.28125
TURN2 = float(np.float32(int((2 * np.pi - TURN1) * 2 ** 20) / 2 ** 20))
TURN3 = float(np.float32(2 * np.pi - TURN1 - TURN2))
MAGIC = 1.5 * 2 ** 23
PI_BELOW = float(np.nextafter(np.float32(np.pi), np.float32(0)))


class Lin:

    def __init__(self, base, coef=0, reg=None):
        self.base, self.coef, self.reg = base, coef, reg

    def __add__(self, k):
        if isinstance(k, Lin):
            return Lin(self.base + k.base, self.coef + k.coef, self.reg if self.reg is not None else k.reg)
        return Lin(self.base + k, self.coef, self.reg)

    __radd__ = __add__

    def __sub__(self, k):
        return self + (-k)

    def __mul__(self, k):
        return Lin(self.base * k, self.coef * k, self.reg)

    __rmul__ = __mul__

    def __mod__(self, k):
        assert self.coef % k == 0
        return self.base % k

    def __floordiv__(self, k):
        assert self.coef % k == 0
        return Lin(self.base // k, self.coef // k, self.reg)

    @property
    def value(self):
        return self.base if self.reg is None or not self.coef else self.reg * self.coef + self.base


def as_lin(x):
    return x if isinstance(x, Lin) else Lin(x)


def val(x):
    return as_lin(x).value


def positive(x):
    x = as_lin(x)
    return x.base + (x.coef if x.reg is not None else 0) > 0


def slot(turn):
    return as_lin(turn) % 2


def nth(turn):
    return (as_lin(turn) // 2).value


def t_zs(m):
    return T_SSM + 3 + 5 * m if m else T_SSM


def t_turned(m):
    return T_SSM + 5 * m - 1 if m else T_SSM + 1


def t_y(m):
    return T_SSM + 5 * m + (7 if m < DT - 1 else 4)


def cols(start, size):
    return bass.ds(as_lin(start).value, size)


def repeat(eng, steps, unroll, body):
    for j in range(unroll):
        body(Lin(j))
    if steps > unroll:
        with eng.Fori(1, steps // unroll) as i:
            for j in range(unroll):
                body(Lin(j, unroll, i))


def halves(ap):
    return ap.rearrange("p (h t) -> p h t", h=2)


def build(nc, weights, cond, params, tokens, bmat, cmat, positions, out):
    ctx = ExitStack()
    with ctx:
        def sem(name):
            return ctx.enter_context(nc.semaphore(name))

        BASE = 16512

        def sb(name, shape, offset, dt=F32):
            return nc.alloc_sbuf_tensor_at(name, shape, dt, offset=BASE + offset)

        UNIT = DT * L1 * 4
        WH = sb("WH", [P, SPLIT, JOB], 0, F32R)
        WL = sb("WL", [P, SPLIT, JOB], 16384, F32R)
        WR = sb("WR", [P, RAW, JOB], 32768)
        U = [40960 + UNIT * k for k in range(9)]

        def act_tile(name, unit, dt=F32R):
            return sb(name, [P, DT * L1], U[unit], dt)

        XH, XL = act_tile("XH", 0), act_tile("XL", 1)
        YH, YL = act_tile("YH", 2), act_tile("YL", 3)
        OH, OL = act_tile("OH", 4), act_tile("OL", 5)
        MH, ML = act_tile("MH", 6), act_tile("ML", 7)
        H = act_tile("H", 2, F32)
        F = act_tile("F", 3, F32)
        FH = sb("FH", [P, FT * L1], U[3], F32R)
        FL = sb("FL", [P, FT * L1], U[3] + FT * L1 * 4, F32R)
        F2 = act_tile("F2", 0, F32)
        X0 = act_tile("X0", 2, F32)

        A0 = U[6]
        LH = sb("LH", [P, SCORE], A0, F32R)
        LL = sb("LL", [P, SCORE], A0 + 4 * SCORE, F32R)
        AH = sb("AH", [P, SCORE], A0 + 8 * SCORE, F32R)
        AL = sb("AL", [P, SCORE], A0 + 12 * SCORE, F32R)
        A1 = A0 + 16 * SCORE
        QH = sb("QH", [P, L1], A1, F32R)
        QL = sb("QL", [P, L1], A1 + 2112, F32R)
        VH = sb("VH", [P, 5 * P], A1 + 4224, F32R)
        VL = sb("VL", [P, 5 * P], A1 + 6784, F32R)
        assert A1 + 9344 <= U[8]

        M0 = U[8]
        E = sb("E", [P, SCORE], M0)
        KH = sb("KH", [P, KPAD], M0 + 4 * SCORE, F32R)
        KL = sb("KL", [P, KPAD], M0 + 4 * SCORE + 2560, F32R)
        M1 = M0 + 4 * SCORE + 5120
        CT = sb("CT", [P, L1], M1)
        VT = sb("VT", [P, L1], M1 + 2112)
        CV = sb("CV", [P, L1], M1 + 4224)
        PP = sb("PP", [P, L1 + 2], M1 + 6336)
        RB = sb("RB", [P, 2, L1], M1 + 8480)
        SQ = sb("SQ", [P, 2, L1], M1 + 12704)
        M2 = M1 + 16928
        IDENT = sb("IDENT", [P, P], M2)
        ONES = sb("ONES", [P, P], M2 + 512)
        STAGE = sb("STAGE", [P, 2, P], M2 + 1024)
        NTRI = sb("NTRI", [P, P], M2 + 2048, F32R)
        NONE = sb("NONE", [P, P], M2 + 2560, F32R)
        CR = sb("CR", [P, 16], M2 + 3072)
        CHL = sb("CHL", [P, DT, 2], M2 + 3136, F32R)
        MOD = sb("MOD", [P, 24], M2 + 3264)
        NP = params.shape[1]
        PRM = sb("PRM", [P, NP], M2 + 3360)
        MROW = sb("MROW", [P, 4 * P], M1 + 8480)
        M3 = -(-(M2 + 3360 + NP * 4) // 32) * 32
        MB = sb("MB", [P, 24], M3)
        GG = sb("GG", [P, 16], M3 + 96)
        assert M3 + 160 <= 212800

        V = [40960 + 16384 * k for k in range(9)]
        assert V[8] == 172032

        def tile2(name, unit, dt=F32R):
            return sb(name, [P, DT * S2], V[unit], dt)

        X2H, X2L = tile2("X2H", 0), tile2("X2L", 1)
        US = sb("US", [P, GROUPS, NC], V[2])
        SZS = tile2("SZS", 3, F32)
        YG = tile2("YG", 4, F32)
        OMH, OML = tile2("OMH", 6), tile2("OML", 7)
        YGH, YGL = tile2("YGH", 2), tile2("YGL", 5)
        YSH = tile2("YSH", 4)
        YSL = sb("YSL", [P, DT * S2], V[8], F32R)
        G1 = sb("G1", [P, S2], V[8] + 16384)
        G2 = sb("G2", [P, S2], V[8] + 16384 + 2048)
        G3 = sb("G3", [P, S2], V[8] + 16384 + 4096)
        G4 = sb("G4", [P, S2], V[8] + 16384 + 6144)
        M2H, M2L = tile2("M2H", 2), tile2("M2L", 5)
        F3 = tile2("F3", 0, F32)
        RES = tile2("RES", 6, F32)

        def places(start, end):
            at = [start]

            def place(name, shape, dt=F32):
                size = 4 * int(np.prod(shape[1:]))
                t = sb(name, shape, at[0], dt)
                at[0] += -(-size // 32) * 32
                assert at[0] <= end, name
                return t
            return place, at

        place, at5 = places(V[5], V[6])
        UT = place("UT", [P, 2, SUB, NC])
        TK = place("TK", [P, GT, P])
        BT = place("BT", [P, 2, PT_ * P])
        BPR = place("BPR", [P, PT_, SUB, GP])
        BPI = place("BPI", [P, PT_, SUB, GP])
        place, at6 = places(V[6], M1)
        BM = place("BM", [P, 2, PAIRS, GP])
        CM = place("CM", [P, 2, PAIRS, GP])
        BBR = place("BBR", [P, PAIRS, GP])
        BBI = place("BBI", [P, PAIRS, GP])
        NCI = place("NCI", [P, PAIRS, GP])
        c1_at = at6[0]
        C1 = place("C1", [P, PAIRS, GP])
        C2 = place("C2", [P, PAIRS, GP])
        PWR = place("PWR", [P, PAIRS, SUB + 1])
        PWI = place("PWI", [P, PAIRS, SUB + 1])
        RVR = place("RVR", [P, PAIRS, SUB])
        RVI = place("RVI", [P, PAIRS, SUB])
        WAR_ = place("WAR_", [P, PAIRS, 8])
        WAI = place("WAI", [P, PAIRS, 8])
        WBR = place("WBR", [P, PAIRS, 8])
        WBI = place("WBI", [P, PAIRS, 8])
        SM = [place(f"SM{i}", [P, PAIRS]) for i in range(24)]
        TS = place("TS", [P, 2, 8 * PAIRS])
        after_setup = at6[0]
        place, at7 = places(after_setup, M2)
        CPR = [place("CPR0", [P, PT_, SUB + 1, GP]), sb("CPR1", [P, PT_, SUB + 1, GP], V[6])]
        CPI = [place("CPI0", [P, PT_, SUB + 1, GP]), sb("CPI1", [P, PT_, SUB + 1, GP], c1_at)]
        K1 = place("K1", [P, PT_, SUB + 1, GP])
        K2 = place("K2", [P, PT_, SUB + 1, GP])
        GS = place("GS", [GP, GT * P])
        WC = place("WC", [P, PT_, 8, 8])
        WS = place("WS", [P, PT_, 8, 8])
        VR = place("VR", [P, PT_, NC])
        VI = place("VI", [P, PT_, NC])
        V1 = place("V1", [P, PT_, NC])
        V2 = place("V2", [P, PT_, NC])
        MT = place("MT", [P, PT_, NC])
        SR = [place(f"SR{k}", [P, PT_, NC + 1]) for k in range(2)]
        SI = [place(f"SI{k}", [P, PT_, NC + 1]) for k in range(2)]
        UD = place("UD", [P, GT, NC])
        YT = place("YT", [P, GT, NC])
        YF = place("YF", [P, SUB, NC])

        place, at8 = places(V[2], V[3])
        LQH = place("LQH", [P, LATT * S2], F32R)
        LQL = place("LQL", [P, LATT * S2], F32R)
        LKH = place("LKH", [P, LATT * S2], F32R)
        LKL = place("LKL", [P, LATT * S2], F32R)
        place, at9 = places(V[5], V[6])
        Q2H = [place(f"Q2H{x}", [P, S2], F32R) for x in range(2)]
        Q2L = [place(f"Q2L{x}", [P, S2], F32R) for x in range(2)]
        K2H = [place(f"K2H{x}", [P, S2], F32R) for x in range(2)]
        K2L = [place(f"K2L{x}", [P, S2], F32R) for x in range(2)]
        LATF = sb("LATF", [P, 2 * LATT * S2], V[6])
        place, at10 = places(V[8], M2)
        TAB = place("TAB", [P, S2])
        RO = place("RO", [P, S2])
        POSI = sb("POSI", [P, S2], V[8] + 2048, I32)
        PTH = place("PTH", [P, 4, S2], F32R)
        PTL = place("PTL", [P, 4, S2], F32R)
        V2H = place("V2H", [P, 4 * P], F32R)
        V2L = place("V2L", [P, 4 * P], F32R)
        PB = place("PB", [P, 2, S2])
        VZ = place("VZ", [P, S2])
        MX = place("MX", [P, 8])
        NM = place("NM", [P, 8])
        SU = place("SU", [P, 8])
        RC = place("RC", [P, 8])
        R2 = sb("R2", [P, S2], M2 + 1024)

        u_dram = nc.dram_tensor("u_dram", (D, SUB, NC), F32).ap()
        y_dram = nc.dram_tensor("y_dram", (DT, P, GT, NC), F32).ap()
        res_dram = nc.dram_tensor("res_dram", (P, DT, S2), F32).ap()

        J = [nc.alloc_psum_tensor(f"J{s}", [P, 1024], F32) for s in range(2)]
        Z = nc.alloc_psum_tensor("Z", [P, 1536], F32)
        ZT = nc.alloc_psum_tensor("ZT", [P, 512], F32)
        PTB = [Z[:, 1024:1536], ZT[:]]
        JV = [halves(j[:])[:, :, 0:HALF] for j in J]
        ZV = halves(Z[:, 0:1024])[:, :, 0:HALF]

        g_pre, g_mix, g_pref, g_ffn, b_gate, cw_mix, cw_ffn = (PARAM[k] for k in (
            "g_pre_mix", "g_post_mix", "g_pre_ffn", "g_post_ffn", "b_gate", "conv_w_mix", "conv_w_ffn"))

        (a_bada, a_gpre2, a_gpost2, a_glat, a_bglu, a_are, a_aim, a_ldt, a_d, a_inv, a_sgn) = (PARAM[k] for k in (
            "b_ada", "g_pre_2", "g_post_2", "g_lat", "b_glu", "a_re", "a_im", "log_dt", "ssm_d", "inv_freq", "sign"))

        in_landed = sem("in_landed")
        x_landed = sem("x_landed")
        h_landed = sem("h_landed")
        w_landed = [sem(f"w_landed{s}") for s in range(RAW)]
        w_hi = sem("w_hi")
        w_lo = sem("w_lo")
        job_done = sem("job_done")
        read_out = [sem(f"read_out{s}") for s in range(2)]
        consts = sem("consts")
        const_r = sem("const_r")
        zeroed = sem("zeroed")
        zeroed_act = sem("zeroed_act")
        c_lo = sem("c_lo")
        sq_done = sem("sq_done")
        sq_summed = sem("sq_summed")
        r_step = sem("r_step")
        r_ready = sem("r_ready")
        xf_ready = sem("xf_ready")
        xh_ready = sem("xh_ready")
        xl_ready = sem("xl_ready")
        t_ready = sem("t_ready")
        h_ready = sem("h_ready")
        qk_hi = sem("qk_hi")
        z_done = sem("z_done")
        soft_step = sem("soft_step")
        sp_ready = sem("sp_ready")
        lf_masked = sem("lf_masked")
        lf_hi = sem("lf_hi")
        lf_lo = sem("lf_lo")
        cum_done = sem("cum_done")
        a_exp = sem("a_exp")
        a_masked = sem("a_masked")
        a_hi = sem("a_hi")
        a_lo = sem("a_lo")
        pv_done = sem("pv_done")
        o_hi = sem("o_hi")
        vt_done = sem("vt_done")
        v_hi = sem("v_hi")
        conv_step = sem("conv_step")
        y_hi = sem("y_hi")
        y_lo = sem("y_lo")
        gate_step = sem("gate_step")
        mf_ready = sem("mf_ready")
        m_hi = sem("m_hi")
        m_lo = sem("m_lo")
        u_copied = sem("u_copied")
        fconv_step = sem("fconv_step")
        gelu_done = sem("gelu_done")
        f_hi = sem("f_hi")
        f_lo = sem("f_lo")
        down_done = sem("down_done")
        stored = sem("stored")
        zeroed_pool = sem("zeroed_pool")

        res_saved = sem("res_saved")
        mat_landed = sem("mat_landed")
        mod_rows = sem("mod_rows")
        mod_turned = sem("mod_turned")
        mod_ready = sem("mod_ready")
        setup = sem("setup")
        trig_in = sem("trig_in")
        trig_out = sem("trig_out")
        ut_copied = sem("ut_copied")
        u_stored = [sem(f"u_stored{k}") for k in range(2)]
        us_landed = [sem(f"us_landed{k}") for k in range(2)]
        pool_step = sem("pool_step")
        cp_ready = sem("cp_ready")
        bp_ready = sem("bp_ready")
        ud_ready = sem("ud_ready")
        pow_ready = sem("pow_ready")
        bt_turned = sem("bt_turned")
        g_done = sem("g_done")
        tk_landed = sem("tk_landed")
        b_done = sem("b_done")
        s_ready = sem("s_ready")
        y_done = sem("y_done")
        tk_zeroed = sem("tk_zeroed")
        turn_ready = sem("turn_ready")
        tables_ready = sem("tables_ready")
        ygelu = sem("ygelu")
        y_stored = sem("y_stored")
        yf_landed = sem("yf_landed")
        yg_ready = sem("yg_ready")
        pos_landed = sem("pos_landed")
        pattern = sem("pattern")
        up_done = sem("up_done")
        q_top = sem("q_top")
        rope_ready = sem("rope_ready")
        rope_hi = sem("rope_hi")
        q_ready = sem("q_ready")
        kr_ready = sem("kr_ready")
        k_hi = sem("k_hi")
        kr_hi = sem("kr_hi")
        roped = sem("roped")
        v2_turned = sem("v2_turned")
        v2_hi = sem("v2_hi")
        s_done = sem("s_done")
        nm_ready = sem("nm_ready")
        p_exp = sem("p_exp")
        rc_ready = sem("rc_ready")
        mx_ready = sem("mx_ready")
        pn_ready = sem("pn_ready")
        pt_done = sem("pt_done")
        pt_hi = sem("pt_hi")
        pt_lo = sem("pt_lo")
        pv2_done = sem("pv2_done")
        om_ready = sem("om_ready")
        om_hi = sem("om_hi")
        om_lo = sem("om_lo")
        yg_hi = sem("yg_hi")
        yg_lo = sem("yg_lo")
        glu_step = sem("glu_step")
        ys_hi = sem("ys_hi")
        ys_lo = sem("ys_lo")
        m2_ready = sem("m2_ready")
        m2_hi = sem("m2_hi")
        m2_lo = sem("m2_lo")
        res_landed = sem("res_landed")
        fin = sem("fin")
        stored2 = sem("stored2")

        def down_slots_after(m):
            return min(N_DOWN + FT * (m + 1) // 8 + SPLIT, N_U + SPLIT - 1)

        block = ctx.enter_context(nc.Block())

        @block.sync
        def _(sp):
            sp.dma_start(PRM[:], params).then_inc(in_landed, 16)
            sp.dma_start(CR[:], cond).then_inc(in_landed, 16)
            x_view = tokens.rearrange("(m p) t -> p m t", p=P)
            for m in range(0, DT, 2):
                sp.dma_start(X0[:, m * L1:(m + 2) * L1].rearrange("p (m t) -> p m t", m=2),
                             x_view[:, m:m + 2]).then_inc(x_landed, 16)

            def load_weights(n, slots=RAW):
                n = as_lin(n)
                for s in range(slots):
                    if positive(n + s - RAW + 1):
                        sp.wait_ge(w_lo, val(n + s - RAW + 1))
                    sp.dma_start(WR[:, s, :], weights[cols(n + s, 1)].rearrange("a p n -> (a p) n"))\
                      .then_inc(w_landed[s], 16)

            def stream(first, last):
                repeat(sp, (last - first) // RAW, 1, lambda i: load_weights(first + RAW * i))

            stream(0, N_OUT + 2)
            sp.wait_ge(job_done, N_OUT)
            sp.dma_start(H[:].rearrange("p (m t) -> p m t", m=DT), x_view).then_inc(h_landed, 16)
            def load_one(n):
                s = n % RAW
                sp.wait_ge(w_lo, val(n - RAW + 1))
                sp.dma_start(WR[:, s, :], weights[n]).then_inc(w_landed[s], 16)

            stream(N_OUT + 2, N_U)
            for m in range(3):
                load_one(N_U + m)
            sp.wait_ge(h_ready, 2 * DT)
            sp.dma_start(res_dram, H[:].rearrange("p (m t) -> p m t", m=DT)[:, :, META:]).then_inc(res_saved, 16)
            sp.dma_start(BM[:], bmat).then_inc(mat_landed, 16)
            sp.dma_start(CM[:], cmat).then_inc(mat_landed, 16)

            def store_u(m):
                sp.wait_ge(ut_copied, val(m + 1))
                sp.dma_start(u_dram[m * P:(m + 1) * P], UT[:, m % 2]).then_inc(u_stored[m % 2], 16)

            def load_us(half):
                for k in range(2):
                    sp.wait_ge(u_stored[k], val(16 * (2 * half + 2)))
                g = slice(half * GROUPS // 2, (half + 1) * GROUPS // 2)
                src = u_dram.rearrange("(g p) j c -> j p g c", p=GP)
                for j in range(SUB):
                    sp.dma_start(US[j * GP:(j + 1) * GP, g], src[j][:, g]).then_inc(us_landed[half], 16)

            for m in range(3, DT):
                load_one(N_U + m)
                if m >= 4:
                    store_u(m - 4)
            sp.wait_ge(res_saved, 16)
            sp.wait_ge(xl_ready, 3 * DT)
            for k in range(4):
                load_one(N_SSM + k)
                store_u(4 + k)
                if k == 0:
                    load_us(0)
            load_us(1)

            def load_kernel(m):
                t = t_turned(m) + 1
                sp.wait_ge(read_out[slot(t)], nth(t) + 1)
                if positive(m):
                    sp.wait_ge(y_done, val(m))
                sp.wait_ge(tk_zeroed, 1)
                src = GS[:].rearrange("p (g n) -> p g n", g=GT)
                for j in range(SUB):
                    sp.dma_start(TK[j * GP:(j + 1) * GP, :, j * GP:], src[:, :, 0:P - j * GP]).then_inc(tk_landed, 16)

            def turn_y(m):
                sp.wait_ge(ygelu, val(m + 1))
                sp.dma_start(y_dram[m], YT[:]).then_inc(y_stored, 16)
                sp.wait_ge(y_stored, 16 * (m + 1))
                if positive(m):
                    sp.wait_ge(yg_ready, val(m))
                src = y_dram[m].rearrange("(i q) g c -> g q i c", q=GP)
                for g in range(GT):
                    sp.dma_start(YF[g * GP:(g + 1) * GP], src[g]).then_inc(yf_landed, 16)

            load_kernel(0)
            for m in range(DT):
                if N_SSM + 4 + m < N_ATT:
                    load_one(N_SSM + 4 + m)
                if m + 1 < DT:
                    load_kernel(m + 1)
                turn_y(m)
            for n in range(N_SSM + 4 + DT, N_ATT):
                load_one(n)
            sp.dma_start(POSI[:], positions.partition_broadcast(P)).then_inc(pos_landed, 16)
            n = N_ATT
            if n % 2:
                load_one(n)
                n += 1
            stream(n, n + (N_LAST - n) // 2 * 2)
            for n in range(n + (N_LAST - n) // 2 * 2, N_LAST):
                load_one(n)
            sp.wait_ge(job_done, N_OUT2)
            sp.dma_start(RES[:].rearrange("p (m t) -> p m t", m=DT), res_dram).then_inc(res_landed, 16)
            o_view = out.rearrange("(m p) t -> p m t", p=P)
            for m in range(DT):
                sp.wait_ge(fin, val(m + 1))
                sp.dma_start(o_view[:, m], F3[:, m * S2:(m + 1) * S2]).then_inc(stored, 16)
            sp.wait_ge(stored, 16 * DT)

        @block.tensor
        def _(pe):
            def job(n, t, xh, xl, ready=None, before=0):
                n, t = as_lin(n), as_lin(t)
                s, o = n % SPLIT, J[t % 2]
                if positive(t - 1):
                    pe.wait_ge(read_out[slot(t)], nth(t))
                pe.wait_ge(w_lo, val(n + 1))
                for k in range(8):
                    w = slice(k * P, (k + 1) * P)
                    if ready is not None:
                        pe.wait_ge(ready, before + k + 1)
                    for i, (ws, xs) in enumerate(((WH, xh), (WH, xl), (WL, xh))):
                        for h in range(2):
                            mm = pe.matmul(o[:, 512 * h:512 * h + HALF], ws[:, s, w],
                                           xs[:, k * L1 + h * HALF:k * L1 + (h + 1) * HALF],
                                           start=(k == 0 and i == 0), stop=(k == 7 and i == 2))
                mm.then_inc(job_done, 1)

            def ada(n, width, first, last, before):
                n, before = as_lin(n), as_lin(before)
                s = n % SPLIT
                pe.wait_ge(w_lo, val(n + 1))
                if first and positive(before):
                    pe.wait_ge(mod_ready, val(before))
                k0 = 0 if first else first_tile[0]
                tiles = JOB // width
                for k in range(tiles):
                    for i, ws in enumerate((WH, WL)):
                        mm = pe.matmul(ZT[0:2, 0:width], CHL[:, k0 + k], ws[:, s, k * width:(k + 1) * width],
                                       start=(first and k == 0 and i == 0), stop=(last and k == tiles - 1 and i == 1))
                first_tile[0] = k0 + tiles
                mm.then_inc(job_done, 1)

            first_tile = [0]

            def turn_ada(chunk, width):
                pe.wait_ge(mod_rows, val(as_lin(chunk) + 1))
                for x in range(width // P):
                    mm = pe.matmul(ZT[:, x:x + 1], MROW[0:2, P * x:P * (x + 1)], ONES[0:2, 0:1],
                                   start=x == 0, stop=True, skip_group_check=True)
                mm.then_inc(mod_turned, 1)

            def sum_squares(q, first, last):
                q = as_lin(q)
                pe.wait_ge(sq_done, val(q + 1))
                for h in range(2):
                    mm = pe.matmul(Z[:, 512 * h:512 * h + HALF], ONES[:],
                                   SQ[:, q % 2, h * HALF:(h + 1) * HALF], start=first, stop=last,
                                   skip_group_check=True)
                mm.then_inc(sq_summed, 1)

            pe.wait_ge(consts, 3)
            for m in range(DT):
                sum_squares(Q_PRE + m, m == 0, m == DT - 1)

            def scores(h):
                h = as_lin(h)
                r = slice(64 * (h % 2), 64 * (h % 2) + 64)
                if positive(h):
                    pe.wait_ge(a_exp, val(h))
                banks = set()
                for kt, t0, w, c in PIECES:
                    for ks, qs in ((KH, QH), (KH, QL), (KL, QH)):
                        mm = pe.matmul(Z[:, c:c + w], ks[r, kt * P:(kt + 1) * P], qs[r, t0:t0 + w],
                                       start=c // 512 not in banks, stop=True, skip_group_check=True)
                        banks.add(c // 512)
                mm.then_inc(z_done, 1)

            def accumulate(h):
                h = as_lin(h)
                pe.wait_ge(lf_lo, val(h + 1))
                for kt, t0, w, c in PIECES:
                    for jt, u0, v, d in PIECES:
                        a, b = max(t0, u0, P * jt), min(t0 + w, u0 + v)
                        if jt < kt or a >= b:
                            continue
                        for ls in (LH, LL):
                            mm = pe.matmul(Z[:, c + a - t0:c + b - t0], (NTRI if jt == kt else NONE)[:],
                                           ls[:, d + a - u0:d + b - u0], start=False, stop=True,
                                           skip_group_check=True)
                mm.then_inc(cum_done, 1)

            def values(h, t):
                h, t = as_lin(h), as_lin(t)
                pe.wait_ge(read_out[slot(t)], nth(t))
                pe.wait_ge(a_lo, val(h + 1))
                o = J[t % 2]
                parts = [(kt, max(t0, P * kt, x), min(t0 + w, x + HALF), c - t0)
                         for x in (0, HALF) for kt, t0, w, c in PIECES
                         if max(t0, P * kt, x) < min(t0 + w, x + HALF)]
                seen = set()
                for kt, a, b, c in parts:
                    half = a // HALF
                    at = 512 * half - HALF * half
                    for vs, ps in ((VH, AH), (VH, AL), (VL, AH)):
                        mm = pe.matmul(o[:, at + a:at + b], vs[:, kt * P:(kt + 1) * P], ps[:, c + a:c + b],
                                       start=half not in seen, stop=True, skip_group_check=True)
                        seen.add(half)
                mm.then_inc(pv_done, 1)

            def turn_values(t, tiles):
                t = as_lin(t)
                pe.wait_ge(read_out[slot(t)], nth(t))
                for i, kt in enumerate(tiles):
                    w = min(P, L1 - kt * P)
                    mm = pe.transpose(J[t % 2][0:w, P * i:P * (i + 1)], VT[:, kt * P:kt * P + w], IDENT[:])
                mm.then_inc(vt_done, 1)

            pe.wait_ge(c_lo, 1)
            pe.wait_ge(const_r, 2)
            pe.wait_ge(zeroed_act, 2)
            pe.wait_ge(zeroed, 2)

            def mix(m):
                n, t, h = N_MIX + 8 * m, T_MIX + 10 * m, 2 * m
                first = m.reg is None and m.base == 0
                job(n, t, XH, XL, xl_ready if first else None)
                job(n + 1, t + 1, XH, XL)
                if m.base or m.reg is not None:
                    values(h - 1, t + 2)
                pe.wait_ge(read_out[slot(t)], nth(t) + 1)
                pe.wait_ge(read_out[slot(t + 1)], nth(t + 1) + 1)
                scores(h)
                job(n + 2, t + 3, XH, XL)
                job(n + 3, t + 4, XH, XL)
                pe.wait_ge(read_out[slot(t + 3)], nth(t + 3) + 1)
                turn_values(t + 5, (0, 1, 2))
                accumulate(h)
                turn_values(t + 6, (3, 4))
                job(n + 4, t + 7, XH, XL)
                scores(h + 1)
                job(n + 5, t + 8, XH, XL)
                pe.wait_ge(read_out[slot(t + 5)], nth(t + 5) + 1)
                pe.wait_ge(read_out[slot(t + 6)], nth(t + 6) + 1)
                values(h, t + 9)
                ada(n + 6, 2 * P, True, False, m)
                ada(n + 7, 2 * P, False, True, m)
                accumulate(h + 1)
                turn_ada(m, 2 * P)

            repeat(pe, DT, 1, mix)
            values(HEADS - 1, T_MIX + 10 * DT)

            def gates(m):
                n, t = N_GATE + 4 * m, T_GATE + 4 * m
                job(n, t, XH, XL)
                job(n + 1, t + 1, XH, XL)
                if m.reg is None and m.base == 0:
                    pe.wait_ge(y_lo, DT)
                    pe.wait_ge(read_out[slot(T_MIX + 10 * DT)], nth(T_MIX + 10 * DT) + 1)
                job(n + 2, t + 2, YH, YL)
                job(n + 3, t + 3, OH, OL)

            repeat(pe, DT, 1, gates)

            for m in range(DT):
                job(N_OUT + 2 * m, T_OUT + m, MH, ML, m_lo if m == 0 else None)
                if m:
                    sum_squares(Q_MIX + m - 1, m == 1, False)
                if m == DT // 2:
                    turn_ada(DT, 4 * P)
                ada(N_OUT + 2 * m + 1, 4 * P, m % 4 == 0, m % 4 == 3, DT + m // 4)
            sum_squares(Q_MIX + DT - 1, False, True)
            turn_ada(DT + 1, 4 * P)
            pe.wait_ge(r_ready, 2)
            for m in range(DT):
                sum_squares(Q_PREF + m, m == 0, m == DT - 1)

            def up(i):
                first = i.reg is None and i.base == 0
                job(N_UP + 2 * i, T_UP + 2 * i, XH, XL, xl_ready if first else None, DT)
                job(N_UP + 2 * i + 1, T_UP + 2 * i + 1, XH, XL)

            repeat(pe, FT, 2, up)

            for m in range(DT):
                t = T_DOWN + m
                pe.wait_ge(read_out[slot(t)], nth(t))
                for k in range(FT):
                    b = FT * m + k
                    n, w = N_DOWN + b // 8, slice(b % 8 * P, (b % 8 + 1) * P)
                    if b % 8 == 0:
                        pe.wait_ge(w_lo, val(n + 1))
                    if m == 0:
                        pe.wait_ge(f_lo, k + 1)
                    for i, (ws, xs) in enumerate(((WH, FH), (WH, FL), (WL, FH))):
                        for h in range(2):
                            mm = pe.matmul(J[t % 2][:, 512 * h:512 * h + HALF], ws[:, n % SPLIT, w],
                                           xs[:, k * L1 + h * HALF:k * L1 + (h + 1) * HALF],
                                           start=(k == 0 and i == 0), stop=(k == FT - 1 and i == 2))
                    if b % 8 == 7:
                        mm.then_inc(job_done, 1)
                    elif k == FT - 1:
                        mm.then_inc(down_done, 1)
                if m:
                    if m == 1:
                        pe.wait_ge(r_ready, 3)
                    sum_squares(Q_FFN + m - 1, m == 1, False)
            sum_squares(Q_FFN + DT - 1, False, True)

            def sum_squares2(q, first, last):
                q = as_lin(q)
                pe.wait_ge(sq_done, val(q + 1))
                pe.matmul(Z[:, 0:S2], ONES[:], SQ[:, q % 2, 0:S2], start=first, stop=last,
                          skip_group_check=True).then_inc(sq_summed, 1)

            def job2(n, t, xh, xl, ready=None, before=0):
                n, t = as_lin(n), as_lin(t)
                s, o = n % SPLIT, J[t % 2]
                pe.wait_ge(read_out[slot(t)], nth(t))
                pe.wait_ge(w_lo, val(n + 1))
                for k in range(8):
                    w = slice(k * P, (k + 1) * P)
                    if ready is not None:
                        pe.wait_ge(ready, before + k + 1)
                    for i, (ws, xs) in enumerate(((WH, xh), (WH, xl), (WL, xh))):
                        mm = pe.matmul(o[:, 0:S2], ws[:, s, w], xs[:, k * S2:(k + 1) * S2],
                                       start=(k == 0 and i == 0), stop=(k == 7 and i == 2))
                mm.then_inc(job_done, 1)

            pe.wait_ge(r_step, 2 * 3 + 2)
            for m in range(DT):
                sum_squares2(Q_PRE2 + m, m == 0, m == DT - 1)
            for m in range(DT):
                job2(N_U + m, T_U + m, X2H, X2L, xl_ready if m == 0 else None, 2 * DT)

            def half_rows(x):
                return slice(64 * x, 64 * x + 64)

            def states_in(m):
                t = t_turned(m)
                pe.wait_ge(read_out[slot(t)], nth(t))
                pe.wait_ge(bp_ready, val(m + 1))
                for x, b in enumerate((BPR, BPI)):
                    for pr in range(PT_):
                        mm = pe.transpose(J[t % 2][:, 512 * x + P * pr:512 * x + P * (pr + 1)],
                                          b[:, pr].rearrange("p j q -> p (j q)"), IDENT[:])
                mm.then_inc(bt_turned, 1)
                pe.wait_ge(read_out[slot(t + 1)], nth(t + 1))
                pe.wait_ge(cp_ready, val(m + 1))
                for g in range(GT):
                    pr, r = g // 2, half_rows(g % 2)
                    for x, (bb, cp) in enumerate(((BBR, CPR[m % 2]), (BBI, CPI[m % 2]))):
                        at = 512 * (g % 2) + P * (g // 2)
                        mm = pe.matmul(J[(t + 1) % 2][0:GP, at:at + P], bb[r, PT_ * m + pr],
                                       cp[r, pr, 0:SUB].rearrange("p i q -> p (i q)"),
                                       start=x == 0, stop=x == 1, skip_group_check=True)
                mm.then_inc(g_done, 1)
                pe.wait_ge(read_out[slot(t + 2)], nth(t + 2))
                pe.wait_ge(read_out[slot(t)], nth(t) + 1)
                pe.wait_ge(us_landed[m // 4], 16 * SUB)
                for g in range(GT):
                    pr, r = g // 2, half_rows(g % 2)
                    for x in range(2):
                        mm = pe.matmul(J[(t + 2) % 2][r, 512 * x + NC * pr:512 * x + NC * (pr + 1)],
                                       BT[:, x, P * pr + 64 * (g % 2):P * pr + 64 * (g % 2) + 64],
                                       US[:, GT * m + g], start=True, stop=True, skip_group_check=True)
                mm.then_inc(b_done, 1)

            for m in range(DT):
                job2(N_SSM + m, t_zs(m), X2H, X2L)
                if m == 0:
                    states_in(0)
                if m + 1 < DT:
                    states_in(m + 1)
                t = t_y(m)
                pe.wait_ge(read_out[slot(t)], nth(t))
                pe.wait_ge(tk_landed, val(16 * SUB * (m + 1)))
                pe.wait_ge(s_ready, val(m + 1))
                for g in range(GT):
                    pr, r = g // 2, half_rows(g % 2)
                    at = 512 * (g % 2) + NC * (g // 2)
                    o = J[t % 2][:, at:at + NC]
                    pe.matmul(o, TK[:, g], US[:, GT * m + g], start=True, stop=False, skip_group_check=True)
                    for x, (cp, st) in enumerate(((CPR[m % 2], SR[m % 2]), (CPI[m % 2], SI[m % 2]))):
                        mm = pe.matmul(o, cp[r, pr, 1:SUB + 1].rearrange("p i q -> p (i q)"), st[r, pr, 0:NC],
                                       start=False, stop=x == 1, skip_group_check=True)
                mm.then_inc(y_done, 1)

            for k in range(4):
                job2(N_LAT + k, T_LAT + k, X2H, X2L)
                if k:
                    if k == 3:
                        pe.wait_ge(r_step, 2 * 5 + 1)
                    sum_squares2(Q_LAT + k - 1, k % 2 == 1, k % 2 == 0)
            job2(N_LAT + 4, T_LAT + 4, X2H, X2L)
            sum_squares2(Q_LAT + 3, False, True)
            pe.wait_ge(xl_ready, 3 * DT + LATT)

            def attend(m):
                n, t, h = N_ATT + 2 * m, T_ATT + 8 * m, 2 * m
                s = n % SPLIT

                def up(j, turn, xh, xl):
                    pe.wait_ge(read_out[slot(turn)], nth(turn))
                    for k in range(LATT):
                        w = slice((LATT * j + k) * P, (LATT * j + k + 1) * P)
                        for i, (ws, xs) in enumerate(((WH, xh), (WH, xl), (WL, xh))):
                            mm = pe.matmul(J[turn % 2][:, 0:S2], ws[:, s, w], xs[:, k * S2:(k + 1) * S2],
                                           start=(k == 0 and i == 0), stop=(k == LATT - 1 and i == 2))
                    return mm

                pe.wait_ge(w_lo, val(n + 1))
                up(0, t, LQH, LQL).then_inc(up_done, 1)
                up(1, t + 1, LQH, LQL).then_inc(up_done, 1)
                if m.reg is None and m.base == 0:
                    pe.wait_ge(xl_ready, 3 * DT + 2 * LATT)
                up(2, t + 2, LKH, LKL).then_inc(up_done, 1)
                up(3, t + 3, LKH, LKL).then_inc(job_done, 1)

                def score(u):
                    g, x, i = 8 * m + u, u // 4, u % 4
                    if positive(g - 1):
                        pe.wait_ge(p_exp, val(g - 1))
                    for a, (qs, ks) in enumerate(((Q2H, K2H), (Q2H, K2L), (Q2L, K2H))):
                        mm = pe.matmul(Z[:, 512 * (u % 2):512 * (u % 2) + P * (i + 1)], qs[x][:, P * i:P * (i + 1)],
                                       ks[x][:, 0:P * (i + 1)], start=a == 0, stop=a == 2, skip_group_check=True)
                    mm.then_inc(s_done, 1)

                def turn_weights(u):
                    g, i = 8 * m + u, u % 4
                    pe.wait_ge(pn_ready, val(g + 1))
                    if positive(g - 1):
                        pe.wait_ge(pt_lo, val(g - 1))
                    for j in range(i + 1):
                        mm = pe.transpose(PTB[u % 2][:, P * j:P * (j + 1)], PB[:, u % 2, P * j:P * (j + 1)], IDENT[:])
                    mm.then_inc(pt_done, 1)

                def values2(x):
                    pe.wait_ge(read_out[slot(t + 6 + x)], nth(t + 6 + x))
                    pe.wait_ge(read_out[slot(t + 4)], nth(t + 4) + 1)
                    pe.wait_ge(pt_lo, val(8 * m + 4 * x + 4))
                    for j in range(4):
                        for a, (vs, ps) in enumerate(((V2H, PTH), (V2H, PTL), (V2L, PTH))):
                            mm = pe.matmul(J[(t + 6 + x) % 2][:, P * j:S2], vs[:, P * j:P * (j + 1)],
                                           ps[:, j, P * j:], start=(j == 0 and a == 0), stop=(j == 3 and a == 2),
                                           skip_group_check=True)
                    mm.then_inc(pv2_done, 1)

                pe.wait_ge(read_out[slot(t + 1)], nth(t + 1) + 1)
                pe.wait_ge(read_out[slot(t + 2)], nth(t + 2) + 1)
                pe.wait_ge(q_ready, val(m + 1))
                if m.reg is None and m.base == 0:
                    pe.wait_ge(kr_ready, 1)
                    pe.wait_ge(kr_hi, 2)
                score(0)
                score(1)
                pe.wait_ge(read_out[slot(t + 4)], nth(t + 4))
                pe.wait_ge(read_out[slot(t + 3)], nth(t + 3) + 1)
                for k in range(4):
                    mm = pe.transpose(J[(t + 4) % 2][:, P * k:P * (k + 1)], R2[:, P * k:P * (k + 1)], IDENT[:])
                mm.then_inc(v2_turned, 1)

                def z_m(first, last):
                    for k in range(first, last):
                        w = slice(k * P, (k + 1) * P)
                        for i, (ws, xs) in enumerate(((WH, X2H), (WH, X2L), (WL, X2H))):
                            mm = pe.matmul(J[(t + 5) % 2][:, 0:S2], ws[:, (n + 1) % SPLIT, w],
                                           xs[:, k * S2:(k + 1) * S2],
                                           start=(k == 0 and i == 0), stop=(k == 7 and i == 2))
                    if last == 8:
                        mm.then_inc(job_done, 1)

                pe.wait_ge(read_out[slot(t + 5)], nth(t + 5))
                pe.wait_ge(w_lo, val(n + 2))
                z_m(0, 3)
                for u in range(8):
                    if u + 2 < 8:
                        score(u + 2)
                    turn_weights(u)
                    if u < 3:
                        z_m((3, 5, 6)[u], (5, 6, 8)[u])
                    if u == 4:
                        values2(0)
                values2(1)

            repeat(pe, DT, 2, attend)


            def glu(m):
                first = m.reg is None and m.base == 0
                job2(N_GLU + 2 * m, T_GLU + 2 * m, YGH, YGL, yg_lo if first else None)
                job2(N_GLU + 2 * m + 1, T_GLU + 2 * m + 1, YGH, YGL)

            repeat(pe, DT, 2, glu)

            def merge(m):
                for j, (xh, xl) in enumerate(((X2H, X2L), (X2H, X2L), (YSH, YSL), (OMH, OML))):
                    if j == 2 and m.reg is None and m.base == 0:
                        pe.wait_ge(om_lo, 2 * DT)
                        pe.wait_ge(ys_lo, DT)
                    job2(N_MERGE + 4 * m + j, T_MERGE + 4 * m + j, xh, xl)

            repeat(pe, DT, 1, merge)
            for m in range(DT):
                job2(N_OUT2 + m, T_OUT2 + m, M2H, M2L, m2_lo if m == 0 else None)
                if m:
                    sum_squares2(Q_POST2 + m - 1, m == 1, False)
            sum_squares2(Q_POST2 + DT - 1, False, True)

        @block.scalar
        def _(act):
            def split_hi(n):
                n = as_lin(n)
                if n.base >= N_LAST:
                    return
                act.wait_ge(w_landed[n % RAW], val(16 * (n // RAW) + 16))
                if positive(n - SPLIT + 1):
                    act.wait_ge(job_done, val(n - SPLIT + 1))
                act.activation(WH[:, n % SPLIT, :], WR[:, n % RAW, :], ACT.Copy).then_inc(w_hi, 1)

            def square(q, src, inc=None):
                q = as_lin(q)
                if positive(q - 1):
                    act.wait_ge(sq_summed, val(q - 1))
                act.activation(halves(SQ[:, q % 2, :]), src, ACT.Square).then_inc(sq_done, 1)

            def job_result(t, n):
                act.wait_ge(job_done, val(as_lin(n) + 1))
                return JV[as_lin(t) % 2]

            act.wait_ge(consts, 3)
            act.activation(NTRI[:], STAGE[:, 0, :], ACT.Copy, scale=-1.0).then_inc(const_r, 1)
            act.activation(NONE[:], STAGE[:, 1, :], ACT.Copy, scale=-1.0).then_inc(const_r, 1)
            act.activation(KH[:, L1:], STAGE[:, 1, 0:KPAD - L1], ACT.Copy, scale=0.0).then_inc(zeroed_act, 1)
            act.activation(KL[:, L1:], STAGE[:, 1, 0:KPAD - L1], ACT.Copy, scale=0.0).then_inc(zeroed_act, 1)
            act.wait_ge(in_landed, 32)
            act.activation(CHL[:].rearrange("p k x -> p (k x)"), CR[:], ACT.Copy).then_inc(w_hi, 1)

            for m in range(DT):
                if m % 2 == 0:
                    act.wait_ge(x_landed, 16 * (DT // 2))
                square(Q_PRE + m, halves(X0[:, m * L1:(m + 1) * L1]))
            for n in range(SPLIT - 2):
                split_hi(n)

            def root(e, width=L1):
                r = RB[:, e % 2, 0:width]
                act.wait_ge(r_step, val(2 * e + 2))
                act.activation(r, r, ACT.Sqrt).then_inc(r_ready, 1)

            root(0)
            for m in range(DT):
                act.wait_ge(xf_ready, val(m + 1))
                act.activation(XH[:, m * L1:(m + 1) * L1], [CT, VT][m % 2][:], ACT.Copy).then_inc(xh_ready, 1)
            split_hi(SPLIT - 2)

            def softplus(h):
                h = as_lin(h)
                act.wait_ge(z_done, val(h + 1))
                if positive(h):
                    act.wait_ge(a_lo, val(h))
                act.activation(E[:], Z[:, 0:SCORE], ACT.Abs).then_inc(soft_step, 1)
                act.wait_ge(soft_step, val(3 * h + 1))
                act.activation(E[:], E[:], ACT.Exp, scale=-1.0).then_inc(soft_step, 1)
                act.wait_ge(soft_step, val(3 * h + 2))
                act.activation(E[:], E[:], ACT.Ln, bias=1.0).then_inc(soft_step, 1)

            def fail_hi(h):
                h = as_lin(h)
                act.wait_ge(lf_masked, val(len(DIAGONAL) * (h + 1)))
                if positive(h):
                    act.wait_ge(cum_done, val(h))
                act.activation(LH[:], E[:], ACT.Copy).then_inc(lf_hi, 1)

            def weight_exp(h):
                h = as_lin(h)
                act.wait_ge(cum_done, val(h + 1))
                act.wait_ge(lf_lo, val(h + 1))
                act.activation(E[:], Z[:, 0:SCORE], ACT.Exp).then_inc(a_exp, 1)

            def weight_hi(h):
                h = as_lin(h)
                act.wait_ge(a_masked, val(len(DIAGONAL) * (h + 1)))
                if positive(h):
                    act.wait_ge(pv_done, val(h))
                act.activation(AH[:], E[:], ACT.Copy).then_inc(a_hi, 1)

            def head_out(h, m, t):
                h = as_lin(h)
                r = slice(64 * (h % 2), 64 * (h % 2) + 64)
                act.wait_ge(pv_done, val(h + 1))
                act.activation(halves(OH[r, cols(m * L1, L1)]), JV[as_lin(t) % 2][r], ACT.Copy).then_inc(o_hi, 1)

            def mix(m):
                n, t, h = N_MIX + 8 * m, T_MIX + 10 * m, 2 * m
                later = m.base or m.reg is not None
                split_hi(n + 3)
                src = job_result(t, n)
                if positive(h):
                    act.wait_ge(z_done, val(h))
                act.activation(halves(QH[:]), src, ACT.Copy, scale=0.125).then_inc(qk_hi, 1)
                split_hi(n + 4)
                src = job_result(t + 1, n + 1)
                act.activation(halves(KH[:, 0:L1]), src, ACT.Copy).then_inc(qk_hi, 1)
                if later:
                    head_out(h - 1, m - 1, t + 2)
                softplus(h)
                split_hi(n + 5)
                fail_hi(h)
                src = job_result(t + 3, n + 2)
                if positive(2 * m):
                    act.wait_ge(vt_done, val(2 * m))
                act.activation(halves(VT[:]), src, ACT.Copy).then_inc(read_out[(t + 3) % 2], 1)
                split_hi(n + 6)
                src = job_result(t + 4, n + 3)
                if positive(m):
                    act.wait_ge(y_lo, val(m))
                act.activation(halves(CT[:]), src, ACT.Copy).then_inc(read_out[(t + 4) % 2], 1)
                act.wait_ge(vt_done, val(2 * m + 1))
                if positive(h):
                    act.wait_ge(pv_done, val(h))
                act.activation(VH[:, 0:3 * P], J[(t + 5) % 2][:, 0:3 * P], ACT.Copy).then_inc(v_hi, 1)
                weight_exp(h)
                act.wait_ge(vt_done, val(2 * m + 2))
                act.activation(VH[:, 3 * P:4 * P], J[(t + 6) % 2][:, 0:P], ACT.Copy)
                act.activation(VH[0:META, 4 * P:], J[(t + 6) % 2][0:META, P:2 * P], ACT.Copy).then_inc(v_hi, 1)
                weight_hi(h)
                split_hi(n + 7)
                split_hi(n + 8)
                softplus(h + 1)
                fail_hi(h + 1)
                act.wait_ge(read_out[slot(t + 8)], nth(t + 8) + 1)
                act.activation(YH[:, cols(m * L1, L1)], CT[:], ACT.Copy).then_inc(y_hi, 1)
                head_out(h, m, t + 9)
                split_hi(n + 9)
                split_hi(n + 10)
                weight_exp(h + 1)
                weight_hi(h + 1)

            repeat(act, DT, 1, mix)
            head_out(HEADS - 1, DT - 1, T_MIX + 10 * DT)

            def gates(m):
                n, t = N_GATE + 4 * m, T_GATE + 4 * m
                for j, g in enumerate((CT, CV)):
                    split_hi(n + 3 + j)
                    src = job_result(t + j, n + j)
                    if m.base == 0 and m.reg is None:
                        act.wait_ge(y_lo, DT)
                    else:
                        act.wait_ge(read_out[slot(t + j - 2)], nth(t + j - 2) + 1)
                    act.activation(halves(g[:]), src, ACT.Sigmoid, bias=PRM[:, cols(b_gate + j * DT + m, 1)])\
                       .then_inc(read_out[(t + j) % 2], 1)
                split_hi(n + 5)
                split_hi(n + 6)
                act.wait_ge(mf_ready, val(m + 1))
                act.activation(MH[:, cols(m * L1, L1)], PP[:, 2:], ACT.Copy).then_inc(m_hi, 1)

            repeat(act, DT, 1, gates)

            for m in range(DT):
                n, t = N_OUT + 2 * m, T_OUT + m
                split_hi(n + 3)
                split_hi(n + 4)
                src = job_result(t, n)
                act.activation(halves(F[:, m * L1:(m + 1) * L1]), src, ACT.Copy)
                act.wait_ge(sq_summed, val(Q_MIX + m - 1))
                act.activation(halves(SQ[:, m % 2, :]), src, ACT.Square).then_inc(sq_done, 1)

            def pre_norm_hi(q, e, count):
                for m in range(DT):
                    act.wait_ge(h_ready, val(count * DT + m + 1))
                    square(q + m, halves(H[:, m * L1:(m + 1) * L1]))
                root(e)
                for m in range(DT):
                    act.wait_ge(xf_ready, val((count + 1) * DT + m + 1))
                    act.activation(XH[:, m * L1:(m + 1) * L1], [CT, VT][m % 2][:], ACT.Copy).then_inc(xh_ready, 1)

            root(1)
            pre_norm_hi(Q_PREF, 2, 0)

            def up(i):
                n, t = N_UP + 2 * i, T_UP + 2 * i
                split_hi(n + 3)
                src = job_result(t, n)
                if positive(3 * i):
                    act.wait_ge(fconv_step, val(3 * i))
                act.activation(halves(PP[:, 2:]), src, ACT.Copy).then_inc(read_out[t % 2], 1)
                split_hi(n + 4)
                act.wait_ge(fconv_step, val(3 * i + 3))
                if i.base or i.reg is not None:
                    act.wait_ge(read_out[slot(t - 1)], nth(t - 1) + 1)
                act.activation(VT[:], CV[:], ACT.Gelu_apprx_tanh).then_inc(gelu_done, 1)
                act.wait_ge(read_out[slot(t + 1)], nth(t + 1) + 1)
                act.activation(FH[:, cols(i * L1, L1)], CT[:], ACT.Copy).then_inc(f_hi, 1)

            repeat(act, FT, 2, up)

            n = N_DOWN + SPLIT - 1
            for m in range(DT):
                t = T_DOWN + m
                while n < down_slots_after(m):
                    split_hi(n)
                    n += 1
                if m % 4 == 3:
                    act.wait_ge(job_done, val(N_DOWN + FT * (m + 1) // 8))
                else:
                    act.wait_ge(down_done, val(m + 1 - m // 4))
                src = JV[t % 2]
                act.activation(halves(F2[:, m * L1:(m + 1) * L1]), src, ACT.Copy)
                act.wait_ge(sq_summed, val(Q_FFN + m - 1))
                act.activation(halves(SQ[:, m % 2, :]), src, ACT.Square).then_inc(sq_done, 1)
            root(3)

            def square2(q, src):
                q = as_lin(q)
                act.wait_ge(sq_summed, val(q - 1))
                return act.activation(SQ[:, q % 2, 0:S2], src, ACT.Square).then_inc(sq_done, 1)

            def result2(n, t):
                act.wait_ge(job_done, val(as_lin(n) + 1))
                return J[as_lin(t) % 2][:, 0:S2]

            for m in range(DT):
                act.wait_ge(h_ready, val(DT + m + 1))
                square2(Q_PRE2 + m, H[:, m * L1 + META:(m + 1) * L1])
            root(4, S2)
            for m in range(DT):
                act.wait_ge(xf_ready, val(2 * DT + m + 1))
                act.activation(X2H[:, m * S2:(m + 1) * S2], [CT, VT][m % 2][:, 0:S2], ACT.Identity,
                               bias=MB[:, m:m + 1]).then_inc(xh_ready, 1)
            for m in range(DT):
                split_hi(N_U + 3 + m)
                src = result2(N_U + m, T_U + m)
                if m >= 2:
                    act.wait_ge(u_stored[m % 2], val(16 * (m // 2)))
                act.activation(UT[:, m % 2], src.rearrange("p (c j) -> p j c", j=SUB), ACT.Copy)\
                   .then_inc(ut_copied, 1)
                if m == 0:
                    act.wait_ge(trig_in, 1)
                    act.activation(SM[0][:], PRM[:, a_ldt:a_ldt + PAIRS], ACT.Exp).then_inc(trig_out, 1)
                if m == 1:
                    act.wait_ge(trig_in, 2)
                    act.activation(SM[5][:], SM[1][:], ACT.Exp).then_inc(trig_out, 1)
                if m == 2:
                    act.wait_ge(trig_in, 3)
                    act.activation(SM[6][:], SM[2][:], ACT.Sin).then_inc(trig_out, 1)
                    act.activation(SM[7][:], SM[2][:], ACT.Sin, scale=0.5).then_inc(trig_out, 1)

            def kernel_out(m):
                t = t_turned(m)
                act.wait_ge(bt_turned, val(m + 1))
                if positive(m):
                    act.wait_ge(b_done, val(m))
                act.activation(BT[:].rearrange("p x n -> p (x n)"), J[t % 2][:], ACT.Copy)\
                   .then_inc(read_out[t % 2], 1)
                act.wait_ge(g_done, val(m + 1))
                if positive(16 * SUB * m):
                    act.wait_ge(tk_landed, val(16 * SUB * m))
                act.activation(GS[:].rearrange("p (r x n) -> p x r n", x=2, n=P),
                               J[(t + 1) % 2][0:GP, :].rearrange("p (x r n) -> p x r n", x=2, n=P), ACT.Copy)\
                   .then_inc(read_out[(t + 1) % 2], 1)

            def y_back(m):
                act.wait_ge(yf_landed, val(16 * GT * (m + 1)))
                act.activation(YG[:, m * S2:(m + 1) * S2].rearrange("p (c i) -> p i c", i=SUB), YF[:], ACT.Copy)\
                   .then_inc(yg_ready, 1)

            for m in range(DT):
                split_hi(N_SSM + m + 3)
                src = result2(N_SSM + m, t_zs(m))
                act.activation(SZS[:, m * S2:(m + 1) * S2], src, ACT.Silu).then_inc(read_out[t_zs(m) % 2], 1)
                if m == 0:
                    kernel_out(0)
                if m:
                    y_back(m - 1)
                if m + 1 < DT:
                    kernel_out(m + 1)
                t = t_y(m)
                act.wait_ge(read_out[slot(t)], nth(t) + 1)
                if positive(16 * m):
                    act.wait_ge(y_stored, val(16 * m))
                act.activation(YT[:], UD[:], ACT.Gelu_apprx_tanh).then_inc(ygelu, 1)
            y_back(DT - 1)

            act.wait_ge(yg_ready, DT)
            for k in range(4):
                split_hi(N_LAT + 3 + k)
                src = result2(N_LAT + k, T_LAT + k)
                act.activation(LATF[:, k * S2:(k + 1) * S2], src, ACT.Copy)
                square2(Q_LAT + k, src)
                if k == 2:
                    act.wait_ge(trig_in, 4)
                    act.activation(TAB[:], TAB[:], ACT.Sin, scale=PRM[:, a_sgn:a_sgn + 1]).then_inc(trig_out, 1)
            for k in range(4):
                if k % LATT == 0:
                    root(5 + k // LATT, S2)
                act.wait_ge(xf_ready, val(3 * DT + k + 1))
                dst = (LQH, LKH)[k // LATT]
                act.activation(dst[:, k % LATT * S2:(k % LATT + 1) * S2], [CT, VT][k % 2][:, 0:S2], ACT.Copy)\
                   .then_inc(xh_ready, 1)
            split_hi(N_LAT + 7)
            act.wait_ge(rope_ready, 1)
            for x in range(2):
                act.activation(K2H[x][64:96], RO[0:32], ACT.Copy).then_inc(rope_hi, 1)
            act.wait_ge(pattern, 6)
            for x in range(2):
                act.activation(Q2H[x][96:P], PB[96:P, 0], ACT.Copy)
                act.activation(Q2L[x][96:P], PB[96:P, 0], ACT.Copy, scale=0.0)
                act.activation(K2H[x][96:P], PB[96:P, 1], ACT.Copy, scale=MASKED)
                act.activation(K2L[x][96:P], PB[96:P, 0], ACT.Copy, scale=0.0).then_inc(kr_hi, 1)

            def attend(m):
                n, t, h = N_ATT + 2 * m, T_ATT + 8 * m, 2 * m
                split_hi(n + 3)
                act.wait_ge(rope_ready, val(m + 2))
                if positive(8 * m):
                    act.wait_ge(s_done, val(8 * m))
                for x in range(2):
                    act.activation(Q2H[x][64:96], RO[32 * x:32 * x + 32], ACT.Copy).then_inc(rope_hi, 1)
                act.wait_ge(up_done, val(3 * m + 2))
                for x in range(2):
                    act.activation(Q2H[x][0:64], J[(t + 1) % 2][64 * x:64 * x + 64, 0:S2], ACT.Copy).then_inc(q_top, 1)
                act.wait_ge(up_done, val(3 * m + 3))
                for x in range(2):
                    mm = act.activation(K2H[x][0:64], J[t % 2][64 * x:64 * x + 64, 0:S2], ACT.Copy)
                mm.then_inc(k_hi, 1)
                src = result2(n, t + 3)
                act.activation(R2[:], src, ACT.Copy).then_inc(read_out[(t + 3) % 2], 1)

                def exponent(u):
                    g, i = 8 * m + u, u % 4
                    act.wait_ge(nm_ready, val(g + 1))
                    if positive(g - 1):
                        act.wait_ge(pt_done, val(g - 1))
                    act.activation(PB[:, u % 2, 0:P * (i + 1)], Z[:, 512 * (u % 2):512 * (u % 2) + P * (i + 1)],
                                   ACT.Exp, scale=SCALE2, bias=NM[:, u:u + 1], accum_out=SU[:, u:u + 1])\
                       .then_inc(p_exp, 1)

                def weights_hi(u):
                    g, i = 8 * m + u, u % 4
                    act.wait_ge(pt_done, val(g + 1))
                    if i == 0:
                        if positive(h + u // 4):
                            act.wait_ge(pv2_done, val(h + u // 4))
                    act.activation(PTH[:, 0:i + 1, P * i:P * (i + 1)],
                                   PTB[u % 2][:, 0:P * (i + 1)].rearrange("p (j s) -> p j s", s=P), ACT.Copy)\
                       .then_inc(pt_hi, 1)

                exponent(0)
                exponent(1)
                act.wait_ge(v2_turned, val(m + 1))
                if positive(h):
                    act.wait_ge(pv2_done, val(h))
                act.activation(V2H[:], J[(t + 4) % 2][:, 0:S2], ACT.Copy).then_inc(v2_hi, 1)
                split_hi(n + 4)
                for u in range(8):
                    if u == 4:
                        src = result2(n + 1, t + 5)
                        if positive(2 * m):
                            act.wait_ge(om_ready, val(2 * m))
                        act.activation(VZ[:], src, ACT.Silu).then_inc(read_out[(t + 5) % 2], 1)
                    weights_hi(u)
                    if u + 2 < 8:
                        exponent(u + 2)
                out_hi(m, 0)
                out_hi(m, 1)

            def out_hi(m, x):
                r = slice(64 * x, 64 * x + 64)
                act.wait_ge(om_ready, val(2 * m + x + 1))
                act.activation(OMH[r, cols(m * S2, S2)], RO[r], ACT.Copy).then_inc(om_hi, 1)

            repeat(act, DT, 2, attend)

            for m in range(DT):
                s = slice(m * S2, (m + 1) * S2)
                act.activation(YGH[:, s], YG[:, s], ACT.Copy).then_inc(yg_hi, 1)

            def glu(m):
                n, t = N_GLU + 2 * m, T_GLU + 2 * m
                split_hi(n + 3)
                src = result2(n, t)
                if positive(2 * m):
                    act.wait_ge(glu_step, val(2 * m))
                act.activation(G2[:], src, ACT.Sigmoid, bias=PRM[:, cols(a_bglu + DT + m, 1)])\
                   .then_inc(read_out[t % 2], 1)
                split_hi(n + 4)
                act.wait_ge(glu_step, val(2 * m + 2))
                if m.base == 0 and m.reg is None:
                    act.wait_ge(yg_lo, DT)
                act.activation(YSH[:, cols(m * S2, S2)], G1[:], ACT.Copy).then_inc(ys_hi, 1)

            repeat(act, DT, 2, glu)

            def merge(m):
                n, t = N_MERGE + 4 * m, T_MERGE + 4 * m
                for j, g in enumerate((G1, G2)):
                    split_hi(n + 3 + j)
                    src = result2(n + j, t + j)
                    if m.base == 0 and m.reg is None:
                        act.wait_ge(ys_lo, DT)
                    else:
                        act.wait_ge(read_out[slot(t + j - 2)], nth(t + j - 2) + 1)
                    act.activation(g[:], src, ACT.Sigmoid).then_inc(read_out[(t + j) % 2], 1)
                split_hi(n + 5)
                split_hi(n + 6)
                act.wait_ge(m2_ready, val(m + 1))
                act.activation(M2H[:, cols(m * S2, S2)], G4[:], ACT.Copy).then_inc(m2_hi, 1)

            repeat(act, DT, 1, merge)

            for m in range(DT):
                n, t = N_OUT2 + m, T_OUT2 + m
                split_hi(n + 3)
                src = result2(n, t)
                act.activation(F3[:, m * S2:(m + 1) * S2], src, ACT.Copy)
                square2(Q_POST2 + m, src)
            root(7, S2)

        @block.vector
        def _(dve):
            def split_lo(n):
                n = as_lin(n)
                if n.base >= N_LAST:
                    return
                dve.wait_ge(w_hi, val(n + 2))
                dve.tensor_tensor(WL[:, n % SPLIT, :], WR[:, n % RAW, :], WH[:, n % SPLIT, :].bitcast(F32),
                                  ALU.subtract).then_inc(w_lo, 1)

            def low(dst, src, hi):
                return dve.tensor_tensor(dst, src, hi.bitcast(F32), ALU.subtract)

            dve.memset(PP[:, 0:2], 0.0).then_inc(zeroed, 1)
            dve.memset(VH[:, 4 * P:].bitcast(F32), 0.0)
            dve.memset(VL[:, 4 * P:].bitcast(F32), 0.0).then_inc(zeroed, 1)
            dve.wait_ge(w_hi, 1)
            low(CHL[:, :, 1], CR[:].rearrange("p (k x) -> p k x", x=2)[:, :, 1], CHL[:, :, 1]).then_inc(c_lo, 1)

            def root(e, last):
                dve.wait_ge(sq_summed, val(last))
                r = RB[:, e % 2, :]
                dve.tensor_scalar(halves(r), ZV, 1.0 / D, EPS, ALU.mult, ALU.add).then_inc(r_step, 1)
                dve.wait_ge(r_step, val(2 * e + 1))
                dve.reciprocal(r, r).then_inc(r_step, 1)
                dve.wait_ge(r_ready, val(e + 1))
                return r

            def normed(src, g, e, r, count):
                for m in range(DT):
                    xf = [CT, VT][m % 2]
                    if m >= 2:
                        dve.wait_ge(xl_ready, val(count * DT + m - 1))
                    dve.scalar_tensor_tensor(out=xf[:], in0=src[:, m * L1:(m + 1) * L1], scalar=PRM[:, g + m:g + m + 1],
                                             in1=r, op0=ALU.mult, op1=ALU.mult).then_inc(xf_ready, 1)
                    if m:
                        k = m - 1
                        dve.wait_ge(xh_ready, val(count * DT + k + 1))
                        low(XL[:, k * L1:(k + 1) * L1], [CT, VT][k % 2][:], XH[:, k * L1:(k + 1) * L1]).then_inc(xl_ready, 1)
                k = DT - 1
                dve.wait_ge(xh_ready, val(count * DT + k + 1))
                low(XL[:, k * L1:(k + 1) * L1], [CT, VT][k % 2][:], XH[:, k * L1:(k + 1) * L1]).then_inc(xl_ready, 1)

            for n in range(SPLIT - 2):
                split_lo(n)
            r = root(0, Q_PRE + DT)
            normed(X0, g_pre, 0, r, 0)
            split_lo(SPLIT - 2)

            def softplus(h):
                h = as_lin(h)
                dve.wait_ge(soft_step, val(3 * h + 3))
                dve.scalar_tensor_tensor(out=E[:], in0=Z[:, 0:SCORE], scalar=0.0, in1=E[:],
                                         op0=ALU.max, op1=ALU.add).then_inc(sp_ready, 1)

            def fail_lo(h):
                h = as_lin(h)
                dve.wait_ge(lf_hi, val(h + 1))
                low(LL[:], E[:], LH[:]).then_inc(lf_lo, 1)

            def weight_lo(h):
                h = as_lin(h)
                dve.wait_ge(a_hi, val(h + 1))
                low(AL[:], E[:], AH[:]).then_inc(a_lo, 1)

            def head_out(h, m, t):
                h, t = as_lin(h), as_lin(t)
                r = slice(64 * (h % 2), 64 * (h % 2) + 64)
                dve.wait_ge(o_hi, val(h + 1))
                low(halves(OL[r, cols(m * L1, L1)]), JV[t % 2][r], halves(OH[r, cols(m * L1, L1)]))\
                    .then_inc(read_out[t % 2], 1)

            def mix(m):
                n, t, h = N_MIX + 8 * m, T_MIX + 10 * m, 2 * m
                later = m.base or m.reg is not None
                split_lo(n + 3)
                dve.wait_ge(qk_hi, val(2 * m + 1))
                dve.scalar_tensor_tensor(out=halves(QL[:]), in0=JV[t % 2], scalar=0.125, in1=halves(QH[:]).bitcast(F32),
                                         op0=ALU.mult, op1=ALU.subtract).then_inc(read_out[t % 2], 1)
                split_lo(n + 4)
                dve.wait_ge(qk_hi, val(2 * m + 2))
                low(halves(KL[:, 0:L1]), JV[(t + 1) % 2], halves(KH[:, 0:L1])).then_inc(read_out[(t + 1) % 2], 1)
                if later:
                    head_out(h - 1, m - 1, t + 2)
                else:
                    dve.nop().then_inc(read_out[(t + 2) % 2], 1)
                softplus(h)
                split_lo(n + 5)
                fail_lo(h)
                split_lo(n + 6)
                dve.wait_ge(v_hi, val(2 * m + 1))
                low(VL[:, 0:3 * P], J[(t + 5) % 2][:, 0:3 * P], VH[:, 0:3 * P]).then_inc(read_out[(t + 5) % 2], 1)
                dve.wait_ge(v_hi, val(2 * m + 2))
                low(VL[:, 3 * P:4 * P], J[(t + 6) % 2][:, 0:P], VH[:, 3 * P:4 * P])
                low(VL[0:META, 4 * P:], J[(t + 6) % 2][0:META, P:2 * P], VH[0:META, 4 * P:])\
                    .then_inc(read_out[(t + 6) % 2], 1)
                weight_lo(h)
                split_lo(n + 7)
                dve.wait_ge(job_done, val(n + 5))
                dve.tensor_tensor(halves(PP[:, 2:]), JV[(t + 7) % 2], halves(CT[:]), ALU.mult)\
                   .then_inc(read_out[(t + 7) % 2], 1)
                dve.wait_ge(read_out[slot(t + 7)], nth(t + 7) + 1)
                if m.base or m.reg is not None:
                    dve.wait_ge(read_out[slot(t + 8 - 10)], nth(t + 8 - 10) + 1)
                taps(m, cw_mix, DT, conv_step)
                split_lo(n + 8)
                softplus(h + 1)
                dve.wait_ge(job_done, val(n + 6))
                dve.tensor_tensor(halves(CT[:]), JV[(t + 8) % 2], halves(CV[:]), ALU.mult)\
                   .then_inc(read_out[(t + 8) % 2], 1)
                fail_lo(h + 1)
                dve.wait_ge(y_hi, val(m + 1))
                low(YL[:, cols(m * L1, L1)], CT[:], YH[:, cols(m * L1, L1)]).then_inc(y_lo, 1)
                head_out(h, m, t + 9)
                split_lo(n + 9)
                dve.wait_ge(job_done, val(n + 8))
                if positive(m):
                    dve.wait_ge(mod_turned, val(m))
                dve.tensor_copy(MROW[0:2, 0:2 * P], ZT[0:2, 0:2 * P]).then_inc(mod_rows, 1)
                split_lo(n + 10)
                weight_lo(h + 1)
                dve.wait_ge(mod_turned, val(m + 1))
                dve.tensor_copy(MOD[:, cols(2 * m, 2)], ZT[:, 0:2]).then_inc(mod_ready, 1)

            def taps(m, w, tiles, step):
                for k in range(3):
                    tap = PRM[:, cols(w + (2 - k) * tiles + m, 1)]
                    src = PP[:, 2 - k:2 - k + L1]
                    if k == 0:
                        dve.tensor_scalar(CV[:], src, tap, None, ALU.mult).then_inc(step, 1)
                    else:
                        dve.scalar_tensor_tensor(out=CV[:], in0=src, scalar=tap, in1=CV[:],
                                                 op0=ALU.mult, op1=ALU.add).then_inc(step, 1)
                    dve.wait_ge(step, val(3 * m + k + 1))

            repeat(dve, DT, 1, mix)
            head_out(HEADS - 1, DT - 1, T_MIX + 10 * DT)

            def gates(m):
                n, t = N_GATE + 4 * m, T_GATE + 4 * m
                split_lo(n + 3)
                split_lo(n + 4)
                split_lo(n + 5)
                dve.wait_ge(job_done, val(n + 3))
                dve.wait_ge(read_out[slot(t)], nth(t) + 1)
                if positive(m):
                    dve.wait_ge(mf_ready, val(m))
                dve.tensor_tensor(halves(VT[:]), JV[(t + 2) % 2], halves(CT[:]), ALU.mult)\
                   .then_inc(read_out[(t + 2) % 2], 1)
                split_lo(n + 6)
                dve.wait_ge(job_done, val(n + 4))
                dve.wait_ge(read_out[slot(t + 1)], nth(t + 1) + 1)
                if positive(m):
                    dve.wait_ge(m_lo, val(m))
                dve.tensor_tensor(halves(PP[:, 2:]), JV[(t + 3) % 2], halves(CV[:]), ALU.mult)\
                   .then_inc(read_out[(t + 3) % 2], 1)
                dve.wait_ge(read_out[slot(t + 3)], nth(t + 3) + 1)
                dve.tensor_tensor(PP[:, 2:], PP[:, 2:], VT[:], ALU.add).then_inc(mf_ready, 1)
                dve.wait_ge(m_hi, val(m + 1))
                low(ML[:, cols(m * L1, L1)], PP[:, 2:], MH[:, cols(m * L1, L1)]).then_inc(m_lo, 1)

            repeat(dve, DT, 1, gates)

            for m in range(DT):
                n, t = N_OUT + 2 * m, T_OUT + m
                split_lo(n + 3)
                split_lo(n + 4)
                dve.wait_ge(sq_done, val(Q_MIX + m + 1))
                dve.nop().then_inc(read_out[t % 2], 1)
                if m % 4 == 3:
                    c = DT + m // 4
                    dve.wait_ge(job_done, val(n + 2))
                    dve.wait_ge(mod_turned, c)
                    dve.tensor_copy(MROW[0:2, :], ZT[0:2, :]).then_inc(mod_rows, 1)
                    dve.wait_ge(mod_turned, c + 1)
                    dve.tensor_copy(MOD[:, 2 * DT + m - 3:2 * DT + m + 1], ZT[:, 0:4]).then_inc(mod_ready, 1)

            def add_normed(f, g, r, count):
                for m in range(DT):
                    s = slice(m * L1, (m + 1) * L1)
                    tmp = [CT, VT][m % 2]
                    if m >= 2:
                        dve.wait_ge(h_ready, val(count * DT + m - 1))
                    dve.scalar_tensor_tensor(out=tmp[:], in0=f[:, s], scalar=PRM[:, g + m:g + m + 1], in1=r,
                                             op0=ALU.mult, op1=ALU.mult).then_inc(t_ready, 1)
                    dve.wait_ge(t_ready, val(count * DT + m + 1))
                    dve.tensor_tensor(H[:, s], H[:, s], tmp[:], ALU.add).then_inc(h_ready, 1)

            r = root(1, Q_MIX + DT)
            dve.wait_ge(h_landed, 16)
            add_normed(F, g_mix, r, 0)
            r = root(2, Q_PREF + DT)
            dve.wait_ge(h_ready, DT)
            normed(H, g_pref, 2, r, 1)

            def up(i):
                n, t = N_UP + 2 * i, T_UP + 2 * i
                split_lo(n + 3)
                dve.wait_ge(read_out[slot(t)], nth(t) + 1)
                if positive(i):
                    dve.wait_ge(gelu_done, val(i))
                taps(i, cw_ffn, FT, fconv_step)
                split_lo(n + 4)
                dve.wait_ge(job_done, val(n + 2))
                dve.wait_ge(gelu_done, val(i + 1))
                if positive(i):
                    dve.wait_ge(f_lo, val(i))
                dve.tensor_tensor(halves(CT[:]), JV[(t + 1) % 2], halves(VT[:]), ALU.mult)\
                   .then_inc(read_out[(t + 1) % 2], 1)
                dve.wait_ge(f_hi, val(i + 1))
                low(FL[:, cols(i * L1, L1)], CT[:], FH[:, cols(i * L1, L1)]).then_inc(f_lo, 1)

            repeat(dve, FT, 2, up)

            n = N_DOWN + SPLIT - 1
            for m in range(DT):
                while n < down_slots_after(m):
                    split_lo(n)
                    n += 1
                dve.wait_ge(sq_done, val(Q_FFN + m + 1))
                dve.nop().then_inc(read_out[(T_DOWN + m) % 2], 1)
            r = root(3, Q_FFN + DT)
            add_normed(F2, g_ffn, r, 1)

            steps = [0]

            def link(ins):
                steps[0] += 1
                ins.then_inc(setup, 1)
                dve.wait_ge(setup, steps[0])

            def mul(o, x, y):
                link(dve.tensor_tensor(o, x, y, ALU.mult))

            def add(o, x, y, op=ALU.add):
                link(dve.tensor_tensor(o, x, y, op))

            def cmul(o_r, o_i, a_r, a_i, b_r, b_i, t1, t2):
                mul(t1, a_r, b_r)
                mul(t2, a_i, b_i)
                add(o_r, t1, t2, ALU.subtract)
                mul(t1, a_r, b_i)
                mul(t2, a_i, b_r)
                add(o_i, t1, t2)

            def reduce_angle(x, n):
                link(dve.tensor_scalar(n, x, float(1 / (2 * np.pi)), MAGIC, ALU.mult, ALU.add))
                link(dve.tensor_scalar(n, n, MAGIC, None, ALU.subtract))
                for part in (TURN1, TURN2, TURN3):
                    link(dve.scalar_tensor_tensor(out=x, in0=n, scalar=-part, in1=x, op0=ALU.mult, op1=ALU.add))
                link(dve.tensor_scalar(x, x, PI_BELOW, -PI_BELOW, ALU.min, ALU.max))

            dve.wait_ge(job_done, N_U)
            link(dve.tensor_tensor(MB[:], MOD[:], PRM[:, a_bada:a_bada + 24], ALU.add))
            link(dve.scalar_tensor_tensor(out=GG[:, 0:8], in0=MB[:, 8:16], scalar=1.0, in1=PRM[:, a_gpre2:a_gpre2 + 8],
                                          op0=ALU.add, op1=ALU.mult))
            link(dve.tensor_tensor(GG[:, 8:16], MB[:, 16:24], PRM[:, a_gpost2:a_gpost2 + 8], ALU.mult))

            def root2(e, last, count):
                dve.wait_ge(sq_summed, val(last))
                r = RB[:, e % 2, 0:S2]
                dve.tensor_scalar(r, Z[:, 0:S2], 1.0 / count, EPS, ALU.mult, ALU.add).then_inc(r_step, 1)
                dve.wait_ge(r_step, val(2 * e + 1))
                dve.reciprocal(r, r).then_inc(r_step, 1)
                dve.wait_ge(r_ready, val(e + 1))
                return r

            dve.wait_ge(h_ready, 2 * DT)
            r = root2(4, Q_PRE2 + DT, D)

            def low2(m):
                dve.wait_ge(xh_ready, val(2 * DT + m + 1))
                s = slice(m * S2, (m + 1) * S2)
                dve.scalar_tensor_tensor(out=X2L[:, s], in0=[CT, VT][m % 2][:, 0:S2], scalar=MB[:, m:m + 1],
                                         in1=X2H[:, s].bitcast(F32), op0=ALU.add, op1=ALU.subtract).then_inc(xl_ready, 1)

            for m in range(DT):
                if m >= 2:
                    dve.wait_ge(xl_ready, val(2 * DT + m - 1))
                dve.scalar_tensor_tensor(out=[CT, VT][m % 2][:, 0:S2], in0=H[:, m * L1 + META:(m + 1) * L1],
                                         scalar=GG[:, m:m + 1], in1=r, op0=ALU.mult, op1=ALU.mult).then_inc(xf_ready, 1)
                if m:
                    low2(m - 1)
            low2(DT - 1)

            split_lo(N_U + 3)
            are, aim = PRM[:, a_are:a_are + PAIRS], PRM[:, a_aim:a_aim + PAIRS]
            dt_, lrdt, th, nn, mag, sn, sh, cs = SM[0][:], SM[1][:], SM[2][:], SM[3][:], SM[5][:], SM[6][:], SM[7][:], SM[8][:]
            dve.nop().then_inc(trig_in, 1)
            dve.wait_ge(trig_out, 1)
            mul(th, aim, dt_)
            reduce_angle(th, nn)
            mul(lrdt, are, dt_)
            dve.nop().then_inc(trig_in, 1)
            split_lo(N_U + 4)
            dve.nop().then_inc(trig_in, 1)

            for m in range(DT):
                if m >= 2:
                    split_lo(N_U + 3 + m)
                dve.wait_ge(ut_copied, val(m + 1))
                dve.nop().then_inc(read_out[(T_U + m) % 2], 1)
                if m == 2:
                    dve.wait_ge(trig_out, 4)
                    mul(cs, sh, sh)
                    link(dve.tensor_scalar(cs, cs, -2.0, 1.0, ALU.mult, ALU.add))
                    dve.nop().then_inc(turn_ready, 1)
                    ar, ai = SM[9][:], SM[10][:]
                    mul(ar, mag, cs)
                    mul(ai, mag, sn)
                    den, t1, t2, nr, fr, fi = (SM[k][:] for k in range(11, 17))
                    mul(t1, are, are)
                    mul(t2, aim, aim)
                    add(den, t1, t2)
                    link(dve.reciprocal(den, den))
                    link(dve.tensor_scalar(nr, ar, 1.0, None, ALU.subtract))
                    mul(t1, nr, are)
                    mul(t2, ai, aim)
                    add(fr, t1, t2)
                    mul(fr, fr, den)
                    mul(t1, ai, are)
                    mul(t2, nr, aim)
                    add(fi, t1, t2, ALU.subtract)
                    mul(fi, fi, den)
                if m == 3:
                    dve.wait_ge(mat_landed, 32)
                    wide = [P, PAIRS, GP]
                    frb, fib = fr.unsqueeze(2).to_broadcast(wide), fi.unsqueeze(2).to_broadcast(wide)
                    cmul(BBR[:], BBI[:], frb, fib, BM[:, 0], BM[:, 1], C1[:], C2[:])
                    link(dve.tensor_scalar(NCI[:], CM[:, 1], -1.0, None, ALU.mult))
                if m == 4:
                    link(dve.memset(PWR[:, :, 0:1], 1.0))
                    link(dve.memset(PWI[:, :, 0:1], 0.0))
                    link(dve.tensor_copy(PWR[:, :, 1], ar))
                    link(dve.tensor_copy(PWI[:, :, 1], ai))
                    for k in (1, 2, 4):
                        w = [P, PAIRS, k]
                        t1_, t2_ = (TS[:, x, 0:PAIRS * k].rearrange("p (a b) -> p a b", b=k) for x in range(2))
                        cmul(PWR[:, :, k + 1:2 * k + 1], PWI[:, :, k + 1:2 * k + 1],
                             PWR[:, :, k:k + 1].to_broadcast(w), PWI[:, :, k:k + 1].to_broadcast(w),
                             PWR[:, :, 1:k + 1], PWI[:, :, 1:k + 1], t1_, t2_)
                    for j in range(SUB):
                        dve.tensor_copy(RVR[:, :, j], PWR[:, :, SUB - 1 - j])
                        ins = dve.tensor_copy(RVI[:, :, j], PWI[:, :, SUB - 1 - j])
                    ins.then_inc(pow_ready, 1)

            for k in range(2):
                link(dve.memset(SR[k][:, :, 0:1], 0.0))
                link(dve.memset(SI[k][:, :, 0:1], 0.0))
            dve.memset(TK[:], 0.0).then_inc(tk_zeroed, 1)
            dve.wait_ge(tables_ready, 1)
            link(dve.memset(WAR_[:, :, 0:1], 1.0))
            link(dve.memset(WAI[:, :, 0:1], 0.0))
            turn, twice = (SM[17][:], SM[18][:]), (SM[19][:], SM[20][:])
            for k in (1, 2, 4):
                w = [P, PAIRS, k]
                t1_, t2_ = (TS[:, x, 0:PAIRS * k].rearrange("p (a b) -> p a b", b=k) for x in range(2))
                cmul(WAR_[:, :, k:2 * k], WAI[:, :, k:2 * k],
                     turn[0].unsqueeze(2).to_broadcast(w), turn[1].unsqueeze(2).to_broadcast(w),
                     WAR_[:, :, 0:k], WAI[:, :, 0:k], t1_, t2_)
                if k < 4:
                    cmul(*twice, *turn, *turn, SM[22][:], SM[23][:])
                    turn, twice = twice, turn

            def states(m):
                t = t_turned(m) + 2
                ps = slice(PT_ * m, PT_ * (m + 1))
                w4 = [P, PT_, 8, 8]
                cmul(WC[:], WS[:], WAR_[:, ps].unsqueeze(3).to_broadcast(w4), WAI[:, ps].unsqueeze(3).to_broadcast(w4),
                     WBR[:, ps].unsqueeze(2).to_broadcast(w4), WBI[:, ps].unsqueeze(2).to_broadcast(w4),
                     VR[:].rearrange("p a (b c) -> p a b c", b=8), VI[:].rearrange("p a (b c) -> p a b c", b=8))
                link(dve.tensor_copy(MT[:], SM[21][:, ps].unsqueeze(2).to_broadcast([P, PT_, NC])))
                link(dve.memset(MT[:, :, 0:1], 0.0))
                wc, ws = (x[:].rearrange("p a b c -> p a (b c)") for x in (WC, WS))
                dve.wait_ge(b_done, val(m + 1))
                br, bi = (J[t % 2][:, 512 * x:512 * x + PT_ * NC].rearrange("p (a c) -> p a c", a=PT_) for x in range(2))
                mul(V1[:], br, wc)
                mul(V2[:], bi, ws)
                add(VR[:], V1[:], V2[:])
                mul(V1[:], bi, wc)
                mul(V2[:], br, ws)
                dve.nop().then_inc(read_out[t % 2], 1)
                add(VI[:], V1[:], V2[:], ALU.subtract)
                flat = [x[:].rearrange("p a c -> p (a c)") for x in (MT, VR, VI, V1, V2)]
                link(dve.tensor_tensor_scan(flat[3], flat[0], flat[1], 0.0, ALU.mult, ALU.add))
                link(dve.tensor_tensor_scan(flat[4], flat[0], flat[2], 0.0, ALU.mult, ALU.add))
                if positive(m - 1):
                    dve.wait_ge(y_done, val(m - 1))
                mul(VR[:], V1[:], wc)
                mul(VI[:], V2[:], ws)
                add(SR[m % 2][:, :, 1:], VR[:], VI[:], ALU.subtract)
                mul(VR[:], V1[:], ws)
                mul(VI[:], V2[:], wc)
                dve.tensor_tensor(SI[m % 2][:, :, 1:], VR[:], VI[:], ALU.add).then_inc(s_ready, 1)
                dve.wait_ge(s_ready, m + 1)

            for m in range(DT):
                split_lo(N_SSM + m + 3)
                if m == 0:
                    states(0)
                if m + 1 < DT:
                    states(m + 1)
                t = t_y(m)
                dve.wait_ge(y_done, val(m + 1))
                dve.wait_ge(ud_ready, val(m + 1))
                ud = UD[:].rearrange("p (r x) c -> p x r c", x=2)
                ys = J[t % 2][:].rearrange("p (x r c) -> p x r c", x=2, c=NC)[:, :, 0:PT_]
                dve.tensor_tensor(ud, ys, ud, ALU.add).then_inc(read_out[t % 2], 1)

            for k in range(4):
                split_lo(N_LAT + 3 + k)
                dve.wait_ge(sq_done, val(Q_LAT + k + 1))
                dve.nop().then_inc(read_out[(T_LAT + k) % 2], 1)
                if k == 1:
                    dve.wait_ge(pos_landed, 16)
                    link(dve.tensor_copy(TAB[:], POSI[:]))
                    link(dve.tensor_scalar(TAB[:], TAB[:], PRM[:, a_inv:a_inv + 1], None, ALU.mult))
                    reduce_angle(TAB[:], R2[:])
                    dve.nop().then_inc(trig_in, 1)

            def low_lat(k):
                dve.wait_ge(xh_ready, val(3 * DT + k + 1))
                s = slice(k % LATT * S2, (k % LATT + 1) * S2)
                low((LQL, LKL)[k // LATT][:, s], [CT, VT][k % 2][:, 0:S2], (LQH, LKH)[k // LATT][:, s]).then_inc(xl_ready, 1)

            def latent(first, r):
                for k in range(first, first + LATT):
                    if k >= 2:
                        dve.wait_ge(xl_ready, val(3 * DT + k - 1))
                    dve.scalar_tensor_tensor(out=[CT, VT][k % 2][:, 0:S2], in0=LATF[:, k * S2:(k + 1) * S2],
                                             scalar=PRM[:, a_glat + k:a_glat + k + 1], in1=r,
                                             op0=ALU.mult, op1=ALU.mult).then_inc(xf_ready, 1)
                for k in range(first, first + LATT):
                    low_lat(k)

            def rope(src):
                dve.tensor_tensor(RO[0:64], src[64:P], TAB[64:P], ALU.mult)
                return dve.tensor_tensor(R2[0:64], src[0:64], TAB[0:64], ALU.mult)

            latent(0, root2(5, Q_LAT + LATT, 256))
            dve.wait_ge(trig_out, 5)
            mul(R2[0:64], TAB[0:64], TAB[0:64])
            link(dve.tensor_scalar(TAB[0:64], R2[0:64], -2.0, 1.0, ALU.mult, ALU.add))
            dve.wait_ge(job_done, N_LAT + 5)
            link(rope(J[(T_LAT + 4) % 2][:, 0:S2]))
            dve.nop().then_inc(read_out[(T_LAT + 4) % 2], 1)
            dve.tensor_tensor(RO[0:64], RO[0:64], R2[0:64], ALU.add).then_inc(rope_ready, 1)
            latent(LATT, root2(6, Q_KV + LATT, 256))
            split_lo(N_LAT + 7)
            dve.wait_ge(rope_hi, 2)
            for x in range(2):
                ins = low(K2L[x][64:96], RO[0:32], K2H[x][64:96])
            ins.then_inc(kr_ready, 1)
            dve.wait_ge(kr_ready, 1)

            def attend(m):
                n, t, h = N_ATT + 2 * m, T_ATT + 8 * m, 2 * m
                dve.wait_ge(up_done, val(3 * m + 1))
                if positive(h):
                    dve.wait_ge(om_lo, val(h))
                    dve.wait_ge(v2_turned, val(m))
                rope(J[t % 2][:, 0:S2]).then_inc(roped, 1)
                dve.wait_ge(roped, val(m + 1))
                dve.nop().then_inc(read_out[t % 2], 1)
                dve.tensor_tensor(RO[0:64], RO[0:64], R2[0:64], ALU.add).then_inc(rope_ready, 1)
                dve.wait_ge(rope_hi, val(h + 4))
                for x in range(2):
                    ins = low(Q2L[x][64:96], RO[32 * x:32 * x + 32], Q2H[x][64:96])
                ins.then_inc(q_ready, 1)
                dve.wait_ge(q_top, val(h + 2))
                for x in range(2):
                    ins = low(Q2L[x][0:64], J[(t + 1) % 2][64 * x:64 * x + 64, 0:S2], Q2H[x][0:64])
                ins.then_inc(read_out[(t + 1) % 2], 1)
                dve.wait_ge(k_hi, val(m + 1))
                for x in range(2):
                    ins = low(K2L[x][0:64], J[t % 2][64 * x:64 * x + 64, 0:S2], K2H[x][0:64])
                ins.then_inc(read_out[t % 2], 1)
                split_lo(n + 3)
                dve.wait_ge(q_ready, val(m + 1))

                def peak(u):
                    g, i = 8 * m + u, u % 4
                    dve.wait_ge(s_done, val(g + 1))
                    dve.reduce_max(MX[:, u:u + 1], Z[:, 512 * (u % 2):512 * (u % 2) + P * (i + 1)], AX.X)\
                       .then_inc(mx_ready, 1)
                    dve.wait_ge(mx_ready, val(g + 1))
                    dve.tensor_scalar(NM[:, u:u + 1], MX[:, u:u + 1], -SCALE2, None, ALU.mult).then_inc(nm_ready, 1)

                def normalise(u):
                    g, i = 8 * m + u, u % 4
                    dve.wait_ge(p_exp, val(g + 1))
                    dve.reciprocal(RC[:, u:u + 1], SU[:, u:u + 1]).then_inc(rc_ready, 1)
                    dve.wait_ge(rc_ready, val(g + 1))
                    p = PB[:, u % 2, 0:P * (i + 1)]
                    dve.tensor_scalar(p, p, RC[:, u:u + 1], None, ALU.mult).then_inc(pn_ready, 1)

                def weights_lo(u):
                    g, i = 8 * m + u, u % 4
                    dve.wait_ge(pt_hi, val(g + 1))
                    low(PTL[:, 0:i + 1, P * i:P * (i + 1)],
                        PTB[u % 2][:, 0:P * (i + 1)].rearrange("p (j s) -> p j s", s=P),
                        PTH[:, 0:i + 1, P * i:P * (i + 1)]).then_inc(pt_lo, 1)

                def out_lo(x):
                    r = slice(64 * x, 64 * x + 64)
                    dve.wait_ge(pv2_done, val(h + x + 1))
                    if positive(h + x):
                        dve.wait_ge(om_lo, val(h + x))
                    dve.wait_ge(read_out[slot(t + 5)], nth(t + 5) + 1)
                    dve.tensor_tensor(RO[r], J[(t + 6 + x) % 2][r, 0:S2], VZ[r], ALU.mult).then_inc(om_ready, 1)
                    dve.wait_ge(om_ready, val(h + x + 1))
                    dve.nop().then_inc(read_out[(t + 6 + x) % 2], 1)
                    dve.wait_ge(om_hi, val(h + x + 1))
                    low(OML[r, cols(m * S2, S2)], RO[r], OMH[r, cols(m * S2, S2)]).then_inc(om_lo, 1)

                peak(0)
                normalise(0)
                peak(1)
                normalise(1)
                dve.wait_ge(v2_hi, val(m + 1))
                low(V2L[:], J[(t + 4) % 2][:, 0:S2], V2H[:]).then_inc(read_out[(t + 4) % 2], 1)
                split_lo(n + 4)
                for u in range(8):
                    if u + 2 < 8:
                        peak(u + 2)
                    weights_lo(u)
                    if u + 2 < 8:
                        normalise(u + 2)
                out_lo(0)
                out_lo(1)

            repeat(dve, DT, 2, attend)

            for m in range(DT):
                s = slice(m * S2, (m + 1) * S2)
                dve.wait_ge(yg_hi, val(m + 1))
                low(YGL[:, s], YG[:, s], YGH[:, s]).then_inc(yg_lo, 1)

            def glu(m):
                n, t = N_GLU + 2 * m, T_GLU + 2 * m
                split_lo(n + 3)
                split_lo(n + 4)
                dve.wait_ge(job_done, val(n + 2))
                dve.wait_ge(read_out[slot(t)], nth(t) + 1)
                if positive(m):
                    dve.wait_ge(ys_lo, val(m))
                dve.scalar_tensor_tensor(out=G1[:], in0=J[(t + 1) % 2][:, 0:S2], scalar=PRM[:, cols(a_bglu + m, 1)],
                                         in1=G2[:], op0=ALU.add, op1=ALU.mult).then_inc(glu_step, 1)
                dve.wait_ge(glu_step, val(2 * m + 1))
                dve.nop().then_inc(read_out[(t + 1) % 2], 1)
                dve.tensor_tensor(G1[:], G1[:], SZS[:, cols(m * S2, S2)], ALU.mult).then_inc(glu_step, 1)
                dve.wait_ge(ys_hi, val(m + 1))
                low(YSL[:, cols(m * S2, S2)], G1[:], YSH[:, cols(m * S2, S2)]).then_inc(ys_lo, 1)

            repeat(dve, DT, 2, glu)

            def merge(m):
                n, t = N_MERGE + 4 * m, T_MERGE + 4 * m
                split_lo(n + 3)
                split_lo(n + 4)
                split_lo(n + 5)
                dve.wait_ge(job_done, val(n + 3))
                dve.wait_ge(read_out[slot(t)], nth(t) + 1)
                if positive(m):
                    dve.wait_ge(m2_ready, val(m))
                dve.tensor_tensor(G3[:], J[(t + 2) % 2][:, 0:S2], G1[:], ALU.mult).then_inc(read_out[(t + 2) % 2], 1)
                split_lo(n + 6)
                dve.wait_ge(job_done, val(n + 4))
                dve.wait_ge(read_out[slot(t + 1)], nth(t + 1) + 1)
                if positive(m):
                    dve.wait_ge(m2_lo, val(m))
                dve.tensor_tensor(G4[:], J[(t + 3) % 2][:, 0:S2], G2[:], ALU.mult).then_inc(read_out[(t + 3) % 2], 1)
                dve.wait_ge(read_out[slot(t + 3)], nth(t + 3) + 1)
                dve.tensor_tensor(G4[:], G4[:], G3[:], ALU.add).then_inc(m2_ready, 1)
                dve.wait_ge(m2_hi, val(m + 1))
                low(M2L[:, cols(m * S2, S2)], G4[:], M2H[:, cols(m * S2, S2)]).then_inc(m2_lo, 1)

            repeat(dve, DT, 1, merge)

            for m in range(DT):
                split_lo(N_OUT2 + m + 3)
                dve.wait_ge(sq_done, val(Q_POST2 + m + 1))
                dve.nop().then_inc(read_out[(T_OUT2 + m) % 2], 1)
            r = root2(7, Q_POST2 + DT, D)
            dve.wait_ge(res_landed, 16)
            for m in range(DT):
                s = slice(m * S2, (m + 1) * S2)
                link(dve.scalar_tensor_tensor(out=F3[:, s], in0=F3[:, s], scalar=GG[:, 8 + m:9 + m], in1=r,
                                              op0=ALU.mult, op1=ALU.mult))
                dve.tensor_tensor(F3[:, s], F3[:, s], RES[:, s], ALU.add).then_inc(fin, 1)

        @block.gpsimd
        def _(pool):
            pool.memset(STAGE[:], 1.0).then_inc(zeroed_pool, 1)
            pool.memset(IDENT[:], 1.0).then_inc(zeroed_pool, 1)
            pool.wait_ge(zeroed_pool, 2)
            pool.memset(ONES[:], 1.0).then_inc(consts, 1)
            pool.affine_select(out=STAGE[:, 0, :], in_=STAGE[:, 0, :], compare_op=ALU.is_ge, fill=0.0,
                               base=0, pattern=[[-1, P]], channel_multiplier=1).then_inc(consts, 1)
            pool.affine_select(out=IDENT[:], in_=IDENT[:], compare_op=ALU.is_equal, fill=0.0,
                               base=0, pattern=[[-1, P]], channel_multiplier=1).then_inc(consts, 1)

            def mask(done):
                for c, w in DIAGONAL:
                    d = E[:, c:c + w]
                    pool.affine_select(out=d, in_=d, compare_op=ALU.is_gt, fill=0.0, base=0,
                                       pattern=[[1, w]], channel_multiplier=-1).then_inc(done, 1)

            def mix(m):
                for h in (2 * m, 2 * m + 1):
                    pool.wait_ge(sp_ready, val(h + 1))
                    mask(lf_masked)
                    pool.wait_ge(a_exp, val(h + 1))
                    mask(a_masked)

            for m in range(DT):
                mix(m)

            steps = [0]

            def link(ins):
                steps[0] += 1
                ins.then_inc(pool_step, 1)
                pool.wait_ge(pool_step, steps[0])

            def tt(o, x, y, op=ALU.mult):
                return pool.tensor_tensor(o, x, y, op)

            def skip(m):
                pool.wait_ge(us_landed[m // 4], 16 * SUB)
                if positive(m):
                    pool.wait_ge(ygelu, val(m))
                g = slice(GT * m, GT * (m + 1))
                tt(UD[:], US[:, g], PRM[:, a_d + GT * m:a_d + GT * (m + 1)].unsqueeze(2).to_broadcast([P, GT, NC]))\
                    .then_inc(ud_ready, 1)

            pool.wait_ge(turn_ready, 1)
            m8 = SM[21][:]
            link(tt(m8, SM[5][:], SM[5][:]))
            for _ in range(2):
                link(tt(m8, m8, m8))
            turns = [(SM[8][:], SM[6][:]), (SM[17][:], SM[18][:]), (SM[19][:], SM[20][:])]

            def turned(o_r, o_i, a_r, a_i, b_r, b_i, t1, t2):
                link(tt(t1, a_r, b_r))
                link(tt(t2, a_i, b_i))
                link(tt(o_r, t1, t2, ALU.subtract))
                link(tt(t1, a_r, b_i))
                link(tt(t2, a_i, b_r))
                link(tt(o_i, t1, t2, ALU.add))

            def square_turn(k):
                turn, twice = (turns[0] if i == 0 else turns[1 + i % 2] for i in (k, k + 1))
                turned(*twice, *turn, *turn, SM[22][:], SM[23][:])

            for k in range(3):
                square_turn(k)
            link(pool.memset(WBR[:, :, 0:1], 1.0))
            link(pool.memset(WBI[:, :, 0:1], 0.0))
            for number, k in ((3, 1), (4, 2), (5, 4)):
                w = [P, PAIRS, k]
                t1_, t2_ = (x[:].rearrange("p a b c -> p (a b c)")[:, 0:PAIRS * k]
                            .rearrange("p (a b) -> p a b", b=k) for x in (K1, K2))
                ur, ui = turns[1 + number % 2]
                turned(WBR[:, :, k:2 * k], WBI[:, :, k:2 * k],
                       ur.unsqueeze(2).to_broadcast(w), ui.unsqueeze(2).to_broadcast(w),
                       WBR[:, :, 0:k], WBI[:, :, 0:k], t1_, t2_)
                square_turn(number)
            pool.nop().then_inc(tables_ready, 1)

            pool.wait_ge(pow_ready, 1)
            for m in range(DT):
                ps = slice(PT_ * m, PT_ * (m + 1))
                w = [P, PT_, SUB, GP]
                rr, ri = (x[:, ps].unsqueeze(3).to_broadcast(w) for x in (RVR, RVI))
                bbr, bbi = (x[:, ps].unsqueeze(2).to_broadcast(w) for x in (BBR, BBI))
                k1, k2 = (x[:, :, 0:SUB] for x in (K1, K2))
                if positive(m):
                    pool.wait_ge(bt_turned, val(m))
                link(tt(k1, bbr, rr))
                link(tt(k2, bbi, ri))
                link(tt(BPR[:], k1, k2, ALU.subtract))
                link(tt(k1, bbr, ri))
                link(tt(k2, bbi, rr))
                tt(BPI[:], k1, k2, ALU.add).then_inc(bp_ready, 1)
                pool.wait_ge(bp_ready, m + 1)
                w = [P, PT_, SUB + 1, GP]
                pr, pi = (x[:, ps].unsqueeze(3).to_broadcast(w) for x in (PWR, PWI))
                cr, nci = CM[:, 0, ps].unsqueeze(2).to_broadcast(w), NCI[:, ps].unsqueeze(2).to_broadcast(w)
                if positive(m - 1):
                    pool.wait_ge(y_done, val(m - 1))
                link(tt(K1[:], cr, pr))
                link(tt(K2[:], nci, pi))
                link(tt(CPR[m % 2][:], K1[:], K2[:], ALU.add))
                link(tt(K1[:], nci, pr))
                link(tt(K2[:], cr, pi))
                tt(CPI[m % 2][:], K1[:], K2[:], ALU.subtract).then_inc(cp_ready, 1)
                pool.wait_ge(cp_ready, m + 1)
                if m:
                    skip(m - 1)
            skip(DT - 1)

            pool.wait_ge(xl_ready, 3 * DT + 2 * LATT)
            pool.memset(PB[:], 0.0).then_inc(pattern, 1)
            pool.wait_ge(pattern, 1)
            for x in range(2):
                v = PB[:, x].rearrange("p (i h t) -> p i h t", i=4, h=2)[:, :, x]
                pool.memset(v, 1.0).then_inc(pattern, 1)
                pool.wait_ge(pattern, 2 + 2 * x)
                pool.affine_select(out=v, in_=v, compare_op=ALU.is_equal, fill=0.0, base=96,
                                   pattern=[[1, 4], [0, 64]], channel_multiplier=-1).then_inc(pattern, 1)
                pool.wait_ge(pattern, 3 + 2 * x)
            pool.nop().then_inc(pattern, 1)


PARAM = {}


def tiles(v):
    v = np.asarray(v)
    return np.ascontiguousarray(v.reshape(-1, P).T)


def blocks(w, columns=None):
    w = np.asarray(w)
    k, m = w.shape
    return w.reshape(k // P, P, m // P, P).transpose(2, 0, 1, 3)


def jobs(b):
    b = b.reshape(-1, 8, P, P)
    return b.transpose(0, 2, 1, 3).reshape(-1, P, 8 * P)


def interleave(*ws):
    return np.concatenate([w[:, None] for w in ws], axis=1)


INV_FREQ = np.tile(np.power(np.float32(10000.0), -np.arange(0, ROPE, 2, dtype=np.float32) / np.float32(ROPE)), 8)
SIGN = np.concatenate([np.full(64, 0.5), np.tile(np.repeat([-1.0, 1.0], 16), 2)]).astype(np.float32)


def kernel(**inputs):
    import concourse.bacc as bacc
    from concourse.bass_utils import run_bass_kernel_spmd

    a = {k: np.asarray(v) for k, v in inputs.items()}
    w_in = blocks(a["w_in"][0]).reshape(8, DT, DT, P, P)
    b_c, c_c, h_c, q, k, v, g_conv, g_attn = w_in
    w_ada = a["w_ada_2"][0]
    ada = w_ada[:, :2 * D].reshape(2, 4, P, DT, 2, P).transpose(3, 0, 1, 4, 2, 5).reshape(DT, 2, 8, P, P)
    ada_last = w_ada[:, 2 * D:].reshape(4, 2, P, 2, 4, P).transpose(3, 0, 1, 4, 2, 5).reshape(DT, 8, P, P)
    stream = [
        interleave(q, k, v, c_c, h_c, b_c, ada[:, 0], ada[:, 1]),
        interleave(g_conv, g_attn, blocks(a["w_proj_conv"][0]), blocks(a["w_proj_attn"][0])),
        interleave(blocks(a["w_out"][0]), ada_last),
        blocks(a["w_up_gate"][0]).reshape(2, FT, DT, P, P).transpose(1, 0, 2, 3, 4),
        blocks(a["w_down"][0]),
    ]
    w2 = a["w_in_2"][0]
    u_s, z_s, q_lat, kv_lat, k_rope, z_m, gl_s, gl_m = np.split(
        w2, np.cumsum([1024, 1024, 256, 256, 32, 1024, 1024])[:8], axis=1)

    def swapped(w):
        return np.concatenate([w[..., 16:], w[..., :16]], axis=-1)

    kr = np.concatenate([k_rope, k_rope, swapped(k_rope), swapped(k_rope)], axis=1)
    wq = a["w_q_up_2"][0].reshape(256, HEADS // 2, 2, 96)
    wr = wq[..., 64:]
    wr = np.stack([wr, swapped(wr)], axis=2).reshape(256, 1024)
    wq = wq[..., :64].reshape(256, 1024)
    wkv = a["w_kv_up_2"][0].reshape(256, HEADS, 128)
    wk = wkv[..., :64].reshape(256, 1024)
    wv = wkv[..., 64:].reshape(256, 1024)
    up = np.concatenate([blocks(wr), blocks(wq), blocks(wk), blocks(wv)], axis=1)
    glu = blocks(a["w_glu_2"][0])
    stream += [
        blocks(u_s), blocks(z_s), blocks(q_lat), blocks(kv_lat), blocks(kr),
        interleave(up, blocks(z_m)),
        interleave(glu[8:], glu[:8]),
        interleave(blocks(gl_s), blocks(gl_m), blocks(a["w_br_ssm_2"][0]), blocks(a["w_br_mla_2"][0])),
        blocks(a["w_out_2"][0]),
    ]
    weights = np.concatenate([jobs(s) for s in stream])
    assert weights.shape[0] == N_LAST
    vectors = [
        ("g_pre_mix", a["g_pre_mix"]), ("g_post_mix", a["g_post_mix"]), ("g_pre_ffn", a["g_pre_ffn"]),
        ("g_post_ffn", a["g_post_ffn"]), ("b_gate", a["b_gate"]), ("conv_w_mix", a["conv_w_mix"]),
        ("conv_w_ffn", a["conv_w_ffn"]),
        ("b_ada", a["b_ada_2"]), ("g_pre_2", a["g_pre_2"]), ("g_post_2", a["g_post_2"]),
        ("g_lat", np.concatenate([a["g_q_norm_2"], a["g_kv_norm_2"]])), ("b_glu", a["b_glu_2"]),
        ("a_re", a["ssm_a_re_2"]), ("a_im", a["ssm_a_im_2"]), ("log_dt", np.repeat(a["ssm_log_dt_2"], NS)),
        ("ssm_d", np.tile(a["ssm_d_2"].reshape(GROUPS, GP), (1, SUB))),
        ("inv_freq", INV_FREQ), ("sign", SIGN),
    ]
    params, at = [], 0
    for name, vec in vectors:
        params.append(tiles(vec))
        PARAM[name] = at
        at += params[-1].shape[1]
    params = np.concatenate(params, axis=1)
    cond = np.repeat(tiles(a["c_2"]), 2, axis=1)
    tokens = np.ascontiguousarray(np.concatenate([a["meta_tokens"], a["x"][0]]).T)

    nc = bacc.Bacc("TRN2", target_bir_lowering=False, num_devices=1)
    def states(x):
        return x.reshape(PAIRS, P, GP).transpose(1, 0, 2)

    bmat = np.stack([states(a["ssm_b_re_2"][0]), states(a["ssm_b_im_2"][0])], axis=1)
    cmat = np.stack([states(a["ssm_c_re_2"][0].transpose(0, 2, 1)),
                     states(a["ssm_c_im_2"][0].transpose(0, 2, 1))], axis=1)
    arrays = {"weights": weights, "cond": cond, "params": params, "tokens": tokens,
              "bmat": bmat, "cmat": cmat, "positions": a["positions_2"]}
    aps = [nc.dram_tensor(n, x.shape, mybir.dt.from_np(x.dtype), kind="ExternalInput").ap()
           for n, x in arrays.items()]
    out = nc.dram_tensor("out", (D, SEQ), F32, kind="ExternalOutput").ap()
    build(nc, *aps, out)
    r = run_bass_kernel_spmd(nc, [arrays], core_ids=[0])
    return np.ascontiguousarray(r.results[0]["out"].T)[None]
```
